# Optimizing a Trainium2 kernel written in Bass

```python
import math
import jax
import jax.numpy as jnp
from jax import lax
import numpy as np

D_MODEL = 1024
BATCH = 1
SEQ = 512
DEPTH = 2
DEC_BATCH = 8
DEC_SEQ = 4
PAST_LEN = 2048
PAGE_SIZE = 128

N_A_LAYERS = DEPTH // 2
N_B_LAYERS = DEPTH - N_A_LAYERS
DN_HEADS = 6
DN_DK = 128
DN_DV = 128
DN_QK_W = DN_HEADS * DN_DK
DN_V_W = DN_HEADS * DN_DV
CONV_W = 4
CONV_CH = 2 * DN_QK_W + DN_V_W
DELTA_CHUNK = 64
MLA_HEADS = 6
Q_LORA = 384
KV_LORA = 256
QK_NOPE = 128
QK_ROPE = 64
V_HEAD = 128
MLA_SCALE = (QK_NOPE + QK_ROPE) ** -0.5
ROPE_THETA = 10000.0
Q_BLOCK = 128
MEM_TOKENS = 256
MEM_HEADS = 4
MEM_HD = 64
MEM_W = MEM_HEADS * MEM_HD
N_GROUPS = 4
EXP_PER_GROUP = 8
N_EXPERTS = N_GROUPS * EXP_PER_GROUP
TOP_K = 2
EXPERT_FF = 256
EPS = 1e-6
IN_A = CONV_CH + DN_V_W + 2 * DN_HEADS + MEM_W
OUT_A = DN_V_W + MEM_W
IN_B = Q_LORA + MEM_W
OUT_B = MLA_HEADS * V_HEAD + MEM_W

kernel_name = "yoco_gdn_mla_hmoe_decode_step"

F32 = jnp.float32

def rms_norm(x, g):
    x32 = x.astype(F32)
    y = x32 * lax.rsqrt(jnp.mean(x32 * x32, axis=-1, keepdims=True) + EPS)
    return (y * g.astype(F32)).astype(x.dtype)

def l2_normalize(x):
    x32 = x.astype(F32)
    return x32 * lax.rsqrt(jnp.sum(x32 * x32, axis=-1, keepdims=True) + EPS)

def rope_tables(pos):
    inv = ROPE_THETA ** (-jnp.arange(0, QK_ROPE, 2, dtype=F32) / QK_ROPE)
    ang = pos.astype(F32)[:, None] * inv[None, :]
    return jnp.cos(ang), jnp.sin(ang)

def apply_rope(x, cos, sin):
    half = x.shape[-1] // 2
    x32 = x.astype(F32)
    x1, x2 = x32[..., :half], x32[..., half:]
    return jnp.concatenate([x1 * cos - x2 * sin, x2 * cos + x1 * sin], axis=-1).astype(x.dtype)

def causal_short_conv(x, buf, w):
    L = x.shape[1]
    xp = jnp.concatenate([buf.astype(x.dtype), x], axis=1)
    y = w[0] * xp[:, 0:L]
    for j in range(1, CONV_W):
        y = y + w[j] * xp[:, j:j + L]
    return jax.nn.silu(y), xp[:, L:]

def gated_delta_rule(q, k, v, g, beta, s0):
    B, L, H, DK = q.shape
    DV = v.shape[-1]
    chunk = DELTA_CHUNK if L % DELTA_CHUNK == 0 else L
    n = L // chunk

    def blk(t):
        t = t.astype(F32).reshape((B, n, chunk, H) + t.shape[3:])
        return jnp.moveaxis(t, (1, 3), (0, 2))

    qc, kc, vc, gc, bc = blk(q), blk(k), blk(v), blk(g), blk(beta)
    G = jnp.cumsum(gc, axis=-1)
    idx = jnp.arange(chunk)
    incl = idx[:, None] >= idx[None, :]
    strict = idx[:, None] > idx[None, :]
    gamma = jnp.exp(jnp.where(incl, G[..., :, None] - G[..., None, :], -jnp.inf))
    kk = jnp.einsum('nbhik,nbhjk->nbhij', kc, kc)
    a_mat = jnp.where(strict, kk * gamma * bc[..., :, None], 0.0) + jnp.eye(chunk, dtype=F32)
    rhs = jnp.concatenate([vc * bc[..., None], kc * (bc * jnp.exp(G))[..., None]], axis=-1)
    sol = lax.linalg.triangular_solve(a_mat, rhs, left_side=True, lower=True, unit_diagonal=True)
    u, w = sol[..., :DV], sol[..., DV:]
    q_dec = qc * jnp.exp(G)[..., None]
    qk = jnp.einsum('nbhik,nbhjk->nbhij', qc, kc) * gamma
    k_dec = kc * jnp.exp(G[..., -1:] - G)[..., None]
    chunk_decay = jnp.exp(G[..., -1])

    def step(S, xs):
        q_i, qk_i, u_i, w_i, k_i, d_i = xs
        e = u_i - jnp.einsum('bhck,bhkv->bhcv', w_i, S)
        o = jnp.einsum('bhck,bhkv->bhcv', q_i, S) + jnp.einsum('bhij,bhjv->bhiv', qk_i, e)
        S = S * d_i[..., None, None] + jnp.einsum('bhck,bhcv->bhkv', k_i, e)
        return S, o

    s_fin, o = lax.scan(step, s0.astype(F32), (q_dec, qk, u, w, k_dec, chunk_decay))
    o = jnp.moveaxis(o, (0, 2), (1, 3)).reshape(B, L, H, DV)
    return o, s_fin

def memory_kv(mem, g, wk, wv):
    B, M, _ = mem.shape
    m = rms_norm(mem, g)
    return ((m @ wk).reshape(B, M, MEM_HEADS, MEM_HD), (m @ wv).reshape(B, M, MEM_HEADS, MEM_HD))

def memory_attention(q, mk, mv):
    s = jnp.einsum('blhd,bmhd->bhlm', q, mk, preferred_element_type=F32) * MEM_HD ** -0.5
    p = jax.nn.softmax(s, axis=-1).astype(mv.dtype)
    return jnp.einsum('bhlm,bmhd->blhd', p, mv)

def deltanet_mixer(u, conv_buf, s0, mem_k, mem_v, w_in, conv_w, a_log, dt_bias, g_onorm, w_out):
    B, L, _ = u.shape
    proj = u @ w_in
    qkv, z, a, b, qm = jnp.split(proj, [CONV_CH, CONV_CH + DN_V_W, CONV_CH + DN_V_W + DN_HEADS,
                                        CONV_CH + DN_V_W + 2 * DN_HEADS], axis=-1)
    qkv, new_buf = causal_short_conv(qkv, conv_buf, conv_w)
    q, k, v = jnp.split(qkv, [DN_QK_W, 2 * DN_QK_W], axis=-1)
    q = l2_normalize(q.reshape(B, L, DN_HEADS, DN_DK)) * DN_DK ** -0.5
    k = l2_normalize(k.reshape(B, L, DN_HEADS, DN_DK))
    v = v.reshape(B, L, DN_HEADS, DN_DV)
    g = -jnp.exp(a_log.astype(F32)) * jax.nn.softplus(a.astype(F32) + dt_bias.astype(F32))
    beta = jax.nn.sigmoid(b.astype(F32))
    o, s_new = gated_delta_rule(q, k, v, g, beta, s0)
    o = rms_norm(o, g_onorm) * jax.nn.silu(z.reshape(B, L, DN_HEADS, DN_DV).astype(F32))
    mo = memory_attention(qm.reshape(B, L, MEM_HEADS, MEM_HD), mem_k, mem_v)
    merged = jnp.concatenate([o.reshape(B, L, DN_V_W).astype(u.dtype), mo.reshape(B, L, MEM_W)], axis=-1)
    return merged @ w_out, new_buf, s_new.astype(s0.dtype)

def shared_latent_kv(h, g_in, w_dkv, g_lat, cos, sin):
    ckr = rms_norm(h, g_in) @ w_dkv
    c = rms_norm(ckr[..., :KV_LORA], g_lat)
    kr = apply_rope(ckr[..., KV_LORA:], cos, sin)
    return c, kr

def mla_scores(q_lat, q_rope, c, kr):
    s = jnp.einsum('bqhc,bkc->bhqk', q_lat, c, preferred_element_type=F32)
    s = s + jnp.einsum('bqhr,bkr->bhqk', q_rope, kr, preferred_element_type=F32)
    return s * MLA_SCALE

def mla_attend_prompt(q_lat, q_rope, c, kr):
    B, L, H, C = q_lat.shape
    nb = L // Q_BLOCK

    def to_blocks(t):
        return jnp.moveaxis(t.reshape(B, nb, Q_BLOCK, H, t.shape[-1]), 1, 0)

    k_pos = jnp.arange(L)

    def block(args):
        ql, qr, start = args
        s = mla_scores(ql, qr, c, kr)
        q_pos = start + jnp.arange(Q_BLOCK)
        s = jnp.where(k_pos[None, :] <= q_pos[:, None], s, -jnp.inf)
        p = jax.nn.softmax(s, axis=-1).astype(c.dtype)
        return jnp.einsum('bhqk,bkc->bqhc', p, c)

    out = lax.map(block, (to_blocks(q_lat), to_blocks(q_rope), jnp.arange(nb) * Q_BLOCK))
    return jnp.moveaxis(out, 0, 1).reshape(B, L, H, C)

def mla_attend_sample(q_lat, q_rope, c_new, kr_new, cache_lat, cache_kr, page_table):
    B, Q = q_lat.shape[:2]
    past_c = cache_lat[page_table].reshape(B, -1, KV_LORA)
    past_r = cache_kr[page_table].reshape(B, -1, QK_ROPE)
    P = past_c.shape[1]
    s_past = mla_scores(q_lat, q_rope, past_c, past_r)
    s_new = mla_scores(q_lat, q_rope, c_new, kr_new)
    causal = jnp.arange(Q)[None, :] <= jnp.arange(Q)[:, None]
    s_new = jnp.where(causal, s_new, -jnp.inf)
    p = jax.nn.softmax(jnp.concatenate([s_past, s_new], axis=-1), axis=-1)
    return (jnp.einsum('bhqk,bkc->bqhc', p[..., :P].astype(past_c.dtype), past_c)
            + jnp.einsum('bhqk,bkc->bqhc', p[..., P:].astype(c_new.dtype), c_new))

def mla_mixer(u, c, kr, mem_k, mem_v, w_in, g_q, w_uq, w_uk, w_uv, w_out, cos, sin, paged):
    B, L, _ = u.shape
    proj = u @ w_in
    cq, qm = proj[..., :Q_LORA], proj[..., Q_LORA:]
    q = (rms_norm(cq, g_q) @ w_uq).reshape(B, L, MLA_HEADS, QK_NOPE + QK_ROPE)
    q_nope, q_rope = q[..., :QK_NOPE], q[..., QK_NOPE:]
    q_rope = apply_rope(q_rope, cos[:, None], sin[:, None])
    q_lat = jnp.einsum('blhn,chn->blhc', q_nope, w_uk)
    if paged is None:
        out_lat = mla_attend_prompt(q_lat, q_rope, c, kr)
    else:
        out_lat = mla_attend_sample(q_lat, q_rope, c, kr, paged[0], paged[1], paged[2])
    o = jnp.einsum('blhc,chv->blhv', out_lat, w_uv).reshape(B, L, MLA_HEADS * V_HEAD)
    mo = memory_attention(qm.reshape(B, L, MEM_HEADS, MEM_HD), mem_k, mem_v).reshape(B, L, MEM_W)
    return jnp.concatenate([o, mo], axis=-1) @ w_out

def hier_moe(x, w_rg, b_rg, w_re, b_re, w_gate, w_up, w_down):
    shp = x.shape
    t = x.reshape(-1, shp[-1])
    T = t.shape[0]
    p_group = jax.nn.softmax(jnp.dot(t, w_rg, preferred_element_type=F32) + b_rg.astype(F32), axis=-1)
    g_val, g_idx = lax.top_k(p_group, 1)
    e_logit = (jnp.dot(t, w_re, preferred_element_type=F32) + b_re.astype(F32)).reshape(T, N_GROUPS, EXP_PER_GROUP)
    sel = jnp.broadcast_to(g_idx[:, :, None], (T, 1, EXP_PER_GROUP))
    e_in = jnp.take_along_axis(e_logit, sel, axis=1)[:, 0]
    e_val, e_idx = lax.top_k(e_in, TOP_K)
    gate = g_val * jax.nn.softmax(e_val, axis=-1)
    expert_id = g_idx * EXP_PER_GROUP + e_idx
    combine = jnp.sum(jax.nn.one_hot(expert_id, N_EXPERTS, dtype=F32) * gate[..., None], axis=1)

    def expert(acc, xs):
        wg, wu, wd, cw = xs
        h = jax.nn.silu(t @ wg) * (t @ wu)
        return acc + (h * cw[:, None]) @ wd, None

    y, _ = lax.scan(expert, jnp.zeros_like(t), (w_gate, w_up, w_down, combine.T.astype(t.dtype)))
    return y.reshape(shp)

def setup_inputs(seed: int = 0) -> dict:
    key = jax.random.key(seed)
    ks = iter(jax.random.split(key, 48))

    def nrm(shape, scale):
        return jax.random.normal(next(ks), shape, F32) * scale

    n_pages = PAST_LEN // PAGE_SIZE
    n_phys = (DEC_BATCH * n_pages * 5) // 4
    d = {}
    d["x_prompt"] = nrm((BATCH, SEQ, D_MODEL), 1.0)
    d["x_sample"] = nrm((DEC_BATCH, DEC_SEQ, D_MODEL), 1.0)
    d["mem_prompt"] = nrm((BATCH, MEM_TOKENS, D_MODEL), 1.0)
    d["state_delta"] = nrm((N_A_LAYERS, DEC_BATCH, DN_HEADS, DN_DK, DN_DV), 0.5)
    d["cache_conv"] = nrm((N_A_LAYERS, DEC_BATCH, CONV_W - 1, CONV_CH), 1.0)
    d["cache_kv_latent"] = nrm((n_phys, PAGE_SIZE, KV_LORA), 1.0)
    d["cache_k_rope"] = nrm((n_phys, PAGE_SIZE, QK_ROPE), 1.0)
    d["cache_mem_k"] = nrm((DEPTH, DEC_BATCH, MEM_TOKENS, MEM_HEADS, MEM_HD), 1.0)
    d["cache_mem_v"] = nrm((DEPTH, DEC_BATCH, MEM_TOKENS, MEM_HEADS, MEM_HD), 1.0)
    perm = jax.random.permutation(next(ks), n_phys)
    d["page_table"] = perm[:DEC_BATCH * n_pages].reshape(DEC_BATCH, n_pages).astype(jnp.int32)
    d["g_mix"] = 1.0 + nrm((DEPTH, D_MODEL), 0.05)
    d["g_ffn"] = 1.0 + nrm((DEPTH, D_MODEL), 0.05)
    d["g_final"] = 1.0 + nrm((D_MODEL,), 0.05)
    d["w_in_a"] = nrm((N_A_LAYERS, D_MODEL, IN_A), D_MODEL ** -0.5)
    d["conv_w"] = nrm((N_A_LAYERS, CONV_W, CONV_CH), 0.5)
    d["a_log"] = jnp.log(jax.random.uniform(next(ks), (N_A_LAYERS, DN_HEADS), F32, 1.0, 16.0))
    dt = jnp.exp(jax.random.uniform(next(ks), (N_A_LAYERS, DN_HEADS), F32, math.log(1e-3), math.log(1e-1)))
    d["dt_bias"] = dt + jnp.log(-jnp.expm1(-dt))
    d["g_onorm"] = 1.0 + nrm((N_A_LAYERS, DN_DV), 0.05)
    d["w_out_a"] = nrm((N_A_LAYERS, OUT_A, D_MODEL), OUT_A ** -0.5)
    d["g_kv_in"] = 1.0 + nrm((D_MODEL,), 0.05)
    d["w_dkv"] = nrm((D_MODEL, KV_LORA + QK_ROPE), D_MODEL ** -0.5)
    d["g_kv_latent"] = 1.0 + nrm((KV_LORA,), 0.05)
    d["w_uk"] = nrm((KV_LORA, MLA_HEADS, QK_NOPE), KV_LORA ** -0.5)
    d["w_uv"] = nrm((KV_LORA, MLA_HEADS, V_HEAD), KV_LORA ** -0.5)
    d["w_in_b"] = nrm((N_B_LAYERS, D_MODEL, IN_B), D_MODEL ** -0.5)
    d["g_q"] = 1.0 + nrm((N_B_LAYERS, Q_LORA), 0.05)
    d["w_uq"] = nrm((N_B_LAYERS, Q_LORA, MLA_HEADS * (QK_NOPE + QK_ROPE)), Q_LORA ** -0.5)
    d["w_out_b"] = nrm((N_B_LAYERS, OUT_B, D_MODEL), OUT_B ** -0.5)
    d["g_mem"] = 1.0 + nrm((DEPTH, D_MODEL), 0.05)
    d["w_mem_k"] = nrm((DEPTH, D_MODEL, MEM_W), D_MODEL ** -0.5)
    d["w_mem_v"] = nrm((DEPTH, D_MODEL, MEM_W), D_MODEL ** -0.5)
    d["w_router_group"] = nrm((DEPTH, D_MODEL, N_GROUPS), D_MODEL ** -0.5)
    d["b_router_group"] = nrm((DEPTH, N_GROUPS), 0.01)
    d["w_router_expert"] = nrm((DEPTH, D_MODEL, N_EXPERTS), D_MODEL ** -0.5)
    d["b_router_expert"] = nrm((DEPTH, N_EXPERTS), 0.01)
    d["w_exp_gate"] = nrm((DEPTH, N_EXPERTS, D_MODEL, EXPERT_FF), D_MODEL ** -0.5)
    d["w_exp_up"] = nrm((DEPTH, N_EXPERTS, D_MODEL, EXPERT_FF), D_MODEL ** -0.5)
    d["w_exp_down"] = nrm((DEPTH, N_EXPERTS, EXPERT_FF, D_MODEL), EXPERT_FF ** -0.5)
    return d

def reference(x_prompt, x_sample, mem_prompt, state_delta, cache_conv, cache_kv_latent, cache_k_rope,
              cache_mem_k, cache_mem_v, page_table, g_mix, g_ffn, g_final, w_in_a, conv_w, a_log, dt_bias,
              g_onorm, w_out_a, g_kv_in, w_dkv, g_kv_latent, w_uk, w_uv, w_in_b, g_q, w_uq, w_out_b,
              g_mem, w_mem_k, w_mem_v, w_router_group, b_router_group, w_router_expert, b_router_expert,
              w_exp_gate, w_exp_up, w_exp_down):
    past_len = page_table.shape[1] * PAGE_SIZE

    def run(x, pos, mem_k, mem_v, conv_bufs, d_states, paged):
        cos, sin = rope_tables(pos)
        new_bufs, new_states = [], []
        c_kv, k_rope = None, None
        for l in range(DEPTH):
            u = rms_norm(x, g_mix[l])
            if l < N_A_LAYERS:
                mix, buf, st = deltanet_mixer(u, conv_bufs[l], d_states[l], mem_k[l], mem_v[l], w_in_a[l],
                                              conv_w[l], a_log[l], dt_bias[l], g_onorm[l], w_out_a[l])
                new_bufs.append(buf)
                new_states.append(st)
            else:
                b = l - N_A_LAYERS
                mix = mla_mixer(u, c_kv, k_rope, mem_k[l], mem_v[l], w_in_b[b], g_q[b], w_uq[b], w_uk, w_uv,
                                w_out_b[b], cos, sin, paged)
            x = x + mix
            x = x + hier_moe(rms_norm(x, g_ffn[l]), w_router_group[l], b_router_group[l], w_router_expert[l],
                             b_router_expert[l], w_exp_gate[l], w_exp_up[l], w_exp_down[l])
            if l == N_A_LAYERS - 1:
                c_kv, k_rope = shared_latent_kv(x, g_kv_in, w_dkv, g_kv_latent, cos, sin)
        return rms_norm(x, g_final), c_kv, k_rope, jnp.stack(new_bufs), jnp.stack(new_states)

    Bp, Lp, _ = x_prompt.shape
    mkv = [memory_kv(mem_prompt, g_mem[l], w_mem_k[l], w_mem_v[l]) for l in range(DEPTH)]
    mem_k_prompt = jnp.stack([m[0] for m in mkv])
    mem_v_prompt = jnp.stack([m[1] for m in mkv])
    conv0 = jnp.zeros((N_A_LAYERS, Bp, CONV_W - 1, CONV_CH), x_prompt.dtype)
    state0 = jnp.zeros((N_A_LAYERS, Bp, DN_HEADS, DN_DK, DN_DV), x_prompt.dtype)
    y_prompt, kv_latent_prompt, k_rope_prompt, cache_conv_prompt, state_delta_prompt = run(
        x_prompt, jnp.arange(Lp), mem_k_prompt, mem_v_prompt, conv0, state0, None)

    Ls = x_sample.shape[1]
    y_sample, kv_latent_sample, k_rope_sample, cache_conv_sample, state_delta_sample = run(
        x_sample, past_len + jnp.arange(Ls), cache_mem_k, cache_mem_v, cache_conv, state_delta,
        (cache_kv_latent, cache_k_rope, page_table))

    return (y_prompt, y_sample, kv_latent_prompt, k_rope_prompt, kv_latent_sample, k_rope_sample,
            state_delta_prompt, cache_conv_prompt, state_delta_sample, cache_conv_sample,
            mem_k_prompt, mem_v_prompt)


_drawn_inputs = setup_inputs


def setup_inputs(seed=0):
    import zlib

    import numpy as np

    out = dict(_drawn_inputs(seed))
    spreads = {}
    factors = {'g_q': 2.887}
    for name, (base, spread) in spreads.items():
        noise = np.random.default_rng([zlib.crc32(name.encode()), seed]).standard_normal(out[name].shape)
        drawn = base * np.exp(spread * noise) if base else spread * noise
        out[name] = jnp.asarray(drawn.astype(out[name].dtype))
    for name, factor in factors.items():
        out[name] = (out[name] * factor).astype(out[name].dtype)
    return out
```

```python
from contextlib import ExitStack

import numpy as np

import concourse.bass as bass
from concourse import mybir

P = 128
F32 = mybir.dt.float32
I32 = mybir.dt.int32
U32 = mybir.dt.uint32
ALU = mybir.AluOpType
ACT = mybir.ActivationFunctionType
AX = mybir.AxisListType.X

D = 1024
DJ = D // P
SEQ, DB, DS = 512, 8, 4
NS = DB * DS
T = SEQ + NS
NC_P = SEQ // P
NCH = NC_P + 1
DN_H = 6
CONV_W = 4
CONV_CH = 3 * DN_H * P
MEM, MH, MHD = 256, 4, 64
QL, KL, RP = 384, 256, 64
NE, NG, EPG, FF = 32, 4, 8, 256
SLOTS = 64
EPS = 1e-6
BIG = 1e30
PAST = 2048
PAGE = 128
NPG = PAST // PAGE
MLA_SCALE = (P + RP) ** -0.5
OVER = 2 * T // SLOTS
XS_ROWS = 2 * T + SLOTS

ROWS = [P] * NC_P + [NS]
LEVELS = [1, 2, 4, 8, 16, 32, 64]


def shape_constants():
    i, j = np.arange(P)[:, None], np.arange(P)[None, :]
    parts = {}
    parts["ident"] = (i == j)
    parts["upper"] = (i <= j)
    parts["lower_big"] = np.where(i > j, 0.0, BIG)
    parts["upper_neg"] = np.where(i <= j, 0.0, -BIG)
    parts["ones"] = np.ones((P, P))
    for s in LEVELS:
        parts[f"level{s}"] = ((i // s) % 2 == 1) & (j // s == i // s - 1)
    parts["level1T"] = (((i // 1) % 2 == 1) & (j // 1 == i // 1 - 1)).T
    same = (i // DS == j // DS) & (i < NS) & (j < NS)
    parts["upper_s"] = ((i <= j) & same)[:, :NS]
    parts["lower_s"] = ((i > j) & same)[:, :NS]
    parts["same_s"] = same[:, :NS]
    b, t = np.arange(DB)[None, :, None], np.arange(NS)[None, None, :]
    parts["row_of"] = np.broadcast_to(t // DS == b, (P, DB, NS)).reshape(P, -1)
    parts["col_of"] = (np.arange(P)[:, None] // DS == np.arange(DB)[None, :])
    pos = np.concatenate([np.arange(SEQ), np.tile(PAST + np.arange(DS), DB)]).astype(np.float32)
    inv = (np.float32(10000.0) ** (-np.arange(0, RP, 2, dtype=np.float32) / np.float32(RP))).astype(np.float32)
    ang = pos[:, None] * inv[None, :]
    for name, f in (("cos", np.cos), ("sin", np.sin)):
        a = np.zeros((NCH * P, RP // 2), np.float32)
        a[:T] = f(ang)
        parts[name] = a.reshape(NCH, P, RP // 2).transpose(1, 0, 2).reshape(P, -1)
    parts["experts"] = np.broadcast_to(np.arange(NE)[None, :], (P, NE))
    parts["rows"] = np.arange(P)[:, None]
    parts["over_shift"] = SLOTS * (np.arange(P)[:, None] + 1)
    parts["first_of_4"] = np.broadcast_to(NG - np.arange(NG)[None, :], (P, NG))
    parts["first_of_32"] = np.broadcast_to(NE - np.arange(NE)[None, :], (P, NE))
    hq = np.arange(P)[:, None, None] % DS
    bb, tt = np.arange(DB)[None, :, None], np.arange(NS)[None, None, :]
    parts["new_keys"] = np.where((tt // DS == bb) & (tt % DS <= hq), 0.0, -BIG).reshape(P, -1)
    parts["same_row"] = (i % 32 == j % 32)
    parts["eighth"] = np.arange(P)[:, None] % 8
    parts["causal"] = np.where(j <= i, 0.0, -BIG)
    at, cols = {}, 0
    for n, a in parts.items():
        at[n] = (cols, a.shape[1])
        cols += a.shape[1]
    return at, np.ascontiguousarray(np.concatenate([np.asarray(a, np.float32) for a in parts.values()], 1))


CONST_AT, CONSTS = shape_constants()


class Chain:

    def __init__(self, eng, sem):
        self.eng, self.sem, self.n = eng, sem, 0

    def __call__(self, ins):
        ins.then_inc(self.sem, 1)
        self.n += 1
        self.eng.wait_ge(self.sem, self.n)


def wait_after(eng, sem, value):
    if value > 0:
        eng.wait_ge(sem, value)


def build(nc, I, O, debug=()):
    ctx = ExitStack()
    with ctx:
        def sb(name, shape, dt=F32, where=ctx):
            return where.enter_context(nc.sbuf_tensor(name, shape, dt))

        stage_sems = []

        def sem(name):
            s = nc.alloc_semaphore(name=name)
            stage_sems.append(s)
            return s

        def reuse_semaphores():
            nc.clear_and_free_semaphores(stage_sems)
            nc.all_engine_barrier()
            stage_sems.clear()

        pp = [ctx.enter_context(nc.psum_tensor(f"pp{i}", [P, 1024], F32)) for i in range(4)]
        V, S, TE, G = nc.vector, nc.scalar, nc.tensor, nc.gpsimd

        consts = sb("consts", [P, CONSTS.shape[1]])

        def const(name):
            at, n = CONST_AT[name]
            return consts[:, at:at + n]

        ident, ones = const("ident"), const("ones")

        def bc(ap, axis, n):
            a = ap.unsqueeze(axis)
            shape = list(a.shape)
            shape[axis] = n
            return a.to_broadcast(shape)

        x = sb("x", [P, NCH, D])
        uT = sb("uT", [P, DJ, T])
        ring = [sb(f"ring{i}", [P, 6144]) for i in range(2)]
        gains = sb("gains", [P, 7, DJ])
        G_MIX, G_FFN, G_KV, G_MEM = 0, 2, 4, 5
        mem_kT = sb("mem_kT", [P, 2, 2, MEM])
        mem_v = sb("mem_v", [P, 2, 2, MEM])
        small = sb("small", [P, 12 + 36 * 2])
        landed = {}

        s_in = sem("inputs_landed")
        s_ring = [sem(f"ring{i}_landed") for i in range(2)]
        ring_count = [0, 0]
        stage_sems.clear()

        def load(eng, slot, name, *pairs):
            for dst, src in pairs:
                eng.dma_start(dst, src).then_inc(s_ring[slot], 16)
                ring_count[slot] += 16
            landed[name] = (s_ring[slot], ring_count[slot])

        def arrived(eng, name):
            eng.wait_ge(*landed[name])

        def pj(ap):
            return ap.rearrange("(p j) n -> p j n", p=P)

        def slot3(slot, n, j=DJ):
            return ring[slot][:, 0:j * n].rearrange("p (j n) -> p j n", j=j)

        def offset(c):
            return c * P

        HALVES = ((slice(0, T // 2), slice(0, T // 2)), (slice(T // 2, T), slice(512, 512 + T // 2)))

        def halves(q):
            return q[:].rearrange("p (b t) -> p b t", b=2)[:, :, 0:T // 2]

        def all_tokens(ap):
            return ap.rearrange("p (b t) -> p b t", b=2)

        debug_out = {}

        def dump(name, ap):
            if name in debug:
                d = nc.dram_tensor(f"dbg_{name}", tuple(ap.shape), F32, kind="ExternalOutput").ap()
                debug_out[name] = d
                s_dbg = sem(f"dbg_{name}")
                with nc.Block() as block:
                    @block.sync
                    def _(sp):
                        sp.dma_start(d, ap).then_inc(s_dbg, 16)
                        sp.wait_ge(s_dbg, 16)

        def norm_transposed(tag, src, rows, gain_to, waits=(), sync_extra=None, kept_rows=None, on_chunk=None):
            n = len(rows)
            with ExitStack() as cx:
                junk = sb(f"{tag}_junk", [P, 2, D], where=cx)
                nb = 2 if kept_rows is None else n
                xn = sb(f"{tag}_xn", [P, 2, D], where=cx) if kept_rows is None else kept_rows
                ss = sb(f"{tag}_ss", [P, n], where=cx)
                s_ss, s_dve, s_rt, s_xn, s_tr, s_ev = (sem(f"{tag}_{m}") for m in ("squares", "dve", "root", "scaled", "turned", "kept"))
                with nc.Block() as block:
                    if sync_extra:
                        block.sync(sync_extra)

                    @block.scalar
                    def _(act):
                        act.wait_ge(s_dve, 1)
                        for w, v in waits:
                            act.wait_ge(w, v)
                        for c, r in enumerate(rows):
                            if c >= 2:
                                act.wait_ge(s_ss, c - 1)
                            S.activation(junk[:r, c % 2, :], src[:r, c, :], ACT.Square, accum_out=ss[:r, c:c + 1]).then_inc(s_ss, 1)
                        act.wait_ge(s_dve, 2)
                        S.activation(ss[:], ss[:], ACT.Sqrt).then_inc(s_rt, 1)

                    def keep(dve, c):
                        r = rows[c]
                        dve.wait_ge(s_tr, c + 1)
                        for g, dst in gain_to:
                            V.tensor_tensor(dst[:, :, offset(c):offset(c) + r],
                                            pp[c % 2][:].rearrange("p (j t) -> p j t", j=DJ)[:, :, :r],
                                            bc(gains[:, g, :], 2, r), ALU.mult).then_inc(s_ev, 1)

                    @block.vector
                    def _(dve):
                        chain = Chain(dve, s_dve)
                        for w, v in waits:
                            dve.wait_ge(w, v)
                        chain(V.memset(ss[:], 1.0))
                        dve.wait_ge(s_ss, n)
                        chain(V.tensor_scalar(ss[:], ss[:], 1.0 / D, EPS, ALU.mult, ALU.add))
                        dve.wait_ge(s_rt, 1)
                        chain(V.reciprocal(ss[:], ss[:]))
                        for c, r in enumerate(rows):
                            if c >= nb:
                                dve.wait_ge(s_tr, c - nb + 1)
                            V.tensor_scalar(xn[:r, c % nb, :], src[:r, c, :], ss[:r, c:c + 1], None, ALU.mult).then_inc(s_xn, 1)
                            if c >= 1:
                                keep(dve, c - 1)
                        keep(dve, n - 1)

                    @block.tensor
                    def _(pe):
                        for c, r in enumerate(rows):
                            pe.wait_ge(s_xn, c + 1)
                            if c >= 2:
                                pe.wait_ge(s_ev, len(gain_to) * (c - 1))
                            xv = xn[:r, c % nb, :].rearrange("t (p j) -> t j p", j=DJ)
                            for j in range(DJ):
                                m = TE.transpose(pp[c % 2][:, j * P:j * P + r], xv[:, j, :], ident[:r, :r])
                            m.then_inc(s_tr, 1)
                            if on_chunk and c >= 1:
                                pe.wait_ge(s_ev, len(gain_to) * c)
                                on_chunk(c - 1)
                        if on_chunk:
                            pe.wait_ge(s_ev, len(gain_to) * n)
                            on_chunk(n - 1)

        xs = nc.dram_tensor("sorted_rows", (XS_ROWS, D), F32, kind="Internal").ap()
        ys = nc.dram_tensor("expert_rows", ((NE + OVER) * SLOTS, D), F32, kind="Internal").ap()
        over_rows = nc.dram_tensor("over_table", (P, 2), I32, kind="Internal").ap()

        n_in = 0
        w_rt = sb("router_weights", [P, 2, DJ, NG + NE])
        conv_wT = sb("conv_wT", [P, CONV_W * 18])
        g_on = sb("g_on", [P, P])
        mem_x = ctx.enter_context(ExitStack())
        mx = sb("mem_x", [P, 2, D], where=mem_x)
        mT = sb("mem_T", [P, 2, DJ, MEM], where=mem_x)
        conv_rows = sb("conv_rows", [CONV_W * 18, P], where=mem_x)

        def load_inputs(sp):
            nonlocal n_in
            loads = [(mx[:], I["mem_prompt"][0].rearrange("(c p) d -> p c d", p=P)),
                     (consts[:], I["consts"])]
            for k, ap in ((G_MEM, I["g_mem"][0]), (G_MEM + 1, I["g_mem"][1]), (G_MIX, I["g_mix"][0]), (G_MIX + 1, I["g_mix"][1]),
                          (G_FFN, I["g_ffn"][0]), (G_FFN + 1, I["g_ffn"][1]), (G_KV, I["g_kv_in"])):
                loads.append((gains[:, k, :], ap.rearrange("(p j) -> p j", p=P)))
            loads += [(x[:, 0:NC_P, :], I["x_prompt"][0].rearrange("(c p) d -> p c d", p=P)),
                      (x[0:NS, NC_P, :], I["x_sample"].rearrange("b s d -> (b s) d")),
                      (conv_rows[:], I["conv_w"][0].rearrange("w (c p) -> (w c) p", p=P)),
                      (g_on[:], I["g_onorm"][0].partition_broadcast(P)),
                      (small[:, 0:6], I["a_log"][0].partition_broadcast(P)),
                      (small[:, 6:12], I["dt_bias"][0].partition_broadcast(P))]
            for l in range(2):
                loads += [(small[:, 12 + 36 * l:16 + 36 * l], I["b_router_group"][l].partition_broadcast(P)),
                          (small[:, 16 + 36 * l:48 + 36 * l], I["b_router_expert"][l].partition_broadcast(P))]
                loads += [(w_rt[:, l, :, 0:NG], pj(I["w_router_group"][l])), (w_rt[:, l, :, NG:], pj(I["w_router_expert"][l]))]
            for dst, src in loads:
                sp.dma_start(dst, src).then_inc(s_in, 16)
                n_in += 16
                if n_in == 16 * 9:
                    for l in range(2):
                        w = slot3(l, 2 * MEM)
                        load(sp, l, f"mem{l}", (w[:, :, 0:MEM], pj(I["w_mem_k"][l])), (w[:, :, MEM:2 * MEM], pj(I["w_mem_v"][l])))
            sp.wait_ge(s_in, n_in)

        with nc.Block() as block:
            block.sync(load_inputs)

        norm_transposed("memn", mx, [P, P], [(G_MEM, mT[:, 0]), (G_MEM + 1, mT[:, 1])])
        w_in = pj(I["w_in_a"][0])
        Z0 = CONV_CH
        R0 = Z0 + DN_H * P
        NR = 2 * DN_H + MH * MHD

        with ExitStack() as cx:
            kv = sb("mem_kv_rows", [P, 4, 2 * MEM], where=cx)
            s_mm, s_ev, s_tr, s_k, s_st = (sem(f"memkv_{m}") for m in ("product", "kept", "turned", "keys", "stored"))
            with nc.Block() as block:
                @block.tensor
                def _(pe):
                    for n in range(4):
                        l, m = divmod(n, 2)
                        arrived(pe, f"mem{l}")
                        w = slot3(l, 2 * MEM)
                        for j in range(DJ):
                            ins = TE.matmul(pp[n % 2][:, 0:512], mT[:, l, j, m * P:(m + 1) * P], w[:, j, :], start=(j == 0), stop=(j == DJ - 1))
                        ins.then_inc(s_mm, 1)
                        pe.wait_ge(s_ev, n + 1)
                        if n >= 2:
                            pe.wait_ge(s_k, 2 * (n - 1))
                        for pr in range(2):
                            ins = TE.transpose(pp[2 + n % 2][:, pr * P:(pr + 1) * P], kv[:, n, pr * P:(pr + 1) * P], ident)
                        ins.then_inc(s_tr, 1)
                    TE.transpose(pp[0][:, 0:72], conv_rows[:], ident[0:72, 0:72]).then_inc(s_tr, 1)

                @block.scalar
                def _(act):
                    for n in range(4):
                        act.wait_ge(s_mm, n + 1)
                        S.activation(kv[:, n, :], pp[n % 2][:, 0:512], ACT.Copy).then_inc(s_ev, 1)

                @block.vector
                def _(dve):
                    for n in range(4):
                        l, m = divmod(n, 2)
                        dve.wait_ge(s_tr, n + 1)
                        V.tensor_copy(mem_kT[:, l, :, m * P:(m + 1) * P], pp[2 + n % 2][:, 0:MEM].rearrange("p (a m) -> p a m", a=2)).then_inc(s_k, 1)
                        V.tensor_copy(mem_v[:, l, m, :], kv[:, n, MEM:2 * MEM]).then_inc(s_k, 1)
                    dve.wait_ge(s_tr, 5)
                    V.tensor_copy(conv_wT[:], pp[0][:, 0:72]).then_inc(s_k, 1)

                @block.sync
                def _(sp):
                    for n in range(4):
                        l, m = divmod(n, 2)
                        sp.wait_ge(s_ev, n + 1)
                        for k, o in ((0, "mem_k_prompt"), (1, "mem_v_prompt")):
                            sp.dma_start(O[o][l, 0].rearrange("m h d -> m (h d)")[m * P:(m + 1) * P, :],
                                         kv[:, n, k * MEM:(k + 1) * MEM]).then_inc(s_st, 16)
                    sp.wait_ge(s_mm, 4)
                    load(sp, 0, "q", (slot3(0, 768), w_in[:, :, 0:768]))
                    load(sp, 1, "k", (slot3(1, 768), w_in[:, :, 768:1536]))
                    sp.wait_ge(s_st, 16 * 8)
        mem_x.close()

        norm_transposed("norm0", x, ROWS, [(G_MIX, uT)])
        L0 = ctx.enter_context(ExitStack())
        toks = sb("qkv_rows", [P, 3, NCH, 768], where=L0)
        tok = [toks[:, g] for g in range(3)]
        zs = sb("z_rows", [P, NCH, 768], where=L0)
        ab = sb("ab", [P, NCH, 12], where=L0)
        qmT = sb("qmT", [P, 2, T], where=L0)
        IN = ctx.enter_context(ExitStack())
        CW = 3 + SEQ + DB * (3 + DS)
        CN = CW - 3
        raw = sb("conv_in", [P, 2, CW], where=IN)
        yc = sb("conv_sum", [P, 2, CW], where=IN)
        ya = sb("conv_out", [P, 2, T], where=IN)
        crow = sb("conv_tail", [P, 2, 27], where=IN)
        cache_in = sb("cache_rows", [24, CONV_CH], where=IN)
        cache_out = sb("cache_out_rows", [27, CONV_CH], where=IN)
        zero = sb("zero_rows", [SLOTS, D // 2], where=IN)
        w_out = I["w_out_a"][0].rearrange("(j p) n -> p j n", p=P)
        NT = 18
        with nc.Block() as block:
            s_c, s_mm, s_raw, s_ch, s_sum, s_silu, s_tail, s_tr, s_tok, s_free, s_z, s_zk, s_st, s_zero, s_zrow = (
                sem(f"in_{m}") for m in ("cache", "product", "raw", "chain", "summed", "silu", "tail", "turned", "rows", "slot_free", "z", "z_kept", "stored", "zeroed", "zero_row"))

            @block.sync
            def _(sp):
                sp.dma_start(cache_in[:], I["cache_conv"][0].rearrange("b r c -> (b r) c")).then_inc(s_c, 16)
                sp.wait_ge(s_zrow, 1)
                sp.dma_start(xs[2 * T:XS_ROWS, :].rearrange("s (q d) -> s q d", q=2), bc(zero[:], 1, 2)).then_inc(s_st, 16)
                for q in range(2):
                    sp.dma_start(ys[NE * SLOTS:, q * 512:(q + 1) * 512].rearrange("(j s) d -> s j d", s=SLOTS), bc(zero[:], 1, OVER)).then_inc(s_st, 16)
                for n, (slot, name, a, b) in enumerate((((0, "v", 1536, Z0)), (1, "z", Z0, R0), (0, "rest", R0, R0 + NR))):
                    sp.wait_ge(s_free, n + 1)
                    load(sp, slot, name, (slot3(slot, b - a), w_in[:, :, a:b]))
                for n, slot in ((0, 1), (1, 0)):
                    sp.wait_ge(s_free, 4 + n)
                    load(sp, slot, f"out{n}", (slot3(slot, 512), w_out[:, :, n * 512:(n + 1) * 512]))
                sp.wait_ge(s_tok, NT)
                sp.dma_start(O["cache_conv_prompt"][0, 0], cache_out[0:3, :]).then_inc(s_st, 16)
                sp.dma_start(O["cache_conv_sample"][0].rearrange("b r c -> (b r) c"), cache_out[3:27, :]).then_inc(s_st, 16)
                sp.wait_ge(s_st, 80)

            @block.gpsimd
            def _(pool):
                G.memset(zero[:], 0.0).then_inc(s_zrow, 1)

            @block.tensor
            def _(pe):
                def turn(n):
                    pe.wait_ge(s_silu, 2 * (n + 1))
                    pe.wait_ge(s_tail, n + 1)
                    if n >= 2:
                        pe.wait_ge(s_tok, n - 1)
                    for c in range(NC_P):
                        TE.transpose(pp[2 + n % 2][:, c * P:(c + 1) * P], ya[:, n % 2, c * P:(c + 1) * P], ident)
                    TE.transpose(pp[2 + n % 2][0:NS, 512:640], ya[:, n % 2, SEQ:T], ident)
                    TE.transpose(pp[2 + n % 2][0:27, 640:768], crow[:, n % 2, :], ident).then_inc(s_tr, 1)

                pe.wait_ge(s_c, 16)
                for n in range(NT):
                    g, ct = divmod(n, 6)
                    if ct == 0:
                        arrived(pe, "qkv"[g])
                    w = slot3(g % 2, 768)
                    if n >= 2:
                        pe.wait_ge(s_raw, n - 1)
                    TE.transpose(pp[n % 2][:, 784:808], cache_in[:, n * P:(n + 1) * P], ident[0:24, 0:24])
                    for t, at in HALVES:
                        for j in range(DJ):
                            ins = TE.matmul(pp[n % 2][:, at], w[:, j, ct * P:(ct + 1) * P], uT[:, j, t], start=(j == 0), stop=(j == DJ - 1))
                    ins.then_inc(s_mm, 1)
                    if n >= 1:
                        turn(n - 1)
                    if ct == 5:
                        pe.wait_ge(s_mm, n + 1)
                        pe.sem_inc(s_free, 1)
                turn(NT - 1)
                arrived(pe, "z")
                w = slot3(1, 768)
                pe.wait_ge(s_raw, NT)
                for c, r in enumerate(ROWS):
                    if c >= 2:
                        pe.wait_ge(s_zk, 2 * (c - 1))
                    for o, k in ((0, 512), (512, 256)):
                        for j in range(DJ):
                            ins = TE.matmul(pp[c % 2][:r, o:o + k], uT[:, j, offset(c):offset(c) + r], w[:, j, o:o + k], start=(j == 0), stop=(j == DJ - 1))
                    ins.then_inc(s_z, 1)
                pe.wait_ge(s_z, NCH)
                pe.sem_inc(s_free, 1)
                arrived(pe, "rest")
                w = slot3(0, NR)
                pe.wait_ge(s_tok, NT)
                for c, r in enumerate(ROWS):
                    for j in range(DJ):
                        ins = TE.matmul(pp[2][:r, c * 12:(c + 1) * 12], uT[:, j, offset(c):offset(c) + r], w[:, j, 0:12], start=(j == 0), stop=(j == DJ - 1))
                ins.then_inc(s_z, 1)
                for pr in range(2):
                    pe.wait_ge(s_zk, 2 * (NC_P + pr))
                    for t, at in HALVES:
                        for j in range(DJ):
                            ins = TE.matmul(pp[1 - pr][:, at], w[:, j, 12 + pr * P:12 + (pr + 1) * P], uT[:, j, t], start=(j == 0), stop=(j == DJ - 1))
                    ins.then_inc(s_z, 1)
                pe.wait_ge(s_z, NCH + 3)
                pe.sem_inc(s_free, 1)

            @block.vector
            def _(dve):
                chain = Chain(dve, s_ch)
                for t in (*tok, zs, ab):
                    V.memset(t[:, NC_P, :], 0.0).then_inc(s_zero, 1)
                chain(V.memset(raw[:, :, 0:3], 0.0))
                for n in range(NT):
                    k = n % 2
                    dve.wait_ge(s_mm, n + 1)
                    if n >= 2:
                        dve.wait_ge(s_tail, n - 1)
                        dve.wait_ge(s_silu, 2 * (n - 1))
                    sv = raw[:, k, 3 + SEQ:CW].rearrange("p (b r) -> p b r", b=DB)
                    chain(V.tensor_copy(raw[:, k, 3:3 + T // 2], pp[k][:, 0:T // 2]))
                    chain(V.tensor_copy(raw[:, k, 3 + T // 2:3 + SEQ], pp[k][:, 512:784 - NS]))
                    chain(V.tensor_copy(sv[:, :, 3:7], pp[k][:, 784 - NS:784].rearrange("p (b r) -> p b r", b=DB)))
                    ins = V.tensor_copy(sv[:, :, 0:3], pp[k][:, 784:808].rearrange("p (b r) -> p b r", b=DB))
                    chain(ins)
                    dve.sem_inc(s_raw, 1)
                    for j in range(CONV_W):
                        wj = conv_wT[:, j * 18 + n:j * 18 + n + 1]
                        if j == 0:
                            chain(V.tensor_scalar(yc[:, k, 0:CN], raw[:, k, 0:CN], wj, None, ALU.mult))
                        elif j < CONV_W - 1:
                            chain(V.scalar_tensor_tensor(yc[:, k, 0:CN], raw[:, k, j:j + CN], wj, yc[:, k, 0:CN], ALU.mult, ALU.add))
                        else:
                            V.scalar_tensor_tensor(yc[:, k, 0:CN], raw[:, k, j:j + CN], wj, yc[:, k, 0:CN], ALU.mult, ALU.add).then_inc(s_sum, 1)
                    if n >= 2:
                        dve.wait_ge(s_tr, n - 1)
                    chain(V.tensor_copy(crow[:, k, 0:3], raw[:, k, SEQ:SEQ + 3]))
                    V.tensor_copy(crow[:, k, 3:27].rearrange("p (b r) -> p b r", b=DB), sv[:, :, 4:7]).then_inc(s_tail, 1)
                dve.wait_ge(s_z, NCH + 1)
                dve.wait_ge(s_zero, 5)
                chain(V.tensor_copy(ab[:, 0:NC_P, :], pp[2][:, 0:12 * NC_P].rearrange("p (c k) -> p c k", c=NC_P)))
                chain(V.tensor_copy(ab[0:NS, NC_P, :], pp[2][0:NS, 12 * NC_P:12 * NCH]))
                for pr in range(2):
                    dve.wait_ge(s_z, NCH + 2 + pr)
                    chain(V.tensor_copy(all_tokens(qmT[:, pr, :]), halves(pp[1 - pr])))

            @block.scalar
            def _(act):
                act.wait_ge(s_zero, 5)

                def rows(n):
                    g, ct = divmod(n, 6)
                    act.wait_ge(s_tr, n + 1)
                    q = pp[2 + n % 2]
                    S.activation(tok[g][:, 0:NC_P, ct * P:(ct + 1) * P], q[:, 0:512].rearrange("p (c t) -> p c t", c=NC_P), ACT.Copy)
                    S.activation(tok[g][0:NS, NC_P, ct * P:(ct + 1) * P], q[0:NS, 512:640], ACT.Copy)
                    S.activation(cache_out[:, n * P:(n + 1) * P], q[0:27, 640:768], ACT.Copy).then_inc(s_tok, 1)

                for n in range(NT):
                    k = n % 2
                    act.wait_ge(s_sum, n + 1)
                    if n >= 2:
                        act.wait_ge(s_tr, n - 1)
                    S.activation(ya[:, k, 0:SEQ], yc[:, k, 0:SEQ], ACT.Silu).then_inc(s_silu, 1)
                    S.activation(ya[:, k, SEQ:T].rearrange("p (b r) -> p b r", b=DB),
                                 yc[:, k, 3 + SEQ:CW].rearrange("p (b r) -> p b r", b=DB)[:, :, 0:DS], ACT.Silu).then_inc(s_silu, 1)
                    if n >= 1:
                        rows(n - 1)
                rows(NT - 1)
                for c, r in enumerate(ROWS):
                    act.wait_ge(s_z, c + 1)
                    S.activation(zs[:r, c, 0:512], pp[c % 2][:r, 0:512], ACT.Silu).then_inc(s_zk, 1)
                    S.activation(zs[:r, c, 512:768], pp[c % 2][:r, 512:768], ACT.Silu).then_inc(s_zk, 1)
        IN.close()
        dump("q_rows", tok[0][:])
        dump("v_rows", tok[2][:])
        dump("z_rows", zs[:])
        dump("ab", ab[:])
        dump("qmT", qmT[:])

        x_flat = x[:].rearrange("p c d -> p (c d)")
        uT_flat = uT[:].rearrange("p j t -> p (j t)")
        sx = L0
        qkT = sb("qkT", [P, 12, T], where=L0)
        gb = sb("decays", [P, 8, NCH, DN_H], where=L0)
        g_, G_, tot, eG, ekd, dec, beta, beG = (gb[:, k] for k in range(8))
        dS = sb("decay_s", [P, DB, DN_H], where=L0)
        with ExitStack() as cx:
            sq = [x_flat[:, 0:768 * NCH], uT_flat[:, 0:768 * NCH]]
            ss = sb("l2", [P, 2, NCH * DN_H], where=cx)
            gm = sb("g_masked", [NS, DB, DN_H], where=cx)
            t1 = sb("softplus", [P, 3, NCH, DN_H], where=cx)
            ea = sb("exp_a", [P, DN_H], where=cx)
            s_a, s_d, s_t, s_k, s_g, s_n = (sem(f"prep_{m}") for m in ("act", "dve", "turned", "kept", "sums", "scaled"))
            with nc.Block() as block:
                @block.scalar
                def _(act):
                    a = Chain(act, s_a)
                    for k in range(2):
                        a(S.activation(sq[k], tok[k][:].rearrange("p c n -> p (c n)"), ACT.Square))
                    act.wait_ge(s_d, 3)
                    a(S.activation(ss[:], ss[:], ACT.Sqrt))
                    act.wait_ge(s_d, 9)
                    a(S.activation(t1[:, 1], t1[:, 0], ACT.Abs))
                    a(S.activation(t1[:, 1], t1[:, 1], ACT.Exp, scale=-1.0))
                    a(S.activation(ea[:], small[:, 0:6], ACT.Exp))
                    a(S.activation(t1[:, 1], t1[:, 1], ACT.Ln, bias=1.0))
                    a(S.activation(beta, ab[:, :, 6:12], ACT.Sigmoid))
                    for n in range(12):
                        act.wait_ge(s_t, n + 1)
                        S.activation(qkT[:, n, 0:SEQ], pp[n % 2][:, 0:SEQ], ACT.Copy)
                        S.activation(qkT[:, n, SEQ:T], pp[n % 2][:, 512:512 + NS], ACT.Copy).then_inc(s_k, 1)
                    act.wait_ge(s_g, 2)
                    act.wait_ge(s_d, 18)
                    a(S.activation(eG, G_, ACT.Exp))
                    a(S.activation(ekd, ekd, ACT.Exp))
                    a(S.activation(dec, tot, ACT.Exp))
                    a(S.activation(dS[:], dS[:], ACT.Exp))

                @block.vector
                def _(dve):
                    d = Chain(dve, s_d)
                    for k in range(2):
                        dve.wait_ge(s_a, k + 1)
                        d(V.tensor_reduce(ss[:, k, :], sq[k].rearrange("p (n d) -> p n d", d=P), AX, ALU.add))
                    d(V.tensor_scalar(ss[:], ss[:], EPS, None, ALU.add))
                    dve.wait_ge(s_a, 3)
                    d(V.reciprocal(ss[:], ss[:]))
                    d(V.tensor_scalar(ss[:, 0, :], ss[:, 0, :], P ** -0.5, None, ALU.mult))
                    for k in range(2):
                        v = tok[k][:].rearrange("p c (h d) -> p (c h) d", d=P)
                        d(V.tensor_tensor(v, v, bc(ss[:, k, :], 2, P), ALU.mult))
                    d(V.tensor_tensor(t1[:, 0], ab[:, :, 0:6], bc(small[:, 6:12], 1, NCH), ALU.add))
                    d(V.tensor_scalar(t1[:, 2], t1[:, 0], 0.0, None, ALU.max))
                    dve.wait_ge(s_a, 8)
                    d(V.tensor_tensor(g_, t1[:, 1], t1[:, 2], ALU.add))
                    d(V.tensor_tensor(g_, g_, bc(ea[:], 1, NCH), ALU.mult))
                    d(V.tensor_scalar(g_, g_, -1.0, None, ALU.mult))
                    d(V.tensor_tensor(gm[:], bc(g_[0:NS, NC_P, :], 1, DB), bc(const("col_of")[0:NS, :], 2, DN_H), ALU.mult))
                    d(V.memset(gb[:, 1:3], 0.0))
                    dve.wait_ge(s_g, 1)
                    for k, o in ((G_, 0), (tot, 32)):
                        V.tensor_copy(k[:, 0:NC_P, :], pp[2][:, o:o + 24].rearrange("p (c h) -> p c h", h=DN_H))
                        d(V.tensor_copy(k[0:NS, NC_P, :], pp[2][0:NS, o + 24:o + 30]))
                    d(V.tensor_copy(dS[:], pp[2][:, 64:112].rearrange("p (b h) -> p b h", h=DN_H)))
                    d(V.tensor_tensor(ekd, tot, G_, ALU.subtract))
                    dve.wait_ge(s_a, 9)
                    d(V.tensor_tensor(beG, beta, eG, ALU.mult))

                @block.tensor
                def _(pe):
                    for n in range(12):
                        k, ct = divmod(n, 6)
                        pe.wait_ge(s_d, 6 + k)
                        if n >= 2:
                            pe.wait_ge(s_k, n - 1)
                        for c in range(NC_P):
                            TE.transpose(pp[n % 2][:, c * P:(c + 1) * P], tok[k][:, c, ct * P:(ct + 1) * P], ident)
                        TE.transpose(pp[n % 2][:, 512:512 + NS], tok[k][0:NS, NC_P, ct * P:(ct + 1) * P], ident[0:NS, 0:NS]).then_inc(s_t, 1)
                    pe.wait_ge(s_d, 14)
                    for c in range(NC_P):
                        TE.matmul(pp[2][:, c * 6:c * 6 + 6], const("upper"), g_[:, c, :], start=True, stop=True)
                        TE.matmul(pp[2][:, 32 + c * 6:38 + c * 6], ones, g_[:, c, :], start=True, stop=True)
                    TE.matmul(pp[2][0:NS, 24:30], const("upper_s")[0:NS, :], g_[0:NS, NC_P, :], start=True, stop=True)
                    TE.matmul(pp[2][0:NS, 56:62], const("same_s")[0:NS, :], g_[0:NS, NC_P, :], start=True, stop=True)
                    TE.matmul(pp[2][:, 64:112], ones[0:NS, :], gm[:].rearrange("p b h -> p (b h)"), start=True, stop=True).then_inc(s_g, 2)

        state = sb("state", [P, DN_H, P], where=L0)
        DL = ctx.enter_context(ExitStack())
        A, GT, AT, X, XT, Y = (x_flat[:, n * 768:(n + 1) * 768].rearrange("p (h t) -> p h t", h=DN_H) for n in range(6))
        Kb, Vb, Kd = (uT_flat[:, n * 768:(n + 1) * 768].rearrange("p (h t) -> p h t", h=DN_H) for n in range(3))
        wT = AT
        e = Y

        def delta_chunk(tag, c, r, first):
            prompt = False
            levels = LEVELS[1:2]
            upper, lower = const("upper_s"), const("lower_s")
            tk = slice(offset(c), offset(c) + r)
            W = DN_H * r

            def heads(t, n=r):
                return t[:n, :, :r]

            def ph(k, rows=r, w=r):
                return pp[k][:rows, 0:DN_H * w].rearrange("p (h t) -> p h t", h=DN_H)

            s_pe, s_d, s_a, s_g = (sem(f"{tag}_{m}") for m in ("pe", "dve", "act", "pool"))
            D_A, D_X = 8, 12
            return prompt, levels, upper, lower, tk, W, heads, ph, s_pe, s_d, s_a, s_g

        def delta_solve(tag, c, r, pe_tail, dve_tail, act_tail, sync_tail=None):
            prompt, levels, upper, lower, tk, W, heads, ph, s_pe, s_d, s_a, s_g = delta_chunk(tag, c, r, c == 0)
            q, k = (lambda h: qkT[:, h, tk]), (lambda h: qkT[:, DN_H + h, tk])
            n_lv = len(levels)
            with nc.Block() as block:
                if sync_tail:
                    @block.sync
                    def _(sp):
                        sync_tail(sp, s_pe, s_d, s_a, s_g, n_lv)

                @block.tensor
                def _(pe):
                    for h in range(DN_H):
                        TE.matmul(ph(0)[:, h, :], bc(g_[:r, c, h], 1, r), upper[:r, :r], start=True, stop=True)
                    for h in range(DN_H):
                        TE.matmul(ph(1)[:, h, :], k(h), k(h), start=True, stop=True)
                    for h in range(DN_H):
                        ins = TE.matmul(ph(2)[:, h, :], k(h), q(h), start=True, stop=True)
                    ins.then_inc(s_pe, 1)
                    pe.wait_ge(s_d, 8)
                    for h in range(DN_H):
                        ins = TE.transpose(ph(0)[:, h, :], A[:r, h, :r], ident[:r, :r])
                    ins.then_inc(s_pe, 1)
                    for n in range(n_lv):
                        pe.wait_ge(s_d, 12 + 3 * n)
                        for h in range(DN_H):
                            ins = TE.matmul(ph(1)[:, h, :], AT[:r, h, :r], X[:r, h, :r], start=True, stop=True)
                        ins.then_inc(s_pe, 1)
                        pe.wait_ge(s_d, 13 + 3 * n)
                        for h in range(DN_H):
                            TE.matmul(ph(2)[:, h, :], XT[:r, h, :r], Y[:r, h, :r], start=True, stop=True)
                        for h in range(DN_H):
                            ins = TE.matmul(ph(3)[:, h, :], Y[:r, h, :r], XT[:r, h, :r], start=True, stop=True)
                        ins.then_inc(s_pe, 1)
                    pe.wait_ge(s_d, 12 + 3 * n_lv)
                    pe.wait_ge(s_g, 1)
                    for h in range(DN_H):
                        ins = TE.matmul(ph(1, P, r)[:, h, :], Kb[:r, h, :], XT[:r, h, :r], start=True, stop=True)
                    ins.then_inc(s_pe, 1)
                    pe_tail(pe, s_pe, s_d, s_a, s_g, n_lv)

                @block.gpsimd
                def _(pool):
                    for dst, src, f in ((Kb, 1, beG), (Vb, 2, beta), (Kd, 1, ekd)):
                        G.tensor_tensor(dst[:r], tok[src][:r, c, :].rearrange("p (h d) -> p h d", h=DN_H), bc(f[:r, c, :], 2, P), ALU.mult).then_inc(s_g, 1)

                @block.scalar
                def _(act):
                    a = Chain(act, s_a)
                    act.wait_ge(s_d, 3)
                    a(S.activation(heads(A), heads(A), ACT.Exp, scale=-1.0))
                    a(S.activation(heads(GT), heads(GT), ACT.Exp))
                    act.wait_ge(s_pe, 2)
                    a(S.activation(heads(AT), ph(0), ACT.Copy))
                    act_tail(act, a, s_pe, s_d, s_a, s_g, n_lv)

                @block.vector
                def _(dve):
                    d = Chain(dve, s_d)
                    dve.wait_ge(s_pe, 1)
                    d(V.tensor_tensor(heads(Y), ph(0), bc(G_[:r, c, :], 2, r), ALU.subtract))
                    d(V.tensor_scalar(heads(A), heads(Y), 0.0, None, ALU.max))
                    d(V.tensor_scalar(heads(GT), heads(Y), 0.0, None, ALU.min))
                    dve.wait_ge(s_a, 2)
                    d(V.tensor_tensor(heads(A), heads(A), bc(lower[:r, :r], 1, DN_H), ALU.mult))
                    d(V.tensor_tensor(heads(A), heads(A), ph(1), ALU.mult))
                    d(V.tensor_tensor(heads(GT), heads(GT), bc(upper[:r, :r], 1, DN_H), ALU.mult))
                    d(V.tensor_tensor(heads(GT), heads(GT), ph(2), ALU.mult))
                    d(V.tensor_tensor(heads(A), heads(A), bc(beta[:r, c, :], 2, r), ALU.mult))
                    d(V.tensor_tensor(heads(X), heads(A), bc(const("level1")[:r, :r], 1, DN_H), ALU.mult))
                    d(V.scalar_tensor_tensor(heads(X), heads(X), -1.0, bc(ident[:r, :r], 1, DN_H), ALU.mult, ALU.add))
                    dve.wait_ge(s_a, 3)
                    d(V.tensor_tensor(heads(XT), heads(AT), bc(const("level1T")[:r, :r], 1, DN_H), ALU.mult))
                    d(V.scalar_tensor_tensor(heads(XT), heads(XT), -1.0, bc(ident[:r, :r], 1, DN_H), ALU.mult, ALU.add))
                    for n, lv in enumerate(levels):
                        dve.wait_ge(s_pe, 3 + 2 * n)
                        d(V.tensor_tensor(heads(Y), ph(1), bc(const(f"level{lv}")[:r, :r], 1, DN_H), ALU.mult))
                        dve.wait_ge(s_pe, 4 + 2 * n)
                        d(V.tensor_tensor(heads(X), heads(X), ph(2), ALU.subtract))
                        d(V.tensor_tensor(heads(XT), heads(XT), ph(3), ALU.subtract))
                    dve_tail(dve, d, s_pe, s_d, s_a, s_g, n_lv)

        rows_o = tok[0]

        GH = DN_H // 2
        LV = LEVELS[1:]
        NL = len(LV)
        PS = 5 + 2 * NL
        W_T, E_ROWS, LAST = PS - 2, PS - 1, PS
        DV_A, DV_X, DV_N = 6, 10, 14 + 3 * NL
        ACT_N, POOL_N = 5, 3
        LAG = 1
        d_pe, d_d, d_a, d_g = ([sem(f"delta_{m}{g}") for g in range(2)] for m in ("products", "dve", "act", "pool"))
        s_zero = sem("state_zero")

        def group(t, g, rows=P):
            return t[:rows, GH * g:GH * (g + 1), :]

        def bank(k, g):
            return pp[k][:, 512 * g:512 * g + GH * P].rearrange("p (h t) -> p h t", h=GH)

        def staggered(do):
            for t in range(NC_P * PS + LAG):
                for g in range(2):
                    n = t - LAG * g
                    if 0 <= n < NC_P * PS:
                        do(g, n // PS, n % PS + 1)

        with nc.Block() as block:
            @block.tensor
            def _(pe):
                def step(g, c, k):
                    tk = slice(offset(c), offset(c) + P)
                    hs = [(h, GH * g + h) for h in range(GH)]
                    at_d, at_a, at_g = DV_N * c, ACT_N * c, POOL_N * c
                    if k == 1:
                        wait_after(pe, d_d[g], at_d)
                        for i, h in hs:
                            TE.matmul(bank(0, g)[:, i, :], bc(g_[:, c, h], 1, P), const("upper"), start=True, stop=True)
                        for i, h in hs:
                            TE.matmul(bank(1, g)[:, i, :], qkT[:, DN_H + h, tk], qkT[:, DN_H + h, tk], start=True, stop=True)
                        for i, h in hs:
                            ins = TE.matmul(bank(2, g)[:, i, :], qkT[:, DN_H + h, tk], qkT[:, h, tk], start=True, stop=True)
                    elif k == 2:
                        pe.wait_ge(d_d[g], at_d + DV_A)
                        for i, h in hs:
                            ins = TE.transpose(bank(0, g)[:, i, :], A[:, h, :], ident)
                    elif k < W_T and k % 2 == 1:
                        pe.wait_ge(d_d[g], at_d + DV_X + 3 * ((k - 3) // 2))
                        for i, h in hs:
                            ins = TE.matmul(bank(1, g)[:, i, :], AT[:, h, :], X[:, h, :], start=True, stop=True)
                    elif k < W_T:
                        pe.wait_ge(d_d[g], at_d + DV_X + 3 * ((k - 3) // 2) + 1)
                        for i, h in hs:
                            TE.matmul(bank(2, g)[:, i, :], XT[:, h, :], Y[:, h, :], start=True, stop=True)
                        for i, h in hs:
                            ins = TE.matmul(bank(3, g)[:, i, :], Y[:, h, :], XT[:, h, :], start=True, stop=True)
                    elif k == W_T:
                        pe.wait_ge(d_d[g], at_d + DV_X + 3 * NL)
                        pe.wait_ge(d_g[g], at_g + 1)
                        for i, h in hs:
                            ins = TE.matmul(bank(1, g)[:, i, :], Kb[:, h, :], XT[:, h, :], start=True, stop=True)
                    elif k == E_ROWS:
                        pe.wait_ge(d_g[g], at_g + 3)
                        for i, h in hs:
                            TE.matmul(bank(2, g)[:, i, :], XT[:, h, :], Vb[:, h, :], start=True, stop=False)
                            if i == 0:
                                pe.wait_ge(d_a[g], at_a + 4)
                                if c == 0:
                                    pe.wait_ge(s_zero, 1)
                            TE.matmul(bank(2, g)[:, i, :], wT[:, h, :], state[:, h, :], start=False, stop=True)
                        for i, h in hs:
                            ins = TE.matmul(bank(0, g)[:, i, :], qkT[:, h, tk], state[:, h, :], start=True, stop=True)
                    else:
                        pe.wait_ge(d_a[g], at_a + 5)
                        for i, h in hs:
                            TE.matmul(bank(3, g)[:, i, :], GT[:, h, :], e[:, h, :], start=True, stop=True)
                        for i, h in hs:
                            ins = TE.matmul(bank(1, g)[:, i, :], Kd[:, h, :], e[:, h, :], start=True, stop=True)
                    ins.then_inc(d_pe[g], 1)

                staggered(step)

            @block.gpsimd
            def _(pool):
                for c in range(NC_P):
                    for g in range(2):
                        for n, (dst, src, f) in enumerate(((Kb, 1, beG), (Vb, 2, beta), (Kd, 1, ekd))):
                            if c >= 1:
                                pool.wait_ge(d_pe[g], PS * (c - 1) + W_T + n)
                            G.tensor_tensor(group(dst, g), tok[src][:, c, GH * g * P:GH * (g + 1) * P].rearrange("p (h d) -> p h d", h=GH),
                                            bc(f[:, c, GH * g:GH * (g + 1)], 2, P), ALU.mult).then_inc(d_g[g], 1)

            @block.scalar
            def _(act):
                chain = [Chain(act, s) for s in d_a]

                def step(g, c, k):
                    a = chain[g]
                    if k == 1:
                        act.wait_ge(d_d[g], DV_N * c + 3)
                        act.activation(group(A, g), group(A, g), ACT.Exp, scale=-1.0).then_inc(d_a[g], 1)
                        act.activation(group(GT, g), group(GT, g), ACT.Exp).then_inc(d_a[g], 1)
                    elif k == 2:
                        act.wait_ge(d_pe[g], PS * c + 2)
                        act.activation(group(AT, g), bank(0, g), ACT.Copy).then_inc(d_a[g], 1)
                    elif k == W_T:
                        act.wait_ge(d_pe[g], PS * c + W_T)
                        act.activation(group(wT, g), bank(1, g), ACT.Copy, scale=-1.0).then_inc(d_a[g], 1)
                    elif k == E_ROWS:
                        act.wait_ge(d_pe[g], PS * c + E_ROWS)
                        act.activation(group(e, g), bank(2, g), ACT.Copy).then_inc(d_a[g], 1)

                staggered(step)

            @block.vector
            def _(dve):
                chain = [Chain(dve, s) for s in d_d]
                masks = {m: bc(const(m), 1, GH) for m in ["lower_big", "upper_neg", "level1", "level1T", "ident"] + [f"level{lv}" for lv in LV]}

                def step(g, c, k):
                    d = chain[g]
                    hg = slice(GH * g, GH * (g + 1))
                    A_, GT_, AT_, X_, XT_, Y_ = (group(t, g) for t in (A, GT, AT, X, XT, Y))
                    orow = rows_o[:, c, GH * g * P:GH * (g + 1) * P].rearrange("p (h d) -> p h d", h=GH)
                    st = group(state, g)
                    if k != W_T:
                        dve.wait_ge(d_pe[g], PS * c + k)
                    if k == 1:
                        d(V.tensor_tensor(Y_, bank(0, g), bc(G_[:, c, hg], 2, P), ALU.subtract))
                        d(V.scalar_tensor_tensor(A_, Y_, 0.0, masks["lower_big"], ALU.max, ALU.add))
                        d(V.scalar_tensor_tensor(GT_, Y_, 0.0, masks["upper_neg"], ALU.min, ALU.add))
                        dve.wait_ge(d_a[g], ACT_N * c + 1)
                        d(V.tensor_tensor(A_, A_, bank(1, g), ALU.mult))
                        dve.wait_ge(d_a[g], ACT_N * c + 2)
                        V.tensor_tensor(GT_, GT_, bank(2, g), ALU.mult).then_inc(d.sem, 1)
                        d.n += 1
                        d(V.tensor_tensor(A_, A_, bc(beta[:, c, hg], 2, P), ALU.mult))
                    elif k == 2:
                        d(V.tensor_tensor(X_, A_, masks["level1"], ALU.mult))
                        d(V.scalar_tensor_tensor(X_, X_, -1.0, masks["ident"], ALU.mult, ALU.add))
                        dve.wait_ge(d_a[g], ACT_N * c + 3)
                        d(V.tensor_tensor(XT_, AT_, masks["level1T"], ALU.mult))
                        d(V.scalar_tensor_tensor(XT_, XT_, -1.0, masks["ident"], ALU.mult, ALU.add))
                    elif k < W_T and k % 2 == 1:
                        d(V.tensor_tensor(Y_, bank(1, g), masks[f"level{LV[(k - 3) // 2]}"], ALU.mult))
                    elif k < W_T:
                        V.tensor_tensor(X_, X_, bank(2, g), ALU.subtract).then_inc(d.sem, 1)
                        d.n += 1
                        d(V.tensor_tensor(XT_, XT_, bank(3, g), ALU.subtract))
                    elif k == E_ROWS:
                        d(V.tensor_tensor(st, st, bc(dec[:, c, hg], 2, P), ALU.mult))
                        d(V.tensor_tensor(orow, bank(0, g), bc(eG[:, c, hg], 2, P), ALU.mult))
                    elif k == LAST:
                        d(V.tensor_tensor(orow, orow, bank(3, g), ALU.add))
                        d(V.tensor_tensor(st, st, bank(1, g), ALU.add))

                V.memset(state[:], 0.0).then_inc(s_zero, 1)
                dve.wait_ge(s_zero, 1)
                staggered(step)
        dump("o_rows", rows_o[:])
        s_state = sem("state_stored")
        sS = uT_flat[:, 3 * 768:3 * 768 + 2 * DB * P].rearrange("p (k b v) -> p k b v", k=2, b=DB)
        wm = sb("w_masked", [P, 2, DB, NS], where=DL)
        qm = sb("q_masked", [P, 2, DB, NS], where=DL)
        km = toks[0:NS, 1, 0:2, :].rearrange("t c n -> t (c n)")[:, 0:DB * P].rearrange("t (b n) -> t b n", b=DB)
        s_sin, s_sout = [sem(f"states_in{k}") for k in range(2)], [sem(f"states_out{k}") for k in range(2)]
        NH_IN = DN_H

        def s_sync(sp, s_pe, s_d, s_a, s_g, n_lv):
            sp.dma_start(O["state_delta_prompt"][0, 0].rearrange("h k v -> k h v"), state[:]).then_inc(s_state, 16)
            B = 12 + 3 * n_lv
            for h in range(DN_H):
                if h >= 2:
                    sp.wait_ge(s_sout[h % 2], 16 * (h // 2))
                sp.dma_start(sS[:, h % 2], I["state_delta"][0, :, h].rearrange("b k v -> k b v")).then_inc(s_sin[h % 2], 16)
                if h >= 1:
                    store_s(sp, h - 1, s_d, B)
            store_s(sp, DN_H - 1, s_d, B)
            for k in range(2):
                sp.wait_ge(s_sout[k], 16 * DN_H // 2)
            sp.wait_ge(s_state, 16)

        def store_s(sp, h, s_d, B):
            sp.wait_ge(s_d, B + 7 * (h + 1))
            sp.dma_start(O["state_delta_sample"][0, :, h].rearrange("b k v -> k b v"), sS[:, h % 2]).then_inc(s_sout[h % 2], 16)

        def s_pe_tail(pe, s_pe, s_d, s_a, s_g, n_lv):
            B, Q = 12 + 3 * n_lv, 3 + 2 * n_lv
            pe.wait_ge(s_g, 3)
            for h in range(DN_H):
                k = h % 2
                pe.wait_ge(s_sin[k], 16 * (h // 2 + 1))
                pe.wait_ge(s_d, B + 7 * h + 2)
                TE.matmul(pp[2][0:NS, 0:P], XT[0:NS, h, 0:NS], Vb[0:NS, h, :], start=True, stop=False)
                for b in range(DB):
                    TE.matmul(pp[2][0:NS, 0:P], wm[:, k, b, :], sS[:, k, b, :], start=False, stop=(b == DB - 1))
                for b in range(DB):
                    ins = TE.matmul(pp[0][0:NS, 0:P], qm[:, k, b, :], sS[:, k, b, :], start=(b == 0), stop=(b == DB - 1))
                ins.then_inc(s_pe, 1)
                pe.wait_ge(s_a, 4 + h)
                pe.wait_ge(s_d, B + 7 * h + 3)
                TE.matmul(pp[3][0:NS, 0:P], GT[0:NS, h, 0:NS], e[0:NS, h, :], start=True, stop=True)
                for b in range(DB):
                    ins = TE.matmul(pp[1 if h % 2 == 0 else 1][:, b * P:(b + 1) * P], km[:, b, :], e[0:NS, h, :], start=True, stop=True)
                ins.then_inc(s_pe, 1)

        def s_act_tail(act, a, s_pe, s_d, s_a, s_g, n_lv):
            Q = 3 + 2 * n_lv
            for h in range(DN_H):
                act.wait_ge(s_pe, Q + 2 * h + 1)
                a(S.activation(e[0:NS, h, :], pp[2][0:NS, 0:P], ACT.Copy))

        wts = sb("w_samples", [P, DN_H, NS], where=DL)

        def s_dve_tail(dve, d, s_pe, s_d, s_a, s_g, n_lv):
            Q = 3 + 2 * n_lv
            c = NC_P
            rowm = const("row_of").rearrange("p (b t) -> p b t", b=DB)
            dve.wait_ge(s_pe, Q)
            V.tensor_scalar(wts[:], pp[1][:, 0:DN_H * NS].rearrange("p (h t) -> p h t", h=DN_H), -1.0, None, ALU.mult).then_inc(s_w, 1)
            dve.wait_ge(s_w, 1)
            dve.wait_ge(s_g, 3)
            for h in range(DN_H):
                k = h % 2
                d(V.tensor_tensor(wm[:, k], bc(wts[:, h, :], 1, DB), rowm, ALU.mult))
                d(V.tensor_tensor(qm[:, k], bc(qkT[:, h, SEQ:T], 1, DB), rowm, ALU.mult))
                d(V.tensor_tensor(km, bc(Kd[0:NS, h, :], 1, DB), bc(const("col_of")[0:NS, :], 2, P), ALU.mult))
                dve.wait_ge(s_pe, Q + 2 * h + 1)
                d(V.tensor_tensor(sS[:, k], sS[:, k], bc(dS[:, :, h], 2, P), ALU.mult))
                orow = rows_o[0:NS, c, h * P:(h + 1) * P]
                d(V.tensor_scalar(orow, pp[0][0:NS, 0:P], eG[0:NS, c, h:h + 1], None, ALU.mult))
                dve.wait_ge(s_pe, Q + 2 * h + 2)
                d(V.tensor_tensor(orow, orow, pp[3][0:NS, 0:P], ALU.add))
                d(V.tensor_tensor(sS[:, k], sS[:, k], pp[1][:].rearrange("p (b v) -> p b v", b=DB), ALU.add))

        s_w = sem("w_samples_kept")
        delta_solve("deltas", NC_P, NS, s_pe_tail, s_dve_tail, s_act_tail, s_sync)
        DL.close()
        dump("o_all", rows_o[:])

        mergedT = uT
        with nc.Block() as block:
            s_a, s_d, s_g, s_t, s_k = (sem(f"gate_{m}") for m in ("act", "dve", "pool", "turned", "kept"))
            gs = sb("o_squares", [P, NCH * DN_H], where=L0)
            oh = rows_o[:].rearrange("p c (h d) -> p (c h) d", d=P)

            @block.scalar
            def _(act):
                act.activation(x_flat[:, 0:768 * NCH], rows_o[:].rearrange("p c n -> p (c n)"), ACT.Square).then_inc(s_a, 1)
                act.wait_ge(s_d, 2)
                act.activation(gs[:], gs[:], ACT.Sqrt).then_inc(s_a, 1)
                for n in range(DN_H):
                    act.wait_ge(s_t, n + 1)
                    act.activation(mergedT[:, n, 0:SEQ], pp[n % 2][:, 0:SEQ], ACT.Copy)
                    act.activation(mergedT[:, n, SEQ:T], pp[n % 2][:, 512:512 + NS], ACT.Copy).then_inc(s_k, 1)

            @block.gpsimd
            def _(pool):
                zv = zs[:].rearrange("p c (h d) -> p (c h) d", d=P)
                G.tensor_tensor(zv, zv, bc(g_on[:], 1, NCH * DN_H), ALU.mult).then_inc(s_g, 1)

            @block.vector
            def _(dve):
                d = Chain(dve, s_d)
                dve.wait_ge(s_a, 1)
                d(V.tensor_reduce(gs[:], x_flat[:, 0:768 * NCH].rearrange("p (n d) -> p n d", d=P), AX, ALU.add))
                d(V.tensor_scalar(gs[:], gs[:], 1.0 / P, EPS, ALU.mult, ALU.add))
                dve.wait_ge(s_a, 2)
                d(V.reciprocal(gs[:], gs[:]))
                d(V.tensor_tensor(oh, oh, bc(gs[:], 2, P), ALU.mult))
                dve.wait_ge(s_g, 1)
                d(V.tensor_tensor(rows_o[:], rows_o[:], zs[:], ALU.mult))

            @block.tensor
            def _(pe):
                pe.wait_ge(s_d, 5)
                for n in range(DN_H):
                    if n >= 2:
                        pe.wait_ge(s_k, n - 1)
                    for c in range(NC_P):
                        TE.transpose(pp[n % 2][:, c * P:(c + 1) * P], rows_o[:, c, n * P:(n + 1) * P], ident)
                    TE.transpose(pp[n % 2][:, 512:512 + NS], rows_o[0:NS, NC_P, n * P:(n + 1) * P], ident[0:NS, 0:NS]).then_inc(s_t, 1)

        def memory_attention(l, qmT, mkc, mvc, KT, pr, prT, Zq, stat):
            s_in, s_s, s_m, s_x, s_p, s_t, s_e, s_o, s_k, s_kt, s_kk, s_z, s_d = (
                sem(f"mem{l}_{m}") for m in ("cache_in", "scores", "max", "exp", "probs", "turned", "turned_kept", "out", "merged",
                                             "keys_turned", "keys_kept", "queries", "dve"))
            scale = MHD ** -0.5
            with nc.Block() as block:
                @block.sync
                def _(sp):
                    for dst, src in ((mkc, I["cache_mem_k"]), (mvc, I["cache_mem_v"])):
                        for m in range(2):
                            sp.dma_start(dst[:, :, m, :], src[l].rearrange("b m h d -> m b (h d)")[m * P:(m + 1) * P]).then_inc(s_in, 16)

                @block.tensor
                def _(pe):
                    def scores(c):
                        if c == NC_P:
                            pe.wait_ge(s_kk, 4)
                            pe.wait_ge(s_z, 1)
                        if c >= 2:
                            pe.wait_ge(s_x, c - 1)
                        if c < NC_P:
                            for h in range(MH):
                                j, a = divmod(h, 2)
                                ins = TE.matmul(pp[c % 2][:, h * MEM:(h + 1) * MEM], qmT[64 * j:64 * j + 64, a, c * P:(c + 1) * P],
                                                mem_kT[64 * j:64 * j + 64, l, a, :], start=True, stop=True)
                        else:
                            for b in range(DB):
                                for a in range(2):
                                    ins = TE.matmul(pp[c % 2][:, 0:MEM], Zq[:, a, b * P:(b + 1) * P], KT[:, a, b, :],
                                                    start=(b == 0 and a == 0), stop=(b == DB - 1 and a == 1))
                        ins.then_inc(s_s, 1)

                    def turn(c):
                        pe.wait_ge(s_p, c + 1)
                        if c >= 1:
                            pe.wait_ge(s_e, c)
                        if c == NC_P - 1:
                            pe.wait_ge(s_kk, 4)
                        for h in range(MH if c < NC_P else 1):
                            for m in range(2):
                                ins = TE.transpose(pp[2][:, (2 * h + m) * P:(2 * h + m + 1) * P], pr[c % 2][:, h * MEM + m * P:h * MEM + (m + 1) * P], ident)
                        ins.then_inc(s_t, 1)

                    def out(c):
                        pe.wait_ge(s_e, c + 1)
                        if c >= 1:
                            pe.wait_ge(s_k, c)
                        if c < NC_P:
                            for h in range(MH):
                                for m in range(2):
                                    ins = TE.matmul(pp[3][:, h * P:(h + 1) * P], mem_v[:, l, m, (h % 2) * P:(h % 2 + 1) * P],
                                                    prT[:, 2 * h + m, :], start=(m == 0), stop=(m == 1))
                        else:
                            for a in range(2):
                                for b in range(DB):
                                    for m in range(2):
                                        o = (a * DB + b) * MH * DS
                                        ins = TE.matmul(pp[3][:, o:o + MH * DS], mvc[:, b, m, a * P:(a + 1) * P],
                                                        prT[:, m, b * MH * DS:(b + 1) * MH * DS], start=(m == 0), stop=(m == 1))
                        ins.then_inc(s_o, 1)

                    def keys():
                        pe.wait_ge(s_in, 64)
                        pe.wait_ge(s_e, 3)
                        pe.wait_ge(s_k, 3)
                        for n in range(4):
                            if n >= 2:
                                pe.wait_ge(s_kk, n - 1)
                            for b in range(2):
                                for a in range(2):
                                    for m in range(2):
                                        o = (a * 2 + b) * MEM + m * P
                                        ins = TE.transpose(pp[2 + n % 2][:, o:o + P], mkc[:, 2 * n + b, m, a * P:(a + 1) * P], ident)
                            ins.then_inc(s_kt, 1)

                    scores(0)
                    scores(1)
                    for c in range(NCH):
                        turn(c)
                        if c + 2 < NC_P:
                            scores(c + 2)
                        out(c)
                        if c + 2 == NC_P:
                            keys()
                            scores(c + 2)

                @block.scalar
                def _(act):
                    def exp(c):
                        act.wait_ge(s_m, c + 1)
                        act.wait_ge(s_s, c + 1)
                        if c >= 2:
                            act.wait_ge(s_t, c - 1)
                        nh = MH if c < NC_P else 1
                        for h in range(nh):
                            ins = act.activation(pr[c % 2][:, h * MEM:(h + 1) * MEM], pp[c % 2][:, h * MEM:(h + 1) * MEM], ACT.Exp,
                                                 bias=stat[:, 1, c, h:h + 1], scale=scale, accum_out=stat[:, 2, c, h:h + 1])
                        ins.then_inc(s_x, 1)

                    exp(0)
                    for c in range(NCH):
                        nh = MH if c < NC_P else 1
                        if c + 1 < NC_P:
                            exp(c + 1)
                        act.wait_ge(s_t, c + 1)
                        if c >= 1:
                            act.wait_ge(s_o, c)
                        act.activation(prT[:, 0:2 * nh, :], pp[2][:, 0:2 * nh * P].rearrange("p (k t) -> p k t", t=P), ACT.Copy).then_inc(s_e, 1)
                        if c + 2 == NC_P:
                            for n in range(4):
                                act.wait_ge(s_kt, n + 1)
                                act.activation(KT[:, :, 2 * n:2 * n + 2, :], pp[2 + n % 2][:].rearrange("p (a b m) -> p a b m", a=2, b=2), ACT.Copy).then_inc(s_kk, 1)
                        if c + 1 == NC_P:
                            exp(c + 1)

                @block.vector
                def _(dve):
                    d = Chain(dve, s_d)

                    def maxima(c):
                        nh = MH if c < NC_P else 1
                        dve.wait_ge(s_s, c + 1)
                        d(V.tensor_reduce(stat[:, 0, c, 0:nh], pp[c % 2][:, 0:nh * MEM].rearrange("p (h m) -> p h m", h=nh), AX, ALU.max))
                        d(V.tensor_scalar(stat[:, 1, c, 0:nh], stat[:, 0, c, 0:nh], -scale, None, ALU.mult))
                        dve.sem_inc(s_m, 1)

                    def merged(c):
                        dve.wait_ge(s_o, c + 1)
                        for j in range(2):
                            k = slice(64 * j, 64 * j + 64)
                            if c < NC_P:
                                ins = V.tensor_copy(mergedT[k, 6:8, c * P:(c + 1) * P],
                                                    pp[3][k, 0:512].rearrange("p (j a t) -> p j a t", a=2, j=2)[:, j])
                                if j == 1:
                                    ins.then_inc(s_k, 1)
                            else:
                                for a in range(2):
                                    src = pp[3][k, a * P:(a + 1) * P].rearrange("p (b h t) -> p b h t", b=DB, h=MH)[:, :, 2 * a + j, :]
                                    V.tensor_copy(mergedT[k, 6 + a, SEQ:T].rearrange("p (b t) -> p b t", b=DB), src)

                    d(V.memset(Zq, 0.0))
                    for a in range(2):
                        for j in range(2):
                            k, o = slice(64 * j, 64 * j + 64), (2 * a + j) * DS
                            ins = V.tensor_copy(Zq[k, a, :].rearrange("p (b w) -> p b w", b=DB)[:, :, o:o + DS],
                                                qmT[k, a, SEQ:T].rearrange("p (b t) -> p b t", b=DB))
                    ins.then_inc(s_z, 1)
                    maxima(0)
                    maxima(1)
                    for c in range(NCH):
                        nh = MH if c < NC_P else 1
                        dve.wait_ge(s_x, c + 1)
                        d(V.reciprocal(stat[:, 3, c, 0:nh], stat[:, 2, c, 0:nh]))
                        v = pr[c % 2][:, 0:nh * MEM].rearrange("p (h m) -> p h m", h=nh)
                        V.tensor_tensor(v, v, bc(stat[:, 3, c, 0:nh], 2, MEM), ALU.mult).then_inc(s_p, 1)
                        if c >= 1:
                            merged(c - 1)
                        if c + 2 < NC_P:
                            maxima(c + 2)
                        if c + 1 == NC_P:
                            maxima(NC_P)
                    merged(NC_P)

        with ExitStack() as cx:
            stat = sb("mem_stat", [P, 4, NCH, MH], where=cx)
            x_b = x_flat[:, 0:4096].rearrange("p (b m n) -> p b m n", b=DB, m=2)
            q_b = qkT[:].rearrange("p n t -> p (n t)")[:, 0:4096].rearrange("p (b m n) -> p b m n", b=DB, m=2)
            f = toks[:].rearrange("p g c n -> p (g c n)")
            KT = f[:, 0:4096].rearrange("p (a b m) -> p a b m", a=2, b=DB)
            Zq = zs[:].rearrange("p c n -> p (c n)")[:, 0:2304].rearrange("p (a n) -> p a n", a=2)
            memory_attention(0, qmT, x_b, q_b, KT, [f[:, 4096:5120], f[:, 5120:6144]], f[:, 6144:7168].rearrange("p (k t) -> p k t", t=P), Zq, stat)

        def project_out(l, halves):
            s_x, s_m, s_v = [sem(f"out{l}_{m}") for m in ("x_landed", "product", "added")]
            with nc.Block() as block:
                @block.sync
                def _(sp):
                    if l == 0:
                        sp.dma_start(x[:, 0:NC_P, :], I["x_prompt"][0].rearrange("(c p) d -> p c d", p=P)).then_inc(s_x, 16)
                        sp.dma_start(x[0:NS, NC_P, :], I["x_sample"].rearrange("b s d -> (b s) d")).then_inc(s_x, 16)

                @block.tensor
                def _(pe):
                    n = 0
                    for k, (w, name) in enumerate(halves):
                        arrived(pe, name)
                        for c, r in enumerate(ROWS):
                            if n >= 8:
                                pe.wait_ge(s_v, n - 7)
                            for j in range(DJ):
                                ins = TE.matmul(pp[(n % 8) // 2][:r, (n % 2) * 512:(n % 2) * 512 + 512], mergedT[:, j, offset(c):offset(c) + r], w[:, j, :],
                                                start=(j == 0), stop=(j == DJ - 1))
                            ins.then_inc(s_m, 1)
                            n += 1

                @block.vector
                def _(dve):
                    if l == 0:
                        dve.wait_ge(s_x, 32)
                    for n in range(2 * NCH):
                        k, c = divmod(n, NCH)
                        r = ROWS[c]
                        dve.wait_ge(s_m, n + 1)
                        V.tensor_tensor(x[:r, c, k * 512:(k + 1) * 512], x[:r, c, k * 512:(k + 1) * 512],
                                        pp[(n % 8) // 2][:r, (n % 2) * 512:(n % 2) * 512 + 512], ALU.add).then_inc(s_v, 1)

        project_out(0, [(slot3(1, 512), "out0"), (slot3(0, 512), "out1")])
        L0.close()


        def experts(l):
            ME = ExitStack()
            with ME:
                def mb(name, shape, dt=F32):
                    return sb(f"{name}{l}", shape, dt, where=ME)

                slots = [ring[0], ring[1], mb("ring2_", [P, 6144]), mb("ring3_", [P, 6144])]
                xn = mb("scaled_rows", [P, NCH, D])
                lg = mb("logits", [P, NCH, NG + NE])
                gate = mb("gates", [P, 2, NCH])
                idx = mb("row_index", [P, NCH, 4], I32)
                base_i = mb("base_int", [P, NE], I32)
                over_i = mb("over_int", [P, 2], I32)
                n_i = mb("n_over_int", [P, 1], I32)
                gw = I["w_exp_gate"][l].rearrange("e (p j) n -> e p (j n)", p=P)
                uw = I["w_exp_up"][l].rearrange("e (p j) n -> e p (j n)", p=P)
                dw = I["w_exp_down"][l].rearrange("e (j p) n -> e p j n", p=P)

                class Lane:

                    def __init__(self, tag, deep, two):
                        self.deep, self.two = deep, two
                        self.w = [sem(f"{tag}_weights{k}") for k in range(deep)]
                        self.x = [sem(f"{tag}_rows{k}") for k in range(deep)]
                        self.st = [sem(f"{tag}_stored{k}") for k in range(two)]
                        self.turned, self.gu, self.sg, self.h, self.ht, self.hT, self.xT, self.dn, self.y, self.order = (
                            sem(f"{tag}_{m}") for m in ("turned", "gate_up", "silu", "hidden", "hidden_turned", "hidden_T", "tile_T", "down", "out", "order"))

                main = Lane(f"moe{l}", 4, 2)
                over = Lane(f"over{l}", 1, 1)

                def fetch_weights(sp, s, k, expert):
                    sp.dma_start(slots[k][:, 0:2048], gw[expert]).then_inc(s.w[k], 16)
                    sp.dma_start(slots[k][:, 2048:4096], uw[expert]).then_inc(s.w[k], 16)
                    sp.dma_start(slots[k][:, 4096:6144].rearrange("p (j n) -> p j n", j=2), dw[expert]).then_inc(s.w[k], 16)

                def first_weights(sp):
                    for k in range(main.deep):
                        fetch_weights(sp, main, k, slice(k, k + 1))

                def chunk_logits(c):
                    r = ROWS[c]
                    for j in range(DJ):
                        ins = TE.matmul(pp[2][:r, 64 * c:64 * c + NG + NE], uT[:, j, offset(c):offset(c) + r], w_rt[:, l, j, :],
                                        start=(j == 0), stop=(j == DJ - 1))
                    ins.then_inc(s_lg, 1)

                s_lg = sem(f"route{l}_logits")
                norm_transposed(f"normf{l}", x, ROWS, [(G_FFN + l, uT)], kept_rows=xn, sync_extra=first_weights, on_chunk=chunk_logits)
                RT = ExitStack()
                with RT:
                    def rb(name, shape, dt=F32):
                        return sb(f"{name}{l}", shape, dt, where=RT)

                    w1, w2, oh1, oh2, em = (rb(n, [P, NCH, NE]) for n in ("rw1", "rw2", "first", "second", "masked"))
                    rank = rb("rank", [P, NCH, NE])
                    sc = rb("rscalars", [P, 12, NCH])
                    ge = rb("gexp", [P, NCH, NG])
                    tb = rb("tables", [P, 9, NE])
                    ov = rb("over_f", [P, 2])
                    before = rb("before", [P, NCH + 1, NE])
                    real = rb("real_rows", [P, 1])
                    s_d, s_a, s_r, s_z, s_sc = (sem(f"route{l}_{m}") for m in ("dve", "act", "ranks", "table", "scattered"))
                    steps = {}
                    with nc.Block() as block:
                        @block.vector
                        def _(dve):
                            d = Chain(dve, s_d)
                            gb4 = small[:, 12 + 36 * l:48 + 36 * l]
                            d(V.memset(before[:, 0, :], 0.0))
                            d(V.tensor_scalar(real[:], const("rows"), float(NS), None, ALU.is_lt))
                            d(V.memset(lg[:], 0.0))
                            dve.wait_ge(s_lg, NCH)
                            d(V.tensor_tensor(lg[:, 0:NC_P, :], pp[2][:, 0:64 * NC_P].rearrange("p (c n) -> p c n", n=64)[:, :, 0:NG + NE],
                                              bc(gb4, 1, NC_P), ALU.add))
                            d(V.tensor_tensor(lg[0:NS, NC_P, :], pp[2][0:NS, 64 * NC_P:64 * NC_P + NG + NE], gb4[0:NS, :], ALU.add))
                            gl, el = lg[:, :, 0:NG], lg[:, :, NG:]
                            gmax, gval, v1, v2, m1, t, r1, a1, o1, lt = (sc[:, k, :] for k in range(10))
                            d(V.tensor_reduce(gmax, gl, AX, ALU.max))
                            d(V.tensor_tensor(ge[:], gl, bc(gmax, 2, NG), ALU.subtract))
                            steps["group"] = d.n
                            dve.wait_ge(s_a, 1)
                            d(V.tensor_reduce(gval, ge[:], AX, ALU.add))
                            d(V.reciprocal(gval, gval))
                            first = const("first_of_4")
                            d(V.tensor_tensor(ge[:], gl, bc(gmax, 2, NG), ALU.is_equal))
                            d(V.tensor_tensor(ge[:], ge[:], bc(first, 1, NCH), ALU.mult))
                            d(V.tensor_reduce(t, ge[:], AX, ALU.max))
                            d(V.tensor_tensor(ge[:], ge[:], bc(t, 2, NG), ALU.is_equal))
                            g8 = ge[:].rearrange("p c g -> p (c g)")
                            fl = lambda a: a.rearrange("p c (g e) -> p (c g) e", e=EPG)
                            w1g = w1[:].rearrange("p c (g e) -> p (c g) e", e=EPG)
                            d(V.tensor_copy(w1g, bc(g8, 2, EPG)))
                            d(V.tensor_tensor(em[:], el, w1[:], ALU.mult))
                            d(V.tensor_scalar(w1[:], w1[:], -1.0, BIG, ALU.add, ALU.mult))
                            d(V.tensor_tensor(em[:], em[:], w1[:], ALU.add))
                            for k, (v, oh) in enumerate(((v1, oh1), (v2, oh2))):
                                d(V.tensor_reduce(v, em[:], AX, ALU.max))
                                d(V.tensor_tensor(oh[:], em[:], bc(v, 2, NE), ALU.is_equal))
                                d(V.tensor_tensor(oh[:], oh[:], bc(const("first_of_32"), 1, NCH), ALU.mult))
                                d(V.tensor_reduce(m1, oh[:], AX, ALU.max))
                                d(V.tensor_tensor(oh[:], oh[:], bc(m1, 2, NE), ALU.is_equal))
                                if k == 0:
                                    d(V.scalar_tensor_tensor(em[:], oh[:], -BIG, em[:], ALU.mult, ALU.add))
                            d(V.tensor_tensor(w1[:], oh1[:], oh2[:], ALU.add))
                            d(V.tensor_scalar(w1[:, NC_P, :], w1[:, NC_P, :], real[:], None, ALU.mult))
                            for c in range(NCH):
                                d(V.tensor_tensor(before[:, c + 1, :], before[:, c, :], w1[:, c, :], ALU.add))
                            d(V.tensor_tensor(t, v2, v1, ALU.subtract))
                            steps["chosen"] = d.n
                            dve.wait_ge(s_a, 2)
                            g1, g2 = gate[:, 0, :], gate[:, 1, :]
                            d(V.tensor_scalar(g1, t, 1.0, None, ALU.add))
                            d(V.reciprocal(g1, g1))
                            d(V.tensor_tensor(g1, g1, gval, ALU.mult))
                            d(V.tensor_tensor(g2, g1, t, ALU.mult))
                            dve.wait_ge(s_r, 1)
                            d(V.tensor_copy(rank[:], pp[0][:, 0:NE * NCH].rearrange("p (c n) -> p c n", n=NE)))
                            cnt, base, no, oin, ob, A, Bt, sel, tmp = (tb[:, k, :] for k in range(9))
                            d(V.tensor_copy(cnt, pp[1][:, 0:NE]))
                            one = ones[:, 0:NE]
                            d(V.tensor_tensor_scan(base, one, cnt, 0.0, ALU.mult, ALU.add))
                            d(V.tensor_tensor(base, base, cnt, ALU.subtract))
                            d(V.scalar_tensor_tensor(em[:], rank[:], -1.0, bc(base, 1, NCH), ALU.add, ALU.add))
                            for k, oh in ((0, oh1), (1, oh2)):
                                d(V.tensor_tensor(w2[:], oh[:], em[:], ALU.mult))
                                d(V.tensor_reduce(t, w2[:], AX, ALU.add))
                                d(V.tensor_copy(idx[:, :, k], t))
                                steps[f"to{k}"] = d.n
                            d(V.tensor_scalar(no, cnt, float(SLOTS), None, ALU.is_gt))
                            for k in range(2, -(-T // SLOTS)):
                                d(V.scalar_tensor_tensor(no, cnt, float(SLOTS * k), no, ALU.is_gt, ALU.add))
                            d(V.tensor_tensor_scan(oin, one, no, 0.0, ALU.mult, ALU.add))
                            d(V.tensor_tensor(ob, oin, no, ALU.subtract))
                            d(V.tensor_copy(base_i[:], base))
                            d(V.tensor_copy(n_i[:], oin[:, NE - 1:NE]))
                            rows = const("rows")
                            d(V.tensor_scalar(sel, ob, rows, None, ALU.is_le))
                            d(V.tensor_scalar(tmp, oin, rows, None, ALU.is_gt))
                            d(V.tensor_tensor(sel, sel, tmp, ALU.mult))
                            d(V.tensor_tensor(tmp, sel, const("experts"), ALU.mult))
                            d(V.tensor_reduce(ov[:, 0:1], tmp, AX, ALU.add))
                            d(V.scalar_tensor_tensor(tmp, ob, -float(SLOTS), base, ALU.mult, ALU.add))
                            d(V.tensor_tensor(tmp, tmp, sel, ALU.mult))
                            d(V.tensor_reduce(ov[:, 1:2], tmp, AX, ALU.add))
                            d(V.tensor_tensor(ov[:, 1:2], ov[:, 1:2], const("over_shift"), ALU.add))
                            d(V.tensor_copy(over_i[:], ov[:]))
                            steps["over"] = d.n
                            d(V.tensor_scalar(Bt, ob, float(NE - 1), float(SLOTS), ALU.add, ALU.mult))
                            d(V.tensor_scalar(A, const("experts"), float(SLOTS), None, ALU.mult))
                            for k, oh in ((0, oh1), (1, oh2)):
                                for dst, src in ((r1, rank[:]), (a1, bc(A, 1, NCH)), (o1, bc(Bt, 1, NCH))):
                                    d(V.tensor_tensor(w2[:], oh[:], src, ALU.mult))
                                    d(V.tensor_reduce(dst, w2[:], AX, ALU.add))
                                d(V.tensor_scalar(r1, r1, -1.0, None, ALU.add))
                                d(V.tensor_scalar(lt, r1, float(SLOTS), None, ALU.is_lt))
                                d(V.tensor_tensor(a1, a1, o1, ALU.subtract))
                                d(V.tensor_tensor(a1, a1, lt, ALU.mult))
                                d(V.tensor_tensor(r1, r1, o1, ALU.add))
                                d(V.tensor_tensor(r1, r1, a1, ALU.add))
                                d(V.tensor_copy(idx[:, :, 2 + k], r1))

                        @block.tensor
                        def _(pe):
                            pe.wait_ge(s_d, steps["chosen"])
                            TE.matmul(pp[0][:, 0:NE * NCH], const("upper"), w1[:].rearrange("p c n -> p (c n)"), start=True, stop=False)
                            TE.matmul(pp[0][:, 0:NE * NCH], ones, before[:, 0:NCH, :].rearrange("p c n -> p (c n)"), start=False, stop=True)
                            ins = TE.matmul(pp[1][:, 0:NE], ones, before[:, NCH, :], start=True, stop=True)
                            ins.then_inc(s_r, 1)

                        @block.scalar
                        def _(act):
                            act.wait_ge(s_d, steps["group"])
                            act.activation(ge[:], ge[:], ACT.Exp).then_inc(s_a, 1)
                            act.wait_ge(s_d, steps["chosen"])
                            t = sc[:, 5, :]
                            act.activation(t, t, ACT.Exp).then_inc(s_a, 1)

                        @block.gpsimd
                        def _(pool):
                            for k in range(2):
                                pool.wait_ge(s_d, steps[f"to{k}"])
                                for c, r in enumerate(ROWS):
                                    pool.indirect_dma_start(xs, bass.IndirectOffsetOnAxis(idx[:r, c, k:k + 1], 0), xn[:r, c, :], None).then_inc(s_sc, 16)
                            pool.wait_ge(s_sc, 16 * 2 * NCH)

                        @block.sync
                        def _(sp):
                            sp.wait_ge(s_d, steps["over"])
                            sp.dma_start(over_rows, over_i[:]).then_inc(s_z, 16)
                            sp.wait_ge(s_z, 16)

                XB = 4
                xg = xn[0:SLOTS, 0:XB, :]
                xT = [mb(f"tile_T{k}_", [P, DJ, SLOTS]) for k in range(2)]
                sg = [mb(f"silu{k}_", [P, P]) for k in range(2)]
                hh = [mb(f"hidden{k}_", [P, P]) for k in range(2)]
                hT = [mb(f"hidden_T{k}_", [P, 2, SLOTS]) for k in range(2)]
                yr = [mb(f"tile_out{k}_", [P, D // 2]) for k in range(2)]
                def credits(pe, dve, act, s):
                    if pe is not None:
                        pe.sem_inc(s.turned, s.deep)
                        pe.sem_inc(s.dn, s.deep)
                        pe.sem_inc(s.gu, s.two)
                    if dve is not None:
                        dve.sem_inc(s.h, s.two)
                        dve.sem_inc(s.xT, 1)
                        dve.sem_inc(s.hT, 1)
                    if act is not None:
                        act.sem_inc(s.y, 1)
                        for st in s.st:
                            act.sem_inc(st, 16)

                def fetch_rows(sp, s, e, k, row):
                    sp.wait_ge(s.turned, e + 1)
                    sp.dma_start(xg[:, k, :], xs[row, :]).then_inc(s.x[k], 16)

                def fetch(sp, s, e, k, expert, row):
                    sp.wait_ge(s.dn, e + 1)
                    fetch_weights(sp, s, k, expert)
                    fetch_rows(sp, s, e, k, row)

                def turn(pe, s, e, k, n):
                    pe.wait_ge(s.x[k], 16 * (n + 1))
                    pe.wait_ge(s.xT, e + 1)
                    xv = xg[:, k, :].rearrange("t (p j) -> t j p", j=DJ)
                    pe.sem_inc(s.order, 1)
                    for j in range(DJ):
                        ins = TE.transpose(pp[3][:, j * SLOTS:(j + 1) * SLOTS], xv[:, j, :], ident[:SLOTS, :SLOTS])
                    ins.then_inc(s.turned, 1)

                def gate_up(pe, s, e, k, n, half):
                    b = k % s.two
                    if half == 0:
                        pe.wait_ge(s.xT, e + 2)
                        pe.wait_ge(s.w[k], 48 * (n + 1))
                        pe.wait_ge(s.h, e + 1)
                    w = slots[k][:, 0:4096].rearrange("p (g j n) -> p g j n", g=2, j=DJ)
                    for j in range(half * DJ // 2, (half + 1) * DJ // 2):
                        for q in range(2):
                            ins = TE.matmul(pp[0][q * SLOTS:(q + 1) * SLOTS, b * 512:b * 512 + 2 * P], xT[b][:, j, :], w[:, :, j, q * P:(q + 1) * P],
                                            start=(j == 0), stop=(j == DJ - 1))
                    if half == 1:
                        ins.then_inc(s.gu, 1)

                def turn_hidden(pe, s, e, k):
                    b = k % s.two
                    pe.wait_ge(s.h, e + 1 + s.two)
                    pe.wait_ge(s.hT, e + 1)
                    pe.sem_inc(s.order, 1)
                    TE.transpose(pp[1][:, 0:P], hh[b][:], ident).then_inc(s.ht, 1)

                def down(pe, s, e, k):
                    b = k % s.two
                    pe.wait_ge(s.hT, e + 2)
                    pe.wait_ge(s.y, e + 1)
                    w = slots[k][:, 4096:6144].rearrange("p (j n) -> p j n", j=2)
                    for j in range(2):
                        for q in range(2):
                            ins = TE.matmul(pp[2][q * SLOTS:(q + 1) * SLOTS, 0:512], hT[b][:, j, :], w[:, j, q * 512:(q + 1) * 512], start=(j == 0), stop=(j == 1))
                    ins.then_inc(s.dn, 1)

                def keep_tile(dve, s, e, k):
                    b = k % s.two
                    dve.wait_ge(s.turned, e + 1 + s.deep)
                    dve.wait_ge(s.gu, e + 1)
                    V.tensor_tensor(xT[b][:], pp[3][:, 0:DJ * SLOTS].rearrange("p (j t) -> p j t", j=DJ), bc(gains[:, G_FFN + l, :], 2, SLOTS),
                                    ALU.mult).then_inc(s.xT, 1)

                def hidden(dve, s, e, k):
                    b = k % s.two
                    dve.wait_ge(s.sg, e + 1)
                    V.tensor_tensor(hh[b][:], sg[b][:], pp[0][:, b * 512 + P:b * 512 + 2 * P], ALU.mult).then_inc(s.h, 1)

                def keep_hidden(dve, s, e, k):
                    b = k % s.two
                    dve.wait_ge(s.ht, e + 1)
                    V.tensor_copy(hT[b][:], pp[1][:, 0:2 * SLOTS].rearrange("p (j t) -> p j t", j=2)).then_inc(s.hT, 1)

                def silu(act, s, e, k):
                    b = k % s.two
                    act.wait_ge(s.gu, e + 1 + s.two)
                    act.wait_ge(s.h, e + 1)
                    act.activation(sg[b][:], pp[0][:, b * 512:b * 512 + P], ACT.Silu).then_inc(s.sg, 1)

                def store(act, s, e, k, n, dst):
                    b = k % s.two
                    act.wait_ge(s.dn, e + 1 + s.deep)
                    act.wait_ge(s.st[b], 16 * n + 16)
                    act.activation(yr[b][:], pp[2][:, 0:512], ACT.Copy).then_inc(s.y, 1)
                    act.wait_ge(s.y, e + 2)
                    act.dma_start(dst.rearrange("t (q n) -> q t n", q=2), yr[b][:]).then_inc(s.st[b], 16)

                with nc.Block() as block:
                    @block.sync
                    def _(sp):
                        def row_of(e):
                            row = sp.value_load(base_i[0:1, e], min_val=0, max_val=2 * T)
                            return bass.ds(row, SLOTS)

                        for e in range(4):
                            sp.dma_start(xg[:, e, :], xs[row_of(slice(e, e + 1)), :]).then_inc(main.x[e], 16)
                        with sp.Fori(0, NE // 4 - 1) as i:
                            for k in range(4):
                                e = i * 4 + 4 + k
                                fetch(sp, main, e, k, bass.ds(e, 1), row_of(bass.ds(e, 1)))

                    @block.tensor
                    def _(pe):
                        def step(e, k, n, n_next):
                            gate_up(pe, main, e, k, n, 0)
                            turn_hidden(pe, main, e - 1, (k - 1) % 4)
                            if n_next is not None:
                                turn(pe, main, e + 1, (k + 1) % 4, n_next)
                            gate_up(pe, main, e, k, n, 1)
                            down(pe, main, e - 1, (k - 1) % 4)

                        credits(pe, None, None, main)
                        turn(pe, main, 0, 0, 0)
                        gate_up(pe, main, 0, 0, 0, 0)
                        turn(pe, main, 1, 1, 0)
                        gate_up(pe, main, 0, 0, 0, 1)
                        with pe.Fori(0, NE // 4 - 1) as i:
                            for k in range(1, 5):
                                step(i * 4 + k, k % 4, i + k // 4, i + (k + 1) // 4)
                        for e in range(NE - 3, NE):
                            step(e, e % 4, e // 4, (e + 1) // 4 if e + 1 < NE else None)
                        turn_hidden(pe, main, NE - 1, 3)
                        down(pe, main, NE - 1, 3)

                    @block.vector
                    def _(dve):
                        def step(e, k, last=False):
                            keep_hidden(dve, main, e - 1, (k - 1) % 4)
                            if not last:
                                keep_tile(dve, main, e + 1, (k + 1) % 4)
                            hidden(dve, main, e, k)

                        credits(None, dve, None, main)
                        keep_tile(dve, main, 0, 0)
                        keep_tile(dve, main, 1, 1)
                        hidden(dve, main, 0, 0)
                        with dve.Fori(0, NE // 4 - 1) as i:
                            for k in range(1, 5):
                                step(i * 4 + k, k % 4)
                        for e in range(NE - 3, NE):
                            step(e, e % 4, last=e == NE - 1)
                        keep_hidden(dve, main, NE - 1, 3)

                    @block.scalar
                    def _(act):
                        def step(e, k, n):
                            silu(act, main, e, k)
                            store(act, main, e - 1, (k - 1) % 4, n, ys[bass.ds((e - 1) * SLOTS, SLOTS), :])

                        credits(None, None, act, main)
                        silu(act, main, 0, 0)
                        with act.Fori(0, NE // 4 - 1) as i:
                            for k in range(1, 5):
                                step(i * 4 + k, k % 4, i * 2 + (k - 1) // 2)
                        for e in range(NE - 3, NE):
                            step(e, e % 4, (e - 1) // 2)
                        store(act, main, NE - 1, 3, (NE - 1) // 2, ys[bass.ds((NE - 1) * SLOTS, SLOTS), :])
                        for b in range(2):
                            act.wait_ge(main.st[b], 16 + 16 * NE // 2)

                with nc.Block() as block:
                    def count(eng):
                        return eng.value_load(n_i[0:1, 0:1], min_val=0, max_val=OVER)

                    @block.sync
                    def _(sp):
                        n = count(sp)
                        with sp.If(n > 0):
                            with sp.Fori(0, n) as j:
                                expert = sp.value_load(over_rows[bass.ds(j, 1), 0:1], min_val=0, max_val=NE - 1)
                                row = sp.value_load(over_rows[bass.ds(j, 1), 1:2], min_val=0, max_val=2 * T)
                                fetch(sp, over, j, 0, bass.ds(expert, 1), bass.ds(row, SLOTS))

                    @block.tensor
                    def _(pe):
                        n = count(pe)
                        credits(pe, None, None, over)
                        with pe.If(n > 0):
                            with pe.Fori(0, n) as j:
                                turn(pe, over, j, 0, j)
                                gate_up(pe, over, j, 0, j, 0)
                                gate_up(pe, over, j, 0, j, 1)
                                turn_hidden(pe, over, j, 0)
                                down(pe, over, j, 0)

                    @block.vector
                    def _(dve):
                        n = count(dve)
                        credits(None, dve, None, over)
                        with dve.If(n > 0):
                            with dve.Fori(0, n) as j:
                                keep_tile(dve, over, j, 0)
                                hidden(dve, over, j, 0)
                                keep_hidden(dve, over, j, 0)

                    @block.scalar
                    def _(act):
                        n = count(act)
                        credits(None, None, act, over)
                        with act.If(n > 0):
                            with act.Fori(0, n) as j:
                                silu(act, over, j, 0)
                                store(act, over, j, 0, j, ys[bass.ds(j * SLOTS + NE * SLOTS, SLOTS), :])
                                act.wait_ge(over.st[0], j * 16 + 32)

                parts = [slots[n // 6][:, (n % 6) * D:(n % 6 + 1) * D] for n in range(2 * NCH)]
                s_y, s_c = [sem(f"gather{l}_{n}") for n in range(2 * NCH)], sem(f"combine{l}")
                with nc.Block() as block:
                    @block.gpsimd
                    def _(pool):
                        for n in range(2 * NCH):
                            c, k = divmod(n, 2)
                            r = ROWS[c]
                            pool.indirect_dma_start(parts[n][:r, :], None, ys, bass.IndirectOffsetOnAxis(idx[:r, c, 2 + k:3 + k], 0)).then_inc(s_y[n], 16)

                    @block.vector
                    def _(dve):
                        d = Chain(dve, s_c)
                        for n in range(2 * NCH):
                            c, k = divmod(n, 2)
                            r = ROWS[c]
                            dve.wait_ge(s_y[n], 16)
                            d(V.scalar_tensor_tensor(x[:r, c, :], parts[n][:r, :], gate[:r, k, c:c + 1], x[:r, c, :], ALU.mult, ALU.add))

        reuse_semaphores()
        experts(0)
        reuse_semaphores()
        dump("x_1", x[:, 0:NC_P, :])
        dump("x_1_s", x[0:NS, NC_P, :])

        L1 = ctx.enter_context(ExitStack())
        cT = sb("latent_T", [P, 2, T], where=L1)
        krT = sb("rope_T", [RP, T], where=L1)
        c_tok = sb("latent_rows", [P, NCH, KL], where=L1)
        qmT1 = sb("qmT1", [P, 2, T], where=L1)
        w_uv = sb("w_uv_rows", [P, 2, DN_H * P], where=L1)
        AT1 = ctx.enter_context(ExitStack())
        q_latT = sb("q_latent_T", [P, DN_H, 2, T], where=AT1)
        qrT = sb("q_rope_T", [RP, DN_H, T], where=AT1)
        w_ukT = sb("w_uk_T", [P, DN_H, KL], where=AT1)
        page_i = sb("page_index", [P, DB], U32, where=AT1)
        QX = ctx.enter_context(ExitStack())
        cqT = sb("cq_T", [P, 3, T], where=QX)
        hT = q_latT[:].rearrange("p h a t -> p (h a t)")[:, 0:DJ * T].rearrange("p (j t) -> p j t", j=DJ)
        norm_transposed("norm1", x, ROWS, [(G_MIX + 1, uT), (G_KV, hT)])
        W_KV = KL + RP
        w_dkv = ring[0][:, 0:DJ * W_KV].rearrange("p (j n) -> p j n", j=DJ)
        w_uq = ring[0][:, DJ * W_KV:DJ * W_KV + 3 * 1152].rearrange("p (j n) -> p j n", j=3)
        w_inb = ring[1][:, 0:DJ * 640].rearrange("p (j n) -> p j n", j=DJ)
        cos = const("cos").rearrange("p (c f) -> p c f", c=NCH)
        sin = const("sin").rearrange("p (c f) -> p c f", c=NCH)

        def rotate(d, out, src, tmp, lead):
            h = RP // 2
            a, b = src[..., 0:h], src[..., h:RP]
            d(V.tensor_tensor(out[..., 0:h], a, lead(cos), ALU.mult))
            d(V.tensor_tensor(tmp, b, lead(sin), ALU.mult))
            d(V.tensor_tensor(out[..., 0:h], out[..., 0:h], tmp, ALU.subtract))
            d(V.tensor_tensor(out[..., h:RP], b, lead(cos), ALU.mult))
            d(V.tensor_tensor(tmp, a, lead(sin), ALU.mult))
            d(V.tensor_tensor(out[..., h:RP], out[..., h:RP], tmp, ALU.add))

        with ExitStack() as cx:
            raw1 = sb("kv_raw", [P, NCH, W_KV], where=cx)
            rawq = sb("cq_raw", [P, NCH, QL], where=cx)
            sqr = sb("sq1", [P, QL], where=cx)
            kr_tok = sb("rope_rows", [P, NCH, RP], where=cx)
            tmp = sb("rope_tmp", [P, NCH, RP // 2], where=cx)
            st = sb("rms1", [P, 2, NCH], where=cx)
            g_lat = sb("g_lat", [P, KL], where=cx)
            gq = sb("g_q", [P, 3], where=cx)
            pg = sb("pages", [P, DB], I32, where=cx)
            pgf = sb("pages_f", [P, DB], where=cx)
            s_w, s_m, s_q, s_d, s_a, s_c, s_t, s_k, s_st, s_v, s_qm, s_i = (
                sem(f"kv_{m}") for m in ("weights", "product", "cq_product", "dve", "act", "copied", "turned", "kept", "stored", "uv", "queries", "small"))
            with nc.Block() as block:
                @block.sync
                def _(sp):
                    sp.dma_start(w_dkv, pj(I["w_dkv"])).then_inc(s_w, 16)
                    sp.dma_start(w_inb, pj(I["w_in_b"][0])).then_inc(s_w, 16)
                    sp.dma_start(g_lat[:], I["g_kv_latent"].partition_broadcast(P)).then_inc(s_i, 16)
                    sp.dma_start(gq[:], I["g_q"][0].rearrange("(p j) -> p j", p=P)).then_inc(s_i, 16)
                    with nc.allow_non_contiguous_dma("a table of 128 page numbers"):
                        for j in range(NPG):
                            sp.dma_start(pg[8 * j:8 * j + 8, :], I["page_table"][:, j].partition_broadcast(8)).then_inc(s_i, 16)
                    sp.dma_start(w_uq, pj(I["w_uq"][0])).then_inc(s_v, 16)
                    sp.dma_start(w_uv[:], I["w_uv"].rearrange("(a p) h v -> p a (h v)", p=P)).then_inc(s_v, 16)
                    sp.wait_ge(s_d, 7 + 11)
                    sp.dma_start(O["kv_latent_prompt"][0].rearrange("(c p) n -> p c n", p=P), c_tok[:, 0:NC_P, :]).then_inc(s_st, 16)
                    sp.dma_start(O["kv_latent_sample"].rearrange("b t n -> (b t) n"), c_tok[0:NS, NC_P, :]).then_inc(s_st, 16)
                    sp.dma_start(O["k_rope_prompt"][0].rearrange("(c p) n -> p c n", p=P), kr_tok[:, 0:NC_P, :]).then_inc(s_st, 16)
                    sp.dma_start(O["k_rope_sample"].rearrange("b t n -> (b t) n"), kr_tok[0:NS, NC_P, :]).then_inc(s_st, 16)
                    sp.wait_ge(s_st, 64)
                    sp.wait_ge(s_v, 32)

                @block.tensor
                def _(pe):
                    pe.wait_ge(s_w, 32)
                    for c, r in enumerate(ROWS):
                        b = (c % 2) * 512
                        if c >= 2:
                            pe.wait_ge(s_c, 2 * (c - 1))
                        for j in range(DJ):
                            ins = TE.matmul(pp[0][:r, b:b + W_KV], hT[:, j, offset(c):offset(c) + r], w_dkv[:, j, :], start=(j == 0), stop=(j == DJ - 1))
                        ins.then_inc(s_m, 1)
                        for j in range(DJ):
                            ins = TE.matmul(pp[1][:r, b:b + QL], uT[:, j, offset(c):offset(c) + r], w_inb[:, j, 0:QL], start=(j == 0), stop=(j == DJ - 1))
                        ins.then_inc(s_m, 1)
                    for pr in range(2):
                        for t, at in HALVES:
                            for j in range(DJ):
                                ins = TE.matmul(pp[2 + pr][:, at], w_inb[:, j, QL + pr * P:QL + (pr + 1) * P], uT[:, j, t], start=(j == 0), stop=(j == DJ - 1))
                        ins.then_inc(s_qm, 1)
                    pe.wait_ge(s_d, 7 + 11)
                    for c, r in enumerate(ROWS):
                        if c >= 2:
                            pe.wait_ge(s_k, 3 * (c - 1))
                        q = pp[c % 2]
                        for a in range(2):
                            TE.transpose(q[:, a * P:a * P + r], c_tok[:r, c, a * P:(a + 1) * P], ident[:r, :r])
                        TE.transpose(q[0:RP, 2 * P:2 * P + r], kr_tok[:r, c, :], ident[:r, :r])
                        qv = rawq[:r, c, :].rearrange("t (p j) -> t j p", j=3)
                        for j in range(3):
                            ins = TE.transpose(q[:, (4 + j) * P:(4 + j) * P + r], qv[:, j, :], ident[:r, :r])
                        ins.then_inc(s_t, 1)

                @block.scalar
                def _(act):
                    a = Chain(act, s_a)
                    for c in range(NCH):
                        act.wait_ge(s_c, 2 * (c + 1))
                        a(act.activation(sqr[:, 0:KL], raw1[:, c, 0:KL], ACT.Square, accum_out=st[:, 0, c:c + 1]))
                        a(act.activation(sqr[:], rawq[:, c, :], ACT.Square, accum_out=st[:, 1, c:c + 1]))
                    act.wait_ge(s_d, 4)
                    a(act.activation(st[:], st[:], ACT.Sqrt))
                    for pr in range(2):
                        act.wait_ge(s_qm, pr + 1)
                        act.activation(all_tokens(qmT1[:, pr, :]), halves(pp[2 + pr]), ACT.Copy).then_inc(s_q, 1)

                @block.vector
                def _(dve):
                    d = Chain(dve, s_d)
                    d(V.memset(raw1[:, NC_P, :], 0.0))
                    d(V.memset(rawq[:, NC_P, :], 0.0))
                    for c, r in enumerate(ROWS):
                        b = (c % 2) * 512
                        for k, (dst, n) in enumerate(((raw1, W_KV), (rawq, QL))):
                            dve.wait_ge(s_m, 2 * c + k + 1)
                            V.tensor_copy(dst[:r, c, :], pp[k][:r, b:b + n]).then_inc(s_c, 1)
                    dve.wait_ge(s_a, 10)
                    dve.wait_ge(s_i, 32 + 16 * NPG)
                    d(V.tensor_scalar(st[:, 0, :], st[:, 0, :], 1.0 / KL, EPS, ALU.mult, ALU.add))
                    d(V.tensor_scalar(st[:, 1, :], st[:, 1, :], 1.0 / QL, EPS, ALU.mult, ALU.add))
                    dve.wait_ge(s_a, 11)
                    d(V.reciprocal(st[:], st[:]))
                    d(V.tensor_tensor(c_tok[:], raw1[:, :, 0:KL], bc(st[:, 0, :], 2, KL), ALU.mult))
                    d(V.tensor_tensor(c_tok[:], c_tok[:], bc(g_lat[:], 1, NCH), ALU.mult))
                    d(V.tensor_tensor(rawq[:], rawq[:], bc(st[:, 1, :], 2, QL), ALU.mult))
                    rotate(d, kr_tok[:], raw1[:, :, KL:], tmp[:], lambda t: t)
                    d(V.tensor_copy(pgf[:], pg[:]))
                    d(V.tensor_scalar(pgf[:], pgf[:], 8.0, const("eighth"), ALU.mult, ALU.add))
                    d(V.tensor_copy(page_i[:], pgf[:]))
                    d(V.memset(tmp[:], 0.0))
                    for c, r in enumerate(ROWS):
                        dve.wait_ge(s_t, c + 1)
                        q = pp[c % 2]
                        V.tensor_copy(cT[:, :, offset(c):offset(c) + r], q[:, 0:2 * P].rearrange("p (a t) -> p a t", a=2)[:, :, :r]).then_inc(s_k, 1)
                        V.tensor_copy(krT[:, offset(c):offset(c) + r], q[0:RP, 2 * P:2 * P + r]).then_inc(s_k, 1)
                        V.tensor_tensor(cqT[:, :, offset(c):offset(c) + r], q[:, 4 * P:7 * P].rearrange("p (j t) -> p j t", j=3)[:, :, :r],
                                        bc(gq[:], 2, r), ALU.mult).then_inc(s_k, 1)

        with ExitStack() as cx:
            w_uk = ring[1][:, 0:1536].rearrange("p (a n) -> p a n", a=2)
            q_nT = sb("q_nope_T", [P, DN_H, T], where=cx)
            qr_raw = ring[1][:, 1536:3456].rearrange("p (c h n) -> p c h n", c=NCH, h=DN_H)
            qr_tok = ring[1][:, 3456:5376].rearrange("p (c h n) -> p c h n", c=NCH, h=DN_H)
            tmq = sb("qr_tmp", [P, NCH, DN_H, RP // 2], where=cx)
            s_w, s_n, s_nk, s_r, s_rk, s_d, s_u, s_uk, s_l, s_lk, s_t, s_tk = (
                sem(f"q_{m}") for m in ("w_uk", "nope", "nope_kept", "rope", "rope_kept", "dve", "uk_turned", "uk_kept", "latent", "latent_kept", "turned", "turned_kept"))
            with nc.Block() as block:
                @block.sync
                def _(sp):
                    sp.dma_start(w_uk, I["w_uk"].rearrange("(a p) h n -> p a (h n)", p=P)).then_inc(s_w, 16)

                @block.tensor
                def _(pe):
                    wr = w_uq.rearrange("p j (h n) -> p j h n", h=DN_H)
                    for c, r in enumerate(ROWS):
                        if c >= 2:
                            pe.wait_ge(s_rk, c - 1)
                        for j in range(3):
                            ins = TE.matmul(pp[3][:r, (c % 2) * 512:(c % 2) * 512 + DN_H * RP], cqT[:, j, offset(c):offset(c) + r],
                                            wr[:, j, :, P:P + RP], start=(j == 0), stop=(j == 2))
                        ins.then_inc(s_r, 1)
                    pe.wait_ge(s_w, 16)
                    for h in range(DN_H):
                        if h >= 2:
                            pe.wait_ge(s_uk, h - 1)
                        for a in range(2):
                            ins = TE.transpose(pp[2][:, (h % 2) * 512 + a * P:(h % 2) * 512 + (a + 1) * P], w_uk[:, a, h * P:(h + 1) * P], ident)
                        ins.then_inc(s_u, 1)
                    for h in range(DN_H):
                        if h >= 2:
                            pe.wait_ge(s_nk, h - 1)
                        for t, at in HALVES:
                            for j in range(3):
                                ins = TE.matmul(pp[h % 2][:, at], wr[:, j, h, 0:P], cqT[:, j, t], start=(j == 0), stop=(j == 2))
                        ins.then_inc(s_n, 1)
                    pe.wait_ge(s_d, 7)
                    for h in range(DN_H):
                        if h == 0:
                            pe.wait_ge(s_rk, NCH)
                        else:
                            pe.wait_ge(s_tk, h)
                        for c in range(NC_P):
                            TE.transpose(pp[3][0:RP, c * P:(c + 1) * P], qr_tok[:, c, h, :], ident)
                        TE.transpose(pp[3][0:RP, SEQ:T], qr_tok[0:NS, NC_P, h, :], ident[0:NS, 0:NS]).then_inc(s_t, 1)
                        for a in range(2):
                            n = 2 * h + a
                            if n == 0:
                                pe.wait_ge(s_nk, DN_H)
                            if n >= 2:
                                pe.wait_ge(s_lk, n - 1)
                            if n == 0:
                                pe.wait_ge(s_uk, DN_H)
                            for t, at in HALVES:
                                ins = TE.matmul(pp[n % 2][:, at], w_ukT[:, h, a * P:(a + 1) * P], q_nT[:, h, t], start=True, stop=True)
                            ins.then_inc(s_l, 1)

                @block.scalar
                def _(act):
                    for h in range(DN_H):
                        act.wait_ge(s_n, h + 1)
                        act.activation(all_tokens(q_nT[:, h, :]), halves(pp[h % 2]), ACT.Copy).then_inc(s_nk, 1)
                    for h in range(DN_H):
                        for a in range(2):
                            act.wait_ge(s_l, 2 * h + a + 1)
                            act.activation(all_tokens(q_latT[:, h, a, :]), halves(pp[a]), ACT.Copy).then_inc(s_lk, 1)

                @block.vector
                def _(dve):
                    d = Chain(dve, s_d)
                    d(V.memset(qr_raw[:, NC_P], 0.0))
                    for c, r in enumerate(ROWS):
                        dve.wait_ge(s_r, c + 1)
                        V.tensor_copy(qr_raw[:r, c], pp[3][:r, (c % 2) * 512:(c % 2) * 512 + DN_H * RP].rearrange("p (h n) -> p h n", h=DN_H)).then_inc(s_rk, 1)
                    for h in range(DN_H):
                        dve.wait_ge(s_u, h + 1)
                        V.tensor_copy(w_ukT[:, h, :], pp[2][:, (h % 2) * 512:(h % 2) * 512 + KL]).then_inc(s_uk, 1)
                    dve.wait_ge(s_rk, NCH)
                    hf = RP // 2
                    for k, (o, f1, f2, op) in enumerate(((0, cos, sin, ALU.subtract), (hf, sin, cos, ALU.add))):
                        for h in range(DN_H):
                            V.tensor_tensor(qr_tok[:, :, h, o:o + hf], qr_raw[:, :, h, 0:hf], f1, ALU.mult)
                            ins = V.tensor_tensor(tmq[:, :, h, :], qr_raw[:, :, h, hf:RP], f2, ALU.mult)
                        d(ins)
                        v = qr_tok.rearrange("p c h n -> p (c h) n")[:, :, o:o + hf]
                        d(V.tensor_tensor(v, v, tmq[:].rearrange("p c h n -> p (c h) n"), op))
                    d(V.memset(tmq[:, 0, 0, :], 0.0))
                    d(V.memset(tmq[:, 0, 0, :], 0.0))
                    for h in range(DN_H):
                        dve.wait_ge(s_t, h + 1)
                        V.tensor_copy(qrT[:, h, :], pp[3][0:RP, 0:T]).then_inc(s_tk, 1)
        QX.close()
        dump("q_latT", q_latT[:])
        dump("qrT", qrT[:])

        E8 = PAGE // 8
        lat_e = I["cache_kv_latent"].rearrange("n (e t) c -> (n e) (t c)", e=8)
        rope_e = I["cache_k_rope"].rearrange("n (e t) c -> (n e) (t c)", e=8)
        CB = 3
        s_pages = [sem(f"pages{k}") for k in range(CB)]
        rope_rows2 = sb("rope_cache2", [P, E8 * RP], where=AT1)

        def cache_of(b):
            k = b % CB
            if k < 2:
                return ring[k][:, 0:E8 * KL], ring[k][:, E8 * KL:E8 * W_KV]
            return uT[:].rearrange("p j t -> p (j t)")[:, 0:E8 * KL], rope_rows2[:]

        def fetch_pages(pool, b):
            for dst, src in zip(cache_of(b), (lat_e, rope_e)):
                pool.indirect_dma_start(dst, None, src, bass.IndirectOffsetOnAxis(page_i[:, b:b + 1], 0)).then_inc(s_pages[b % CB], 16)

        with ExitStack() as cx:
            pr = [sb(f"pr{k}", [P, SEQ], where=cx) for k in range(2)]
            prT = [sb(f"prT{k}", [P, NC_P, P], where=cx) for k in range(2)]
            st = sb("attn_stat", [P, 4, DN_H * NC_P], where=cx)
            units = [(h, i) for h in range(DN_H) for i in range(NC_P)]
            s_s, s_m, s_x, s_p, s_t, s_e, s_o, s_k, s_d = (sem(f"attn_{m}") for m in ("scores", "max", "exp", "probs", "turned", "turned_kept", "out", "kept", "dve"))
            with nc.Block() as block:
                @block.gpsimd
                def _(pool):
                    for b in range(CB):
                        fetch_pages(pool, b)

                @block.tensor
                def _(pe):
                    def scores(n):
                        h, i = units[n]
                        if n >= 2:
                            pe.wait_ge(s_x, n - 1)
                        o, k = (n % 2) * 512, (i + 1) * P
                        tq = slice(i * P, (i + 1) * P)
                        for a in range(2):
                            TE.matmul(pp[0][:, o:o + k], q_latT[:, h, a, tq], cT[:, a, 0:k], start=(a == 0), stop=False)
                        TE.matmul(pp[0][:, o:o + k], qrT[:, h, tq], krT[:, 0:k], start=False, stop=True).then_inc(s_s, 1)

                    def turn(n):
                        h, i = units[n]
                        o = (n % 2) * 512
                        pe.wait_ge(s_p, n + 1)
                        if n >= 2:
                            pe.wait_ge(s_e, n - 1)
                        for k in range(i + 1):
                            ins = TE.transpose(pp[1][:, o + k * P:o + (k + 1) * P], pr[n % 2][:, k * P:(k + 1) * P], ident)
                        ins.then_inc(s_t, 1)

                    def out(n):
                        h, i = units[n]
                        o = (n % 2) * 512
                        pe.wait_ge(s_e, n + 1)
                        if n >= 2:
                            pe.wait_ge(s_k, n - 1)
                        for a in range(2):
                            for k in range(i + 1):
                                ins = TE.matmul(pp[2][:, o + a * P:o + (a + 1) * P], c_tok[:, k, a * P:(a + 1) * P], prT[n % 2][:, k, :], start=(k == 0), stop=(k == i))
                        ins.then_inc(s_o, 1)

                    scores(0)
                    scores(1)
                    turn(0)
                    for n in range(len(units)):
                        if n + 2 < len(units):
                            scores(n + 2)
                        if n + 1 < len(units):
                            turn(n + 1)
                        out(n)

                @block.scalar
                def _(act):
                    def exp(n):
                        h, i = units[n]
                        o, k = (n % 2) * 512, (i + 1) * P
                        act.wait_ge(s_m, n + 1)
                        if n >= 2:
                            act.wait_ge(s_t, n - 1)
                        act.activation(pr[n % 2][:, 0:k], pp[0][:, o:o + k], ACT.Exp, bias=st[:, 1, n:n + 1], scale=MLA_SCALE, accum_out=st[:, 2, n:n + 1]).then_inc(s_x, 1)

                    exp(0)
                    for n, (h, i) in enumerate(units):
                        o, k = (n % 2) * 512, (i + 1) * P
                        if n + 1 < len(units):
                            exp(n + 1)
                        act.wait_ge(s_t, n + 1)
                        if n >= 2:
                            act.wait_ge(s_o, n - 1)
                        act.activation(prT[n % 2][:, 0:i + 1, :], pp[1][:, o:o + k].rearrange("p (k t) -> p k t", t=P), ACT.Copy).then_inc(s_e, 1)

                def keep(dve, n):
                    h, i = units[n]
                    dve.wait_ge(s_o, n + 1)
                    o = (n % 2) * 512
                    V.tensor_copy(q_latT[:, h, :, i * P:(i + 1) * P], pp[2][:, o:o + 2 * P].rearrange("p (a t) -> p a t", a=2)).then_inc(s_k, 1)

                @block.vector
                def _(dve):
                    d = Chain(dve, s_d)

                    def maximum(n):
                        h, i = units[n]
                        o, k = (n % 2) * 512, (i + 1) * P
                        dve.wait_ge(s_s, n + 1)
                        d(V.tensor_tensor(pp[0][:, o + k - P:o + k], pp[0][:, o + k - P:o + k], const("causal"), ALU.add))
                        d(V.tensor_reduce(st[:, 0, n:n + 1], pp[0][:, o:o + k], AX, ALU.max))
                        V.tensor_scalar(st[:, 1, n:n + 1], st[:, 0, n:n + 1], -MLA_SCALE, None, ALU.mult).then_inc(s_m, 1)

                    def normalise(n):
                        k = (units[n][1] + 1) * P
                        dve.wait_ge(s_x, n + 1)
                        d(V.reciprocal(st[:, 3, n:n + 1], st[:, 2, n:n + 1]))
                        V.tensor_scalar(pr[n % 2][:, 0:k], pr[n % 2][:, 0:k], st[:, 3, n:n + 1], None, ALU.mult).then_inc(s_p, 1)

                    maximum(0)
                    maximum(1)
                    normalise(0)
                    for n in range(len(units)):
                        if n + 1 < len(units):
                            normalise(n + 1)
                        if n + 2 < len(units):
                            maximum(n + 2)
                        if n >= 1:
                            keep(dve, n - 1)
                    keep(dve, len(units) - 1)


        HQ, HP = DN_H * DS, 32
        NG4 = P // HP
        KG = E8 // NG4
        with ExitStack() as cx:
            KT = sb("keys_T", [P, 2, E8 * P], where=cx)
            KR = sb("rope_keys_T", [P, E8 * P], where=cx)
            pb = [sb(f"probs{k}", [P, KG * P], where=cx) for k in range(2)]
            pT = mem_v[:, 0].rearrange("p m (k t) -> p (m k) t", t=P)
            st = sb("samples_stat", [P, 7, DB], where=cx)
            mx, nb, ss, s2, wt, Mb, L = (st[:, k, :] for k in range(7))
            qls = w_ukT[:, 0:2, :].rearrange("p a (b q) -> p a b q", b=DB)
            qrs = w_ukT[:, 2, :].rearrange("p (b q) -> p b q", b=DB)
            snT, sn = w_ukT[0:NS, 3, :], w_ukT[0:HP, 4, :]
            pn, pTn, mn, M8, Mg = (w_ukT[0:n, 5, o:o + k] for n, o, k in ((HP, 0, NS), (NS, 32, HP), (HP, 64, DB), (DB, 72, HP), (DB, 104, P)))
            outs = [ring[k][:, E8 * W_KV:E8 * W_KV + DB // 2 * KL].rearrange("p (i c) -> p i c", c=KL) for k in range(2)]
            s_q, s_tr, s_ea, s_ed, s_s, s_m, s_x, s_pt, s_pk, s_o, s_n, s_d, s_nw, s_nc, s_c, s_w = (
                sem(f"samp_{m}") for m in ("queries", "keys_turned", "keys_kept_a", "keys_kept_v", "scores", "max", "exp", "probs_turned", "probs_kept",
                                           "out", "out_kept", "dve", "new_keys", "new_copied", "combine", "weights"))
            NGR = 12

            def group(b, g):
                lat, rope = cache_of(b)
                if g < 8:
                    a, t0 = g // 4, 4 * (g % 4)
                    return [lat[:, (t0 + t) * KL + a * P:(t0 + t) * KL + (a + 1) * P] for t in range(4)], P, KT[:, a, t0 * P:(t0 + 4) * P]
                t0 = 4 * (g - 8)
                return [rope[:, (t0 + t) * RP:(t0 + t + 1) * RP] for t in range(4)], RP, KR[0:RP, t0 * P:(t0 + 4) * P]

            with nc.Block() as block:
                @block.gpsimd
                def _(pool):
                    for b in range(CB, DB):
                        pool.wait_ge(s_o, b - CB + 1)
                        fetch_pages(pool, b)

                @block.tensor
                def _(pe):
                    def keys(b, groups):
                        if groups[0] == 0:
                            pe.wait_ge(s_pages[b % CB], 32 * (b // CB + 1))
                        for g in groups:
                            n = b * NGR + g
                            if n >= 2:
                                pe.wait_ge(s_ea if n % 2 == 0 else s_ed, n // 2)
                            src, m, _ = group(b, g)
                            for t in range(4):
                                ins = TE.transpose(pp[3][0:m, (n % 2) * 512 + t * P:(n % 2) * 512 + (t + 1) * P], src[t], ident)
                            ins.then_inc(s_tr, 1)

                    def scores(b):
                        pe.wait_ge(s_ea, NGR // 2 * (b + 1))
                        pe.wait_ge(s_ed, NGR // 2 * (b + 1))
                        if b == 0:
                            pe.wait_ge(s_q, 1)
                        if b >= 2:
                            pe.wait_ge(s_x, b - 1)
                        for k in range(3):
                            for n in range(NG4):
                                q, kt = (qls[:, k, b, :], KT[:, k, n * 512:(n + 1) * 512]) if k < 2 else (qrs[:, b, :], KR[:, n * 512:(n + 1) * 512])
                                ins = TE.matmul(pp[0][HP * n:HP * (n + 1), (b % 2) * 512:(b % 2) * 512 + 512], q, kt, start=(k == 0), stop=(k == 2))
                        ins.then_inc(s_s, 1)

                    def turn(b):
                        pe.wait_ge(s_x, b + 1)
                        if b >= 1:
                            pe.wait_ge(s_pk, b)
                        for t in range(KG):
                            TE.transpose(pp[1][:, t * P:(t + 1) * P], pb[b % 2][:, t * P:(t + 1) * P], ident)
                        TE.transpose(pp[1][0:NS, 512:512 + HP], pn, ident[:HP, :HP]).then_inc(s_pt, 1)

                    def out(b):
                        pe.wait_ge(s_pk, b + 1)
                        if b >= 2:
                            pe.wait_ge(s_n, b - 1)
                        lat, o = cache_of(b)[0], (b % 2) * 512
                        for t in range(KG):
                            for n in range(NG4):
                                TE.matmul(pp[2][HP * n:HP * (n + 1), o:o + KL], pT[:, t, HP * n:HP * (n + 1)], lat[:, (KG * n + t) * KL:(KG * n + t + 1) * KL],
                                          start=(t == 0), stop=(t == KG - 1 and n > 0))
                        TE.matmul(pp[2][0:HP, o:o + KL], pTn, c_tok[0:NS, NC_P, :], start=False, stop=True).then_inc(s_o, 1)

                    pe.wait_ge(s_q, 1)
                    for a in range(2):
                        TE.matmul(pp[1][0:NS, 512:512 + DB * HP], cT[:, a, SEQ:T], qls[:, a].rearrange("p b q -> p (b q)"), start=(a == 0), stop=False)
                    TE.matmul(pp[1][0:NS, 512:512 + DB * HP], krT[:, SEQ:T], w_ukT[0:RP, 2, :], start=False, stop=True).then_inc(s_nw, 1)
                    keys(0, range(0, 4))
                    pe.wait_ge(s_nc, 1)
                    for b in range(DB):
                        ins = TE.transpose(pp[1][0:HP, b * NS:(b + 1) * NS], snT[:, b * HP:(b + 1) * HP], ident[:NS, :NS])
                    ins.then_inc(s_nw, 1)
                    keys(0, range(4, NGR))
                    scores(0)
                    for b in range(DB):
                        if b + 1 < DB:
                            keys(b + 1, range(0, 8))
                        if b == 0:
                            pe.wait_ge(s_nc, 2)
                        turn(b)
                        if b + 1 < DB:
                            keys(b + 1, range(8, NGR))
                        out(b)
                        if b + 1 < DB:
                            scores(b + 1)
                    TE.transpose(pp[1][0:DB, 0:P], mx, ident).then_inc(s_c, 1)
                    pe.wait_ge(s_w, 1)
                    TE.transpose(pp[1][:, 512:512 + DB], Mg, ident[:DB, :DB]).then_inc(s_c, 1)
                    pe.wait_ge(s_w, 2)
                    TE.matmul(pp[0][:, 0:DB], const("same_row"), L, start=True, stop=True).then_inc(s_c, 1)
                    pe.wait_ge(s_w, 4)
                    for a in range(2):
                        for b in range(DB):
                            o = (a * DB + b) * HP
                            ins = TE.matmul(pp[3][:, o:o + HP], outs[b % 2][:, b // 2, a * P:(a + 1) * P], const("same_row")[:, 0:HP], start=True, stop=True)
                    ins.then_inc(s_c, 1)

                @block.scalar
                def _(act):
                    def keep(b):
                        for g in range(0, NGR, 2):
                            n = b * NGR + g
                            act.wait_ge(s_tr, n + 1)
                            if g == 0 and b >= 1:
                                act.wait_ge(s_s, b)
                            _, m, dst = group(b, g)
                            act.activation(dst, pp[3][0:m, 0:512], ACT.Copy).then_inc(s_ea, 1)

                    keep(0)
                    for b in range(DB):
                        act.wait_ge(s_m, b + 1)
                        if b >= 1:
                            act.wait_ge(s_pt, b)
                        act.activation(pb[b % 2][:], pp[0][:, (b % 2) * 512:(b % 2) * 512 + 512], ACT.Exp, bias=nb[:, b:b + 1], scale=MLA_SCALE, accum_out=ss[:, b:b + 1])
                        act.activation(pn, sn[:, b * NS:(b + 1) * NS], ACT.Exp, bias=nb[0:HP, b:b + 1], scale=MLA_SCALE, accum_out=s2[0:HP, b:b + 1]).then_inc(s_x, 1)
                        if b + 1 < DB:
                            keep(b + 1)
                        act.wait_ge(s_o, b + 1)
                        act.activation(outs[b % 2][:, b // 2, :], pp[2][:, (b % 2) * 512:(b % 2) * 512 + KL], ACT.Copy).then_inc(s_n, 1)
                    act.wait_ge(s_nc, 3)
                    act.activation(wt, wt, ACT.Exp, scale=MLA_SCALE).then_inc(s_nc, 1)

                @block.vector
                def _(dve):
                    d = Chain(dve, s_d)

                    def keep(b):
                        for g in range(1, NGR, 2):
                            n = b * NGR + g
                            dve.wait_ge(s_tr, n + 1)
                            if g == 1 and b >= 1:
                                dve.wait_ge(s_s, b)
                            _, m, dst = group(b, g)
                            V.tensor_copy(dst, pp[3][0:m, 512:1024]).then_inc(s_ed, 1)

                    d(V.memset(w_ukT[:, 0:3, :], 0.0))
                    V.memset(KR[RP:P, :], 0.0).then_inc(s_d, 1)
                    d.n += 1
                    for a in range(2):
                        d(V.tensor_copy(qls[:, a, :, 0:HQ].rearrange("p b (h t) -> p b h t", h=DN_H), q_latT[:, :, a, SEQ:T].rearrange("p h (b t) -> p b h t", b=DB)))
                    V.tensor_copy(qrs[0:RP, :, 0:HQ].rearrange("p b (h t) -> p b h t", h=DN_H), qrT[:, :, SEQ:T].rearrange("p h (b t) -> p b h t", b=DB)).then_inc(s_q, 1)
                    dve.wait_ge(s_nw, 1)
                    V.tensor_copy(snT, pp[1][0:NS, 512:512 + DB * HP]).then_inc(s_nc, 1)
                    keep(0)
                    dve.wait_ge(s_nw, 2)
                    V.tensor_tensor(sn, pp[1][0:HP, 0:DB * NS], const("new_keys")[0:HP, :], ALU.add).then_inc(s_nc, 1)
                    dve.wait_ge(s_nc, 2)
                    d(V.tensor_reduce(mn, sn.rearrange("q (b k) -> q b k", b=DB), AX, ALU.max))
                    for b in range(DB):
                        dve.wait_ge(s_s, b + 1)
                        d(V.tensor_reduce(mx[:, b:b + 1], pp[0][:, (b % 2) * 512:(b % 2) * 512 + 512], AX, ALU.max))
                        d(V.tensor_tensor(mx[0:HP, b:b + 1], mx[0:HP, b:b + 1], mn[:, b:b + 1], ALU.max))
                        V.tensor_scalar(nb[:, b:b + 1], mx[:, b:b + 1], -MLA_SCALE, None, ALU.mult).then_inc(s_m, 1)
                        if b + 1 < DB:
                            keep(b + 1)
                        dve.wait_ge(s_pt, b + 1)
                        if b >= 1:
                            dve.wait_ge(s_o, b)
                        V.tensor_copy(pTn, pp[1][0:NS, 512:512 + HP])
                        V.tensor_copy(pT, pp[1][:, 0:512].rearrange("p (t q) -> p t q", t=KG)).then_inc(s_pk, 1)
                    dve.wait_ge(s_x, DB)
                    d(V.tensor_tensor(ss[0:HP, :], ss[0:HP, :], s2[0:HP, :], ALU.add))
                    dve.wait_ge(s_c, 1)
                    d(V.tensor_reduce(M8, pp[1][0:DB, 0:P].rearrange("b (n q) -> b q n", n=NG4), AX, ALU.max))
                    V.tensor_copy(Mg.rearrange("b (n q) -> b n q", n=NG4), bc(M8, 1, NG4)).then_inc(s_w, 1)
                    dve.wait_ge(s_c, 2)
                    d(V.tensor_copy(Mb, pp[1][:, 512:512 + DB]))
                    V.tensor_tensor(wt, mx, Mb, ALU.subtract).then_inc(s_nc, 1)
                    dve.wait_ge(s_nc, 4)
                    V.tensor_tensor(L, wt, ss, ALU.mult).then_inc(s_w, 1)
                    dve.wait_ge(s_c, 3)
                    d(V.reciprocal(Mb, pp[0][:, 0:DB]))
                    d(V.tensor_tensor(wt, wt, Mb, ALU.mult))
                    dve.wait_ge(s_n, DB)
                    for k in range(2):
                        V.tensor_tensor(outs[k], outs[k], bc(wt.rearrange("p (i k) -> p k i", k=2)[:, k], 2, KL), ALU.mult).then_inc(s_w, 1)
                    dve.wait_ge(s_c, 4)
                    for a in range(2):
                        V.tensor_copy(q_latT[:, :, a, SEQ:T].rearrange("p h (b t) -> p h b t", b=DB),
                                      pp[3][:, a * DB * HP:(a + 1) * DB * HP].rearrange("p (b q) -> p b q", b=DB)[:, :, 0:HQ].rearrange("p b (h t) -> p h b t", h=DN_H))

        w_outb = I["w_out_b"][0].rearrange("(j p) n -> p j n", p=P)
        with nc.Block() as block:
            s_m, s_k = sem("values_product"), sem("values_kept")

            @block.sync
            def _(sp):
                for n in range(2):
                    load(sp, n, f"outb{n}", (slot3(n, 512), w_outb[:, :, n * 512:(n + 1) * 512]))

            @block.tensor
            def _(pe):
                for h in range(DN_H):
                    if h >= 4:
                        pe.wait_ge(s_k, h - 3)
                    for t, at in HALVES:
                        for a in range(2):
                            ins = TE.matmul(pp[h % 4][:, at], w_uv[:, a, h * P:(h + 1) * P], q_latT[:, h, a, t], start=(a == 0), stop=(a == 1))
                    ins.then_inc(s_m, 1)

            @block.scalar
            def _(act):
                for h in range(DN_H):
                    act.wait_ge(s_m, h + 1)
                    act.activation(all_tokens(mergedT[:, h, :]), halves(pp[h % 4]), ACT.Copy).then_inc(s_k, 1)
        AT1.close()
        with ExitStack() as cx:
            mk1, mv1 = (sb(f"mem_cache_{n}", [P, DB, 2, MEM], where=cx) for n in "kv")
            kt1 = sb("mem_keys_T1", [P, 2, DB, MEM], where=cx)
            pr1 = [sb(f"mem_pr{k}", [P, 1024], where=cx) for k in range(2)]
            prT1 = sb("mem_prT", [P, 8, P], where=cx)
            zq1 = sb("mem_q", [P, 2, 1152], where=cx)
            st1 = sb("mem_stat1", [P, 4, NCH, MH], where=cx)
            memory_attention(1, qmT1, mk1[:], mv1[:], kt1, [pr1[0][:], pr1[1][:]], prT1[:], zq1[:], st1)
        project_out(1, [(slot3(0, 512), "outb0"), (slot3(1, 512), "outb1")])
        L1.close()
        dump("x_mixed", x[:, 0:NC_P, :])
        dump("x_mixed_s", x[0:NS, NC_P, :])
        reuse_semaphores()
        experts(1)

        with ExitStack() as cx:
            gf = sb("g_final_rows", [P, D], where=cx)
            y = sb("y", [P, NCH, D], where=cx)
            ss = sb("final_ss", [P, NCH], where=cx)
            s_g, s_q, s_r, s_d, s_y, s_o = (sem(f"final_{m}") for m in ("gain", "squares", "root", "dve", "rows", "stored"))
            with nc.Block() as block:
                @block.sync
                def _(sp):
                    sp.dma_start(gf[:], I["g_final"].partition_broadcast(P)).then_inc(s_g, 16)
                    for c in range(NCH):
                        sp.wait_ge(s_y, c + 1)
                        if c < NC_P:
                            sp.dma_start(O["y_prompt"][0, c * P:(c + 1) * P, :], y[:, c, :]).then_inc(s_o, 16)
                        else:
                            sp.dma_start(O["y_sample"].rearrange("b t d -> (b t) d"), y[0:NS, c, :]).then_inc(s_o, 16)
                    sp.wait_ge(s_o, 16 * NCH)

                @block.scalar
                def _(act):
                    act.wait_ge(s_d, 1)
                    for c, r in enumerate(ROWS):
                        act.activation(y[:r, c, :], x[:r, c, :], ACT.Square, accum_out=ss[:r, c:c + 1]).then_inc(s_q, 1)
                    act.wait_ge(s_d, 2)
                    act.activation(ss[:], ss[:], ACT.Sqrt).then_inc(s_r, 1)

                @block.vector
                def _(dve):
                    d = Chain(dve, s_d)
                    d(V.memset(ss[:], 1.0))
                    dve.wait_ge(s_q, NCH)
                    d(V.tensor_scalar(ss[:], ss[:], 1.0 / D, EPS, ALU.mult, ALU.add))
                    dve.wait_ge(s_r, 1)
                    d(V.reciprocal(ss[:], ss[:]))
                    dve.wait_ge(s_g, 16)
                    for c, r in enumerate(ROWS):
                        V.scalar_tensor_tensor(y[:r, c, :], x[:r, c, :], ss[:r, c:c + 1], gf[:r, :], ALU.mult, ALU.mult).then_inc(s_y, 1)
        return debug_out


_INS = ["x_prompt", "x_sample", "mem_prompt", "state_delta", "cache_conv", "cache_kv_latent", "cache_k_rope",
        "cache_mem_k", "cache_mem_v", "page_table", "g_mix", "g_ffn", "g_final", "w_in_a", "conv_w", "a_log", "dt_bias",
        "g_onorm", "w_out_a", "g_kv_in", "w_dkv", "g_kv_latent", "w_uk", "w_uv", "w_in_b", "g_q", "w_uq", "w_out_b",
        "g_mem", "w_mem_k", "w_mem_v", "w_router_group", "b_router_group", "w_router_expert", "b_router_expert",
        "w_exp_gate", "w_exp_up", "w_exp_down"]
_OUTS = [("y_prompt", (1, SEQ, D)), ("y_sample", (DB, DS, D)), ("kv_latent_prompt", (1, SEQ, KL)), ("k_rope_prompt", (1, SEQ, RP)),
         ("kv_latent_sample", (DB, DS, KL)), ("k_rope_sample", (DB, DS, RP)), ("state_delta_prompt", (1, 1, DN_H, P, P)),
         ("cache_conv_prompt", (1, 1, 3, CONV_CH)), ("state_delta_sample", (1, DB, DN_H, P, P)),
         ("cache_conv_sample", (1, DB, 3, CONV_CH)), ("mem_k_prompt", (2, 1, MEM, MH, MHD)), ("mem_v_prompt", (2, 1, MEM, MH, MHD))]


def kernel(**inputs):
    import concourse.bacc as _bacc
    from concourse.bass_utils import run_bass_kernel_spmd as _run

    nc = _bacc.Bacc("TRN2", target_bir_lowering=False, num_devices=1)
    arrays, I, O = {}, {}, {}
    for name in _INS + ["consts"]:
        a = CONSTS if name == "consts" else np.ascontiguousarray(inputs[name])
        arrays[f"in_{name}"] = a
        I[name] = nc.dram_tensor(f"in_{name}", a.shape, mybir.dt.from_np(a.dtype), kind="ExternalInput").ap()
    for name, shape in _OUTS:
        O[name] = nc.dram_tensor(f"out_{name}", shape, F32, kind="ExternalOutput").ap()
    build(nc, I, O)
    r = _run(nc, [arrays], core_ids=[0])
    return tuple(r.results[0][f"out_{name}"] for name, _ in _OUTS)
```

```python
from contextlib import ExitStack

import numpy as np

import concourse.bass as bass
from concourse import mybir

P = 128
F32 = mybir.dt.float32
I32 = mybir.dt.int32
U32 = mybir.dt.uint32
ALU = mybir.AluOpType
ACT = mybir.ActivationFunctionType
AX = mybir.AxisListType.X

D = 1024
DJ = D // P
SEQ, DB, DS = 512, 8, 4
NS = DB * DS
T = SEQ + NS
NC_P = SEQ // P
NCH = NC_P + 1
DN_H = 6
CONV_W = 4
CONV_CH = 3 * DN_H * P
MEM, MH, MHD = 256, 4, 64
QL, KL, RP = 384, 256, 64
NE, NG, EPG, FF = 32, 4, 8, 256
SLOTS = 64
EPS = 1e-6
BIG = 1e30
PAST = 2048
PAGE = 128
NPG = PAST // PAGE
MLA_SCALE = (P + RP) ** -0.5
OVER = 2 * T // SLOTS
XS_ROWS = 2 * T + SLOTS

ROWS = [P] * NC_P + [NS]
LEVELS = [1, 2, 4, 8, 16, 32, 64]


def shape_constants():
    i, j = np.arange(P)[:, None], np.arange(P)[None, :]
    parts = {}
    parts["ident"] = (i == j)
    parts["upper"] = (i <= j)
    parts["lower_big"] = np.where(i > j, 0.0, BIG)
    parts["upper_neg"] = np.where(i <= j, 0.0, -BIG)
    parts["ones"] = np.ones((P, P))
    for s in LEVELS:
        parts[f"level{s}"] = ((i // s) % 2 == 1) & (j // s == i // s - 1)
    parts["level1T"] = (((i // 1) % 2 == 1) & (j // 1 == i // 1 - 1)).T
    same = (i // DS == j // DS) & (i < NS) & (j < NS)
    parts["upper_s"] = ((i <= j) & same)[:, :NS]
    parts["lower_s"] = ((i > j) & same)[:, :NS]
    parts["same_s"] = same[:, :NS]
    b, t = np.arange(DB)[None, :, None], np.arange(NS)[None, None, :]
    parts["row_of"] = np.broadcast_to(t // DS == b, (P, DB, NS)).reshape(P, -1)
    parts["col_of"] = (np.arange(P)[:, None] // DS == np.arange(DB)[None, :])
    pos = np.concatenate([np.arange(SEQ), np.tile(PAST + np.arange(DS), DB)]).astype(np.float32)
    inv = (np.float32(10000.0) ** (-np.arange(0, RP, 2, dtype=np.float32) / np.float32(RP))).astype(np.float32)
    ang = pos[:, None] * inv[None, :]
    for name, f in (("cos", np.cos), ("sin", np.sin)):
        a = np.zeros((NCH * P, RP // 2), np.float32)
        a[:T] = f(ang)
        parts[name] = a.reshape(NCH, P, RP // 2).transpose(1, 0, 2).reshape(P, -1)
    parts["experts"] = np.broadcast_to(np.arange(NE)[None, :], (P, NE))
    parts["rows"] = np.arange(P)[:, None]
    parts["over_shift"] = SLOTS * (np.arange(P)[:, None] + 1)
    parts["first_of_4"] = np.broadcast_to(NG - np.arange(NG)[None, :], (P, NG))
    parts["first_of_32"] = np.broadcast_to(NE - np.arange(NE)[None, :], (P, NE))
    hq = np.arange(P)[:, None, None] % DS
    bb, tt = np.arange(DB)[None, :, None], np.arange(NS)[None, None, :]
    parts["new_keys"] = np.where((tt // DS == bb) & (tt % DS <= hq), 0.0, -BIG).reshape(P, -1)
    parts["same_row"] = (i % 32 == j % 32)
    parts["eighth"] = np.arange(P)[:, None] % 8
    parts["causal"] = np.where(j <= i, 0.0, -BIG)
    at, cols = {}, 0
    for n, a in parts.items():
        at[n] = (cols, a.shape[1])
        cols += a.shape[1]
    return at, np.ascontiguousarray(np.concatenate([np.asarray(a, np.float32) for a in parts.values()], 1))


CONST_AT, CONSTS = shape_constants()


class Chain:

    def __init__(self, eng, sem):
        self.eng, self.sem, self.n = eng, sem, 0

    def __call__(self, ins):
        ins.then_inc(self.sem, 1)
        self.n += 1
        self.eng.wait_ge(self.sem, self.n)


def wait_after(eng, sem, value):
    if value > 0:
        eng.wait_ge(sem, value)


def build(nc, I, O, debug=()):
    ctx = ExitStack()
    with ctx:
        def sb(name, shape, dt=F32, where=ctx):
            return where.enter_context(nc.sbuf_tensor(name, shape, dt))

        stage_sems = []

        def sem(name):
            s = nc.alloc_semaphore(name=name)
            stage_sems.append(s)
            return s

        def reuse_semaphores():
            nc.clear_and_free_semaphores(stage_sems)
            nc.all_engine_barrier()
            stage_sems.clear()

        pp = [ctx.enter_context(nc.psum_tensor(f"pp{i}", [P, 1024], F32)) for i in range(4)]
        V, S, TE, G = nc.vector, nc.scalar, nc.tensor, nc.gpsimd

        consts = sb("consts", [P, CONSTS.shape[1]])

        def const(name):
            at, n = CONST_AT[name]
            return consts[:, at:at + n]

        ident, ones = const("ident"), const("ones")

        def bc(ap, axis, n):
            a = ap.unsqueeze(axis)
            shape = list(a.shape)
            shape[axis] = n
            return a.to_broadcast(shape)

        x = sb("x", [P, NCH, D])
        uT = sb("uT", [P, DJ, T])
        ring = [sb(f"ring{i}", [P, 6144]) for i in range(2)]
        gains = sb("gains", [P, 7, DJ])
        G_MIX, G_FFN, G_KV, G_MEM = 0, 2, 4, 5
        mem_kT = sb("mem_kT", [P, 2, 2, MEM])
        mem_v = sb("mem_v", [P, 2, 2, MEM])
        small = sb("small", [P, 12 + 36 * 2])
        landed = {}

        s_ring = [sem(f"ring{i}_landed") for i in range(2)]
        ring_count = [0, 0]
        stage_sems.clear()

        def load(eng, slot, name, *pairs):
            for dst, src in pairs:
                eng.dma_start(dst, src).then_inc(s_ring[slot], 16)
                ring_count[slot] += 16
            landed[name] = (s_ring[slot], ring_count[slot])

        def arrived(eng, name):
            eng.wait_ge(*landed[name])

        def pj(ap):
            return ap.rearrange("(p j) n -> p j n", p=P)

        def slot3(slot, n, j=DJ):
            return ring[slot][:, 0:j * n].rearrange("p (j n) -> p j n", j=j)

        def offset(c):
            return c * P

        HALVES = ((slice(0, T // 2), slice(0, T // 2)), (slice(T // 2, T), slice(512, 512 + T // 2)))

        def halves(q):
            return q[:].rearrange("p (b t) -> p b t", b=2)[:, :, 0:T // 2]

        def sample_parts(out, lhs, parts):
            for j in range(DJ):
                for q, rhs in enumerate(parts):
                    w = rhs(j)
                    ins = TE.matmul(out[NS * q:NS * (q + 1), 0:w.shape[-1]], lhs[:, j, SEQ:T], w, start=(j == 0), stop=(j == DJ - 1))
            return ins

        def all_tokens(ap):
            return ap.rearrange("p (b t) -> p b t", b=2)

        debug_out = {}

        def dump(name, ap):
            if name in debug:
                d = nc.dram_tensor(f"dbg_{name}", tuple(ap.shape), F32, kind="ExternalOutput").ap()
                debug_out[name] = d
                s_dbg = sem(f"dbg_{name}")
                with nc.Block() as block:
                    @block.sync
                    def _(sp):
                        sp.dma_start(d, ap).then_inc(s_dbg, 16)
                        sp.wait_ge(s_dbg, 16)

        class Norm:

            def __init__(self, tag, src, rows, gain_to, where, kept_rows=None, sums=None):
                self.src, self.rows, self.gain_to = src, rows, gain_to
                n = len(rows)
                self.nb = 2 if kept_rows is None else n
                self.given = sums is not None
                if not self.given:
                    self.junk = sb(f"{tag}_junk", [P, 2, D], where=where)
                self.xn = sb(f"{tag}_xn", [P, 2, D], where=where) if kept_rows is None else kept_rows
                self.ss = sums if self.given else sb(f"{tag}_ss", [P, n], where=where)
                self.squares, self.dve, self.root, self.scaled, self.turned, self.kept = (
                    sem(f"{tag}_{m}") for m in ("squares", "dve", "root", "scaled", "turned", "kept"))

            def act_part(self, act):
                act.wait_ge(self.dve, 1)
                if not self.given:
                    for c, r in enumerate(self.rows):
                        if c >= 2:
                            act.wait_ge(self.squares, c - 1)
                        S.activation(self.junk[:r, c % 2, :], self.src[:r, c, :], ACT.Square, accum_out=self.ss[:r, c:c + 1]).then_inc(self.squares, 1)
                    act.wait_ge(self.dve, 2)
                S.activation(self.ss[:], self.ss[:], ACT.Sqrt).then_inc(self.root, 1)

            def clear(self, dve):
                self.chain = Chain(dve, self.dve)
                if not self.given:
                    self.chain(V.memset(self.ss[:], 1.0))

            def factors(self, dve):
                if not self.given:
                    dve.wait_ge(self.squares, len(self.rows))
                self.chain(V.tensor_scalar(self.ss[:], self.ss[:], 1.0 / D, EPS, ALU.mult, ALU.add))
                dve.wait_ge(self.root, 1)
                self.chain(V.reciprocal(self.ss[:], self.ss[:]))

            def scale(self, dve, c):
                r = self.rows[c]
                if c >= self.nb:
                    dve.wait_ge(self.turned, c - self.nb + 1)
                V.tensor_scalar(self.xn[:r, c % self.nb, :], self.src[:r, c, :], self.ss[:r, c:c + 1], None, ALU.mult).then_inc(self.scaled, 1)

            def keep(self, dve, c):
                r = self.rows[c]
                dve.wait_ge(self.turned, c + 1)
                for g, dst in self.gain_to:
                    V.tensor_tensor(dst[:, :, offset(c):offset(c) + r], pp[c % 2][:].rearrange("p (j t) -> p j t", j=DJ)[:, :, :r],
                                    bc(gains[:, g, :], 2, r), ALU.mult).then_inc(self.kept, 1)

            def turn(self, pe, c):
                r = self.rows[c]
                pe.wait_ge(self.scaled, c + 1)
                if c >= 2:
                    pe.wait_ge(self.kept, len(self.gain_to) * (c - 1))
                xv = self.xn[:r, c % self.nb, :].rearrange("t (p j) -> t j p", j=DJ)
                for j in range(DJ):
                    ins = TE.transpose(pp[c % 2][:, j * P:j * P + r], xv[:, j, :], ident[:r, :r])
                ins.then_inc(self.turned, 1)

        def norm_transposed(tag, src, rows, gain_to, sync_extra=None, kept_rows=None, on_chunk=None, sums=None):
            n = len(rows)
            with ExitStack() as cx:
                norm = Norm(tag, src, rows, gain_to, cx, kept_rows, sums)
                with nc.Block() as block:
                    if sync_extra:
                        block.sync(sync_extra)

                    @block.scalar
                    def _(act):
                        norm.act_part(act)

                    @block.vector
                    def _(dve):
                        norm.clear(dve)
                        norm.factors(dve)
                        for c in range(n):
                            norm.scale(dve, c)
                            if c >= 1:
                                norm.keep(dve, c - 1)
                        norm.keep(dve, n - 1)

                    @block.tensor
                    def _(pe):
                        for c in range(n):
                            norm.turn(pe, c)
                            if on_chunk and c >= 1:
                                pe.wait_ge(norm.kept, len(gain_to) * c)
                                on_chunk(c - 1)
                        if on_chunk:
                            pe.wait_ge(norm.kept, len(gain_to) * n)
                            on_chunk(n - 1)

        xs = nc.dram_tensor("sorted_rows", (XS_ROWS, D), F32, kind="Internal").ap()
        ys = nc.dram_tensor("expert_rows", ((NE + OVER) * SLOTS, D), F32, kind="Internal").ap()
        over_rows = nc.dram_tensor("over_table", (P, 2), I32, kind="Internal").ap()

        NR3 = 3 * (NG + NE)
        w_rt = sb("router_weights", [P, DJ, 3, NG + NE])
        conv_wT = sb("conv_wT", [P, CONV_W * 18])
        g_on = sb("g_on", [P, P])
        x_sums = sb("x_sums", [P, NCH])
        mem_x = ctx.enter_context(ExitStack())
        mx = sb("mem_x", [P, 2, D], where=mem_x)
        mT = sb("mem_T", [P, 2, DJ, MEM], where=mem_x)
        conv_rows = sb("conv_rows", [CONV_W * 18, P], where=mem_x)

        w_in = pj(I["w_in_a"][0])
        Z0 = CONV_CH
        R0 = Z0 + DN_H * P
        NR = 2 * DN_H + MH * MHD
        norm_m = Norm("memn", mx, [P, P], [(G_MEM, mT[:, 0]), (G_MEM + 1, mT[:, 1])], mem_x)
        norm_x = Norm("norm0", x, ROWS, [(G_MIX, uT)], mem_x)
        kv = sb("mem_kv_rows", [P, 4, 2 * MEM], where=mem_x)
        s_memx, s_consts, s_x, s_rest = (sem(f"landed_{m}") for m in ("memory", "constants", "x", "rest"))
        s_mm, s_ev, s_tr, s_k, s_st, s_k0 = (sem(f"memkv_{m}") for m in ("product", "kept", "turned", "keys", "stored", "router_zeros"))

        with nc.Block() as block:
            @block.sync
            def _(sp):
                def into(s, *pairs):
                    for dst, src in pairs:
                        sp.dma_start(dst, src).then_inc(s, 16)

                def mem_weights(l):
                    w = slot3(l, 2 * MEM)
                    load(sp, l, f"mem{l}", (w[:, :, 0:MEM], pj(I["w_mem_k"][l])), (w[:, :, MEM:2 * MEM], pj(I["w_mem_v"][l])))

                into(s_memx, (mx[:], I["mem_prompt"][0].rearrange("(c p) d -> p c d", p=P)))
                into(s_consts, (consts[:], I["consts"]))
                into(s_consts, *((gains[:, k, :], ap.rearrange("(p j) -> p j", p=P)) for k, ap in (
                    (G_MEM, I["g_mem"][0]), (G_MEM + 1, I["g_mem"][1]), (G_MIX, I["g_mix"][0]))))
                mem_weights(0)
                into(s_x, (x[:, 0:NC_P, :], I["x_prompt"][0].rearrange("(c p) d -> p c d", p=P)),
                     (x[0:NS, NC_P, :], I["x_sample"].rearrange("b s d -> (b s) d")))
                mem_weights(1)
                into(s_rest, (conv_rows[:], I["conv_w"][0].rearrange("w (c p) -> (w c) p", p=P)),
                     (g_on[:], I["g_onorm"][0].partition_broadcast(P)),
                     (small[:, 0:6], I["a_log"][0].partition_broadcast(P)),
                     (small[:, 6:12], I["dt_bias"][0].partition_broadcast(P)))
                into(s_rest, *((gains[:, k, :], ap.rearrange("(p j) -> p j", p=P)) for k, ap in (
                    (G_MIX + 1, I["g_mix"][1]), (G_FFN, I["g_ffn"][0]), (G_FFN + 1, I["g_ffn"][1]), (G_KV, I["g_kv_in"]))))
                for l in range(2):
                    into(s_rest, (small[:, 12 + 36 * l:16 + 36 * l], I["b_router_group"][l].partition_broadcast(P)),
                         (small[:, 16 + 36 * l:48 + 36 * l], I["b_router_expert"][l].partition_broadcast(P)),
                         (w_rt[:, :, l, 0:NG], pj(I["w_router_group"][l])), (w_rt[:, :, l, NG:], pj(I["w_router_expert"][l])))
                for l, name in enumerate("qk"):
                    sp.wait_ge(s_mm, 2 * (l + 1))
                    load(sp, l, name, (slot3(l, 768), w_in[:, :, l * 768:(l + 1) * 768]))
                for n in range(4):
                    l, m = divmod(n, 2)
                    sp.wait_ge(s_ev, n + 1)
                    for k, o in ((0, "mem_k_prompt"), (1, "mem_v_prompt")):
                        sp.dma_start(O[o][l, 0].rearrange("m h d -> m (h d)")[m * P:(m + 1) * P, :],
                                     kv[:, n, k * MEM:(k + 1) * MEM]).then_inc(s_st, 16)
                sp.wait_ge(s_st, 16 * 8)
                sp.wait_ge(s_rest, 16 * 16)

            @block.tensor
            def _(pe):
                def mem_product(n):
                    l, m = divmod(n, 2)
                    if m == 0:
                        arrived(pe, f"mem{l}")
                    if n >= 2:
                        pe.wait_ge(s_ev, n - 1)
                    w = slot3(l, 2 * MEM)
                    for j in range(DJ):
                        ins = TE.matmul(pp[2 + n % 2][:, 0:512], mT[:, l, j, m * P:(m + 1) * P], w[:, j, :], start=(j == 0), stop=(j == DJ - 1))
                    ins.then_inc(s_mm, 1)

                def turn_keys(n):
                    pe.wait_ge(s_ev, n + 1)
                    if n >= 2:
                        pe.wait_ge(s_k, 2 * (n - 1))
                    for pr in range(2):
                        ins = TE.transpose(pp[2 + n % 2][:, 512 + pr * P:512 + (pr + 1) * P], kv[:, n, pr * P:(pr + 1) * P], ident)
                    ins.then_inc(s_tr, 1)

                pe.wait_ge(s_consts, 64)
                norm_m.turn(pe, 0)
                norm_m.turn(pe, 1)
                pe.wait_ge(norm_m.kept, 4)
                mem_product(0)
                mem_product(1)
                turn_keys(0)
                norm_x.turn(pe, 0)
                mem_product(2)
                turn_keys(1)
                norm_x.turn(pe, 1)
                norm_x.turn(pe, 2)
                mem_product(3)
                turn_keys(2)
                norm_x.turn(pe, 3)
                turn_keys(3)
                pe.wait_ge(s_rest, 16 * 16)
                pe.wait_ge(s_k, 6)
                TE.transpose(pp[2][:, 0:72], conv_rows[:], ident[0:72, 0:72]).then_inc(s_tr, 1)
                norm_x.turn(pe, 4)

            @block.scalar
            def _(act):
                act.wait_ge(s_memx, 16)
                norm_m.act_part(act)
                act.wait_ge(s_x, 32)
                norm_x.act_part(act)
                for n in range(4):
                    act.wait_ge(s_mm, n + 1)
                    S.activation(kv[:, n, :], pp[2 + n % 2][:, 0:512], ACT.Copy).then_inc(s_ev, 1)

            @block.vector
            def _(dve):
                def keep_memory(n):
                    l, m = divmod(n, 2)
                    dve.wait_ge(s_tr, n + 1)
                    V.tensor_copy(mem_kT[:, l, :, m * P:(m + 1) * P], pp[2 + n % 2][:, 512:512 + MEM].rearrange("p (a m) -> p a m", a=2)).then_inc(s_k, 1)
                    V.tensor_copy(mem_v[:, l, m, :], kv[:, n, MEM:2 * MEM]).then_inc(s_k, 1)

                V.memset(w_rt[:, :, 2, :], 0.0).then_inc(s_k0, 1)
                norm_m.clear(dve)
                norm_x.clear(dve)
                dve.wait_ge(s_memx, 16)
                norm_m.factors(dve)
                norm_m.scale(dve, 0)
                norm_m.scale(dve, 1)
                dve.wait_ge(s_consts, 64)
                norm_m.keep(dve, 0)
                norm_m.keep(dve, 1)
                dve.wait_ge(s_x, 32)
                norm_x.factors(dve)
                norm_x.scale(dve, 0)
                norm_x.scale(dve, 1)
                keep_memory(0)
                norm_x.keep(dve, 0)
                norm_x.scale(dve, 2)
                keep_memory(1)
                norm_x.keep(dve, 1)
                norm_x.scale(dve, 3)
                norm_x.keep(dve, 2)
                norm_x.scale(dve, 4)
                keep_memory(2)
                norm_x.keep(dve, 3)
                keep_memory(3)
                dve.wait_ge(s_tr, 5)
                V.tensor_copy(conv_wT[:], pp[2][:, 0:72]).then_inc(s_k, 1)
                norm_x.keep(dve, 4)
        mem_x.close()

        L0 = ctx.enter_context(ExitStack())
        toks = sb("qkv_rows", [P, 3, NCH, 768], where=L0)
        tok = [toks[:, g] for g in range(3)]
        zs = sb("z_rows", [P, NCH, 768], where=L0)
        ab = sb("ab", [P, NCH, 12], where=L0)
        qmT = sb("qmT", [P, 2, T], where=L0)
        ss = sb("l2", [P, 2, NCH, DN_H], where=L0)
        IN = ctx.enter_context(ExitStack())
        CW = 3 + SEQ + DB * (3 + DS)
        CN = CW - 3
        raw = sb("conv_in", [P, 2, CW], where=IN)
        yc = sb("conv_sum", [P, 2, CW], where=IN)
        ya = sb("conv_out", [P, 2, T], where=IN)
        crow = sb("conv_tail", [P, 2, 27], where=IN)
        cache_in = sb("cache_rows", [24, CONV_CH], where=IN)
        cache_out = sb("cache_out_rows", [27, CONV_CH], where=IN)
        zero = sb("zero_rows", [SLOTS, D // 2], where=IN)
        squares = sb("squares", [P, P], where=IN)
        w_out = I["w_out_a"][0].rearrange("(j p) n -> p j n", p=P)
        NT = 18
        with nc.Block() as block:
            s_c, s_mm, s_raw, s_ch, s_sum, s_silu, s_tail, s_tr, s_tok, s_free, s_z, s_zk, s_st, s_zero, s_zrow, s_sq = (
                sem(f"in_{m}") for m in ("cache", "product", "raw", "chain", "summed", "silu", "tail", "turned", "rows", "slot_free", "z", "z_kept", "stored", "zeroed", "zero_row", "squares"))

            @block.sync
            def _(sp):
                sp.dma_start(cache_in[:], I["cache_conv"][0].rearrange("b r c -> (b r) c")).then_inc(s_c, 16)
                sp.wait_ge(s_zrow, 1)
                sp.dma_start(xs[2 * T:XS_ROWS, :].rearrange("s (q d) -> s q d", q=2), bc(zero[:], 1, 2)).then_inc(s_st, 16)
                for q in range(2):
                    sp.dma_start(ys[NE * SLOTS:, q * 512:(q + 1) * 512].rearrange("(j s) d -> s j d", s=SLOTS), bc(zero[:], 1, OVER)).then_inc(s_st, 16)
                for n, (slot, name, a, b) in enumerate((((0, "v", 1536, Z0)), (1, "z", Z0, R0), (0, "rest", R0, R0 + NR))):
                    sp.wait_ge(s_free, n + 1)
                    load(sp, slot, name, (slot3(slot, b - a), w_in[:, :, a:b]))
                for n, slot in ((0, 1), (1, 0)):
                    sp.wait_ge(s_free, 4 + n)
                    load(sp, slot, f"out{n}", (slot3(slot, 512), w_out[:, :, n * 512:(n + 1) * 512]))
                sp.wait_ge(s_tok, NT)
                sp.dma_start(O["cache_conv_prompt"][0, 0], cache_out[0:3, :]).then_inc(s_st, 16)
                sp.dma_start(O["cache_conv_sample"][0].rearrange("b r c -> (b r) c"), cache_out[3:27, :]).then_inc(s_st, 16)
                sp.wait_ge(s_st, 80)

            @block.gpsimd
            def _(pool):
                G.memset(zero[:], 0.0).then_inc(s_zrow, 1)

            @block.tensor
            def _(pe):
                def turn(n):
                    pe.wait_ge(s_silu, 2 * (n + 1))
                    pe.wait_ge(s_tail, n + 1)
                    if n >= 2:
                        pe.wait_ge(s_tok, n - 1)
                    for c in range(NC_P):
                        TE.transpose(pp[2 + n % 2][:, c * P:(c + 1) * P], ya[:, n % 2, c * P:(c + 1) * P], ident)
                    TE.transpose(pp[2 + n % 2][0:NS, 512:640], ya[:, n % 2, SEQ:T], ident)
                    TE.transpose(pp[2 + n % 2][0:27, 640:768], crow[:, n % 2, :], ident).then_inc(s_tr, 1)

                for n in range(NT):
                    g, ct = divmod(n, 6)
                    if ct == 0:
                        arrived(pe, "qkv"[g])
                    w = slot3(g % 2, 768)
                    if n >= 2:
                        pe.wait_ge(s_raw, n - 1)
                    for t, at in HALVES:
                        for j in range(DJ):
                            TE.matmul(pp[n % 2][:, at], w[:, j, ct * P:(ct + 1) * P], uT[:, j, t], start=(j == 0), stop=(j == DJ - 1))
                    if n == 0:
                        pe.wait_ge(s_c, 16)
                    TE.transpose(pp[n % 2][:, 784:808], cache_in[:, n * P:(n + 1) * P], ident[0:24, 0:24]).then_inc(s_mm, 1)
                    if n >= 1:
                        turn(n - 1)
                    if ct == 5:
                        pe.wait_ge(s_mm, n + 1)
                        pe.sem_inc(s_free, 1)
                turn(NT - 1)
                arrived(pe, "z")
                w = slot3(1, 768)
                pe.wait_ge(s_raw, NT)
                for c, r in enumerate(ROWS):
                    if c >= 2:
                        pe.wait_ge(s_zk, 2 * (c - 1))
                    if c < NC_P:
                        for o, k in ((0, 512), (512, 256)):
                            for j in range(DJ):
                                ins = TE.matmul(pp[c % 2][:r, o:o + k], uT[:, j, offset(c):offset(c) + r], w[:, j, o:o + k], start=(j == 0), stop=(j == DJ - 1))
                    else:
                        ins = sample_parts(pp[c % 2], uT, [lambda j, q=q: w[:, j, q * 192:(q + 1) * 192] for q in range(4)])
                    ins.then_inc(s_z, 1)
                pe.wait_ge(s_z, NCH)
                pe.sem_inc(s_free, 1)
                arrived(pe, "rest")
                w = slot3(0, NR)
                pe.wait_ge(s_tok, NT)
                for c, r in enumerate(ROWS):
                    for j in range(DJ):
                        ins = TE.matmul(pp[2][:r, c * 12:(c + 1) * 12], uT[:, j, offset(c):offset(c) + r], w[:, j, 0:12], start=(j == 0), stop=(j == DJ - 1))
                ins.then_inc(s_z, 1)
                for pr in range(2):
                    pe.wait_ge(s_zk, 2 * (NC_P + pr))
                    for t, at in HALVES:
                        for j in range(DJ):
                            ins = TE.matmul(pp[1 - pr][:, at], w[:, j, 12 + pr * P:12 + (pr + 1) * P], uT[:, j, t], start=(j == 0), stop=(j == DJ - 1))
                    ins.then_inc(s_z, 1)
                pe.wait_ge(s_z, NCH + 3)
                pe.sem_inc(s_free, 1)

            @block.vector
            def _(dve):
                chain = Chain(dve, s_ch)
                for t in (*tok, zs, ab):
                    V.memset(t[:, NC_P, :], 0.0).then_inc(s_zero, 1)
                chain(V.memset(raw[:, :, 0:3], 0.0))
                for n in range(NT):
                    k = n % 2
                    dve.wait_ge(s_mm, n + 1)
                    if n >= 2:
                        dve.wait_ge(s_tail, n - 1)
                        dve.wait_ge(s_silu, 2 * (n - 1))
                    sv = raw[:, k, 3 + SEQ:CW].rearrange("p (b r) -> p b r", b=DB)
                    chain(V.tensor_copy(raw[:, k, 3:3 + T // 2], pp[k][:, 0:T // 2]))
                    chain(V.tensor_copy(raw[:, k, 3 + T // 2:3 + SEQ], pp[k][:, 512:784 - NS]))
                    chain(V.tensor_copy(sv[:, :, 3:7], pp[k][:, 784 - NS:784].rearrange("p (b r) -> p b r", b=DB)))
                    ins = V.tensor_copy(sv[:, :, 0:3], pp[k][:, 784:808].rearrange("p (b r) -> p b r", b=DB))
                    chain(ins)
                    dve.sem_inc(s_raw, 1)
                    for j in range(CONV_W):
                        wj = conv_wT[:, j * 18 + n:j * 18 + n + 1]
                        if j == 0:
                            chain(V.tensor_scalar(yc[:, k, 0:CN], raw[:, k, 0:CN], wj, None, ALU.mult))
                        elif j < CONV_W - 1:
                            chain(V.scalar_tensor_tensor(yc[:, k, 0:CN], raw[:, k, j:j + CN], wj, yc[:, k, 0:CN], ALU.mult, ALU.add))
                        else:
                            V.scalar_tensor_tensor(yc[:, k, 0:CN], raw[:, k, j:j + CN], wj, yc[:, k, 0:CN], ALU.mult, ALU.add).then_inc(s_sum, 1)
                    if n >= 2:
                        dve.wait_ge(s_tr, n - 1)
                    chain(V.tensor_copy(crow[:, k, 0:3], raw[:, k, SEQ:SEQ + 3]))
                    V.tensor_copy(crow[:, k, 3:27].rearrange("p (b r) -> p b r", b=DB), sv[:, :, 4:7]).then_inc(s_tail, 1)
                dve.wait_ge(s_z, NCH + 1)
                dve.wait_ge(s_zero, 5)
                chain(V.tensor_copy(ab[:, 0:NC_P, :], pp[2][:, 0:12 * NC_P].rearrange("p (c k) -> p c k", c=NC_P)))
                chain(V.tensor_copy(ab[0:NS, NC_P, :], pp[2][0:NS, 12 * NC_P:12 * NCH]))
                for pr in range(2):
                    dve.wait_ge(s_z, NCH + 2 + pr)
                    chain(V.tensor_copy(all_tokens(qmT[:, pr, :]), halves(pp[1 - pr])))

            @block.scalar
            def _(act):
                act.wait_ge(s_zero, 5)

                def rows(n):
                    g, ct = divmod(n, 6)
                    act.wait_ge(s_tr, n + 1)
                    q = pp[2 + n % 2]
                    S.activation(tok[g][:, 0:NC_P, ct * P:(ct + 1) * P], q[:, 0:512].rearrange("p (c t) -> p c t", c=NC_P), ACT.Copy)
                    S.activation(tok[g][0:NS, NC_P, ct * P:(ct + 1) * P], q[0:NS, 512:640], ACT.Copy)
                    S.activation(cache_out[:, n * P:(n + 1) * P], q[0:27, 640:768], ACT.Copy).then_inc(s_tok, 1)
                    if g < 2:
                        act.wait_ge(s_tok, n + 1)
                        for c in range(NCH):
                            i = (n * NCH + c)
                            if i >= 1:
                                act.wait_ge(s_sq, i)
                            S.activation(squares[:], tok[g][:, c, ct * P:(ct + 1) * P], ACT.Square, accum_out=ss[:, g, c, ct:ct + 1]).then_inc(s_sq, 1)

                for n in range(NT):
                    k = n % 2
                    act.wait_ge(s_sum, n + 1)
                    if n >= 2:
                        act.wait_ge(s_tr, n - 1)
                    S.activation(ya[:, k, 0:SEQ], yc[:, k, 0:SEQ], ACT.Silu).then_inc(s_silu, 1)
                    S.activation(ya[:, k, SEQ:T].rearrange("p (b r) -> p b r", b=DB),
                                 yc[:, k, 3 + SEQ:CW].rearrange("p (b r) -> p b r", b=DB)[:, :, 0:DS], ACT.Silu).then_inc(s_silu, 1)
                    if n >= 1:
                        rows(n - 1)
                rows(NT - 1)
                for c, r in enumerate(ROWS):
                    act.wait_ge(s_z, c + 1)
                    if c < NC_P:
                        S.activation(zs[:r, c, 0:512], pp[c % 2][:r, 0:512], ACT.Silu).then_inc(s_zk, 1)
                        S.activation(zs[:r, c, 512:768], pp[c % 2][:r, 512:768], ACT.Silu).then_inc(s_zk, 1)
                    else:
                        for q in range(4):
                            ins = S.activation(zs[:r, c, q * 192:(q + 1) * 192], pp[c % 2][NS * q:NS * (q + 1), 0:192], ACT.Silu)
                        ins.then_inc(s_zk, 2)
        IN.close()
        dump("q_rows", tok[0][:])
        dump("v_rows", tok[2][:])
        dump("z_rows", zs[:])
        dump("ab", ab[:])
        dump("qmT", qmT[:])

        x_flat = x[:].rearrange("p c d -> p (c d)")
        uT_flat = uT[:].rearrange("p j t -> p (j t)")
        sx = L0
        qkT = sb("qkT", [P, 12, T], where=L0)
        gb = sb("decays", [P, 8, NCH, DN_H], where=L0)
        g_, G_, tot, eG, ekd, dec, beta, beG = (gb[:, k] for k in range(8))
        dS = sb("decay_s", [P, DB, DN_H], where=L0)
        with ExitStack() as cx:
            gm = sb("g_masked", [NS, DB, DN_H], where=cx)
            t1 = sb("softplus", [P, 3, NCH, DN_H], where=cx)
            ea = sb("exp_a", [P, DN_H], where=cx)
            s_a, s_d, s_t, s_k, s_g, s_n = (sem(f"prep_{m}") for m in ("act", "dve", "turned", "kept", "sums", "scaled"))
            with nc.Block() as block:
                @block.scalar
                def _(act):
                    a = Chain(act, s_a)
                    act.wait_ge(s_d, 1)
                    a(S.activation(ss[:], ss[:], ACT.Sqrt))
                    act.wait_ge(s_d, 5)
                    a(S.activation(t1[:, 1], t1[:, 0], ACT.Abs))
                    a(S.activation(t1[:, 1], t1[:, 1], ACT.Exp, scale=-1.0))
                    a(S.activation(ea[:], small[:, 0:6], ACT.Exp))
                    a(S.activation(t1[:, 1], t1[:, 1], ACT.Ln, bias=1.0))
                    a(S.activation(beta, ab[:, :, 6:12], ACT.Sigmoid))
                    for n in range(12):
                        act.wait_ge(s_t, n + 1)
                        S.activation(qkT[:, n, 0:SEQ], pp[n % 2][:, 0:SEQ], ACT.Copy)
                        S.activation(qkT[:, n, SEQ:T], pp[n % 2][:, 512:512 + NS], ACT.Copy).then_inc(s_k, 1)
                    act.wait_ge(s_g, 2)
                    act.wait_ge(s_d, 14)
                    a(S.activation(eG, G_, ACT.Exp))
                    a(S.activation(ekd, ekd, ACT.Exp))
                    a(S.activation(dec, tot, ACT.Exp))
                    a(S.activation(dS[:], dS[:], ACT.Exp))

                @block.vector
                def _(dve):
                    d = Chain(dve, s_d)
                    d(V.tensor_scalar(ss[:], ss[:], EPS, None, ALU.add))
                    dve.wait_ge(s_a, 1)
                    d(V.reciprocal(ss[:], ss[:]))
                    d(V.tensor_scalar(ss[:, 0], ss[:, 0], P ** -0.5, None, ALU.mult))
                    d(V.tensor_tensor(t1[:, 0], ab[:, :, 0:6], bc(small[:, 6:12], 1, NCH), ALU.add))
                    d(V.tensor_scalar(t1[:, 2], t1[:, 0], 0.0, None, ALU.max))
                    for n in range(12):
                        k, h = divmod(n, 6)
                        v = tok[k][:, :, h * P:(h + 1) * P]
                        V.tensor_tensor(v, v, bc(ss[:, k, :, h], 2, P), ALU.mult).then_inc(s_n, 1)
                    dve.wait_ge(s_a, 6)
                    d(V.tensor_tensor(g_, t1[:, 1], t1[:, 2], ALU.add))
                    d(V.tensor_tensor(g_, g_, bc(ea[:], 1, NCH), ALU.mult))
                    d(V.tensor_scalar(g_, g_, -1.0, None, ALU.mult))
                    d(V.tensor_tensor(gm[:], bc(g_[0:NS, NC_P, :], 1, DB), bc(const("col_of")[0:NS, :], 2, DN_H), ALU.mult))
                    d(V.memset(gb[:, 1:3], 0.0))
                    dve.wait_ge(s_g, 1)
                    for k, o in ((G_, 0), (tot, 32)):
                        V.tensor_copy(k[:, 0:NC_P, :], pp[2][:, o:o + 24].rearrange("p (c h) -> p c h", h=DN_H))
                        d(V.tensor_copy(k[0:NS, NC_P, :], pp[2][0:NS, o + 24:o + 30]))
                    d(V.tensor_copy(dS[:], pp[2][:, 64:112].rearrange("p (b h) -> p b h", h=DN_H)))
                    d(V.tensor_tensor(ekd, tot, G_, ALU.subtract))
                    dve.wait_ge(s_a, 7)
                    d(V.tensor_tensor(beG, beta, eG, ALU.mult))

                @block.tensor
                def _(pe):
                    for n in range(12):
                        k, ct = divmod(n, 6)
                        pe.wait_ge(s_n, n + 1)
                        if n >= 2:
                            pe.wait_ge(s_k, n - 1)
                        for c in range(NC_P):
                            TE.transpose(pp[n % 2][:, c * P:(c + 1) * P], tok[k][:, c, ct * P:(ct + 1) * P], ident)
                        TE.transpose(pp[n % 2][:, 512:512 + NS], tok[k][0:NS, NC_P, ct * P:(ct + 1) * P], ident[0:NS, 0:NS]).then_inc(s_t, 1)
                    pe.wait_ge(s_d, 10)
                    for c in range(NC_P):
                        TE.matmul(pp[2][:, c * 6:c * 6 + 6], const("upper"), g_[:, c, :], start=True, stop=True)
                        TE.matmul(pp[2][:, 32 + c * 6:38 + c * 6], ones, g_[:, c, :], start=True, stop=True)
                    TE.matmul(pp[2][0:NS, 24:30], const("upper_s")[0:NS, :], g_[0:NS, NC_P, :], start=True, stop=True)
                    TE.matmul(pp[2][0:NS, 56:62], const("same_s")[0:NS, :], g_[0:NS, NC_P, :], start=True, stop=True)
                    TE.matmul(pp[2][:, 64:112], ones[0:NS, :], gm[:].rearrange("p b h -> p (b h)"), start=True, stop=True).then_inc(s_g, 2)

                @block.gpsimd
                def _(pool):
                    zv = zs[:].rearrange("p c (h d) -> p (c h) d", d=P)
                    G.tensor_tensor(zv, zv, bc(g_on[:], 1, NCH * DN_H), ALU.mult)

        state = sb("state", [P, DN_H, P], where=L0)
        gs = sb("o_squares", [P, NCH, DN_H], where=L0)
        DL = ctx.enter_context(ExitStack())
        o_junk = sb("o_junk", [P, P], where=DL)
        s_sq, s_gs = sem("o_squares"), sem("o_squares_set")
        A, GT, AT, X, XT, Y = (x_flat[:, n * 768:(n + 1) * 768].rearrange("p (h t) -> p h t", h=DN_H) for n in range(6))
        Kb, Vb, Kd = (uT_flat[:, n * 768:(n + 1) * 768].rearrange("p (h t) -> p h t", h=DN_H) for n in range(3))
        wT = AT
        e = Y

        def delta_chunk(tag, c, r):
            levels = LEVELS[1:2]
            upper, lower = const("upper_s"), const("lower_s")
            tk = slice(offset(c), offset(c) + r)
            W = DN_H * r

            def heads(t, n=r):
                return t[:n, :, :r]

            def ph(k, rows=r, w=r):
                return pp[k][:rows, 0:DN_H * w].rearrange("p (h t) -> p h t", h=DN_H)

            s_pe, s_d, s_a, s_g = (sem(f"{tag}_{m}") for m in ("pe", "dve", "act", "pool"))
            return levels, upper, lower, tk, W, heads, ph, s_pe, s_d, s_a, s_g

        def delta_solve(tag, c, r, pe_tail, dve_tail, act_tail, sync_tail, pool_tail):
            levels, upper, lower, tk, W, heads, ph, s_pe, s_d, s_a, s_g = delta_chunk(tag, c, r)
            q, k = (lambda h: qkT[:, h, tk]), (lambda h: qkT[:, DN_H + h, tk])
            n_lv = len(levels)
            with nc.Block() as block:
                if sync_tail:
                    @block.sync
                    def _(sp):
                        sync_tail(sp, s_pe, s_d, s_a, s_g, n_lv)

                @block.tensor
                def _(pe):
                    for h in range(DN_H):
                        TE.matmul(ph(0)[:, h, :], bc(g_[:r, c, h], 1, r), upper[:r, :r], start=True, stop=True)
                    for h in range(DN_H):
                        TE.matmul(ph(1)[:, h, :], k(h), k(h), start=True, stop=True)
                    for h in range(DN_H):
                        ins = TE.matmul(ph(2)[:, h, :], k(h), q(h), start=True, stop=True)
                    ins.then_inc(s_pe, 1)
                    pe.wait_ge(s_d, 8)
                    for h in range(DN_H):
                        ins = TE.transpose(ph(0)[:, h, :], A[:r, h, :r], ident[:r, :r])
                    ins.then_inc(s_pe, 1)
                    for n in range(n_lv):
                        pe.wait_ge(s_d, 12 + 3 * n)
                        for h in range(DN_H):
                            ins = TE.matmul(ph(1)[:, h, :], AT[:r, h, :r], X[:r, h, :r], start=True, stop=True)
                        ins.then_inc(s_pe, 1)
                        pe.wait_ge(s_d, 13 + 3 * n)
                        for h in range(DN_H):
                            TE.matmul(ph(2)[:, h, :], XT[:r, h, :r], Y[:r, h, :r], start=True, stop=True)
                        for h in range(DN_H):
                            ins = TE.matmul(ph(3)[:, h, :], Y[:r, h, :r], XT[:r, h, :r], start=True, stop=True)
                        ins.then_inc(s_pe, 1)
                    pe.wait_ge(s_d, 12 + 3 * n_lv)
                    pe.wait_ge(s_g, 1)
                    for h in range(DN_H):
                        ins = TE.matmul(ph(1, P, r)[:, h, :], Kb[:r, h, :], XT[:r, h, :r], start=True, stop=True)
                    ins.then_inc(s_pe, 1)
                    pe_tail(pe, s_pe, s_d, s_a, s_g, n_lv)

                @block.gpsimd
                def _(pool):
                    for dst, src, f in ((Kb, 1, beG), (Vb, 2, beta), (Kd, 1, ekd)):
                        G.tensor_tensor(dst[:r], tok[src][:r, c, :].rearrange("p (h d) -> p h d", h=DN_H), bc(f[:r, c, :], 2, P), ALU.mult).then_inc(s_g, 1)
                    pool_tail(pool, s_g)

                @block.scalar
                def _(act):
                    a = Chain(act, s_a)
                    act.wait_ge(s_d, 3)
                    a(S.activation(heads(A), heads(A), ACT.Exp, scale=-1.0))
                    a(S.activation(heads(GT), heads(GT), ACT.Exp))
                    act.wait_ge(s_pe, 2)
                    a(S.activation(heads(AT), ph(0), ACT.Copy))
                    act_tail(act, a, s_pe, s_d, s_a, s_g, n_lv)

                @block.vector
                def _(dve):
                    d = Chain(dve, s_d)
                    dve.wait_ge(s_pe, 1)
                    d(V.tensor_tensor(heads(Y), ph(0), bc(G_[:r, c, :], 2, r), ALU.subtract))
                    d(V.tensor_scalar(heads(A), heads(Y), 0.0, None, ALU.max))
                    d(V.tensor_scalar(heads(GT), heads(Y), 0.0, None, ALU.min))
                    dve.wait_ge(s_a, 2)
                    d(V.tensor_tensor(heads(A), heads(A), bc(lower[:r, :r], 1, DN_H), ALU.mult))
                    d(V.tensor_tensor(heads(A), heads(A), ph(1), ALU.mult))
                    d(V.tensor_tensor(heads(GT), heads(GT), bc(upper[:r, :r], 1, DN_H), ALU.mult))
                    d(V.tensor_tensor(heads(GT), heads(GT), ph(2), ALU.mult))
                    d(V.tensor_tensor(heads(A), heads(A), bc(beta[:r, c, :], 2, r), ALU.mult))
                    d(V.tensor_tensor(heads(X), heads(A), bc(const("level1")[:r, :r], 1, DN_H), ALU.mult))
                    d(V.scalar_tensor_tensor(heads(X), heads(X), -1.0, bc(ident[:r, :r], 1, DN_H), ALU.mult, ALU.add))
                    dve.wait_ge(s_a, 3)
                    d(V.tensor_tensor(heads(XT), heads(AT), bc(const("level1T")[:r, :r], 1, DN_H), ALU.mult))
                    d(V.scalar_tensor_tensor(heads(XT), heads(XT), -1.0, bc(ident[:r, :r], 1, DN_H), ALU.mult, ALU.add))
                    for n, lv in enumerate(levels):
                        dve.wait_ge(s_pe, 3 + 2 * n)
                        d(V.tensor_tensor(heads(Y), ph(1), bc(const(f"level{lv}")[:r, :r], 1, DN_H), ALU.mult))
                        dve.wait_ge(s_pe, 4 + 2 * n)
                        d(V.tensor_tensor(heads(X), heads(X), ph(2), ALU.subtract))
                        d(V.tensor_tensor(heads(XT), heads(XT), ph(3), ALU.subtract))
                    dve_tail(dve, d, s_pe, s_d, s_a, s_g, n_lv)

        rows_o = tok[0]

        GH = DN_H // 2
        LV = LEVELS[1:]
        NL = len(LV)
        PS = 5 + 2 * NL
        W_T, E_ROWS, LAST = PS - 2, PS - 1, PS
        DV_A, DV_X, DV_N = 6, 10, 14 + 3 * NL
        ACT_N, POOL_N = 5, 3
        LAG = 1
        d_pe, d_d, d_a, d_g = ([sem(f"delta_{m}{g}") for g in range(2)] for m in ("products", "dve", "act", "pool"))
        s_zero = sem("state_zero")

        def group(t, g, rows=P):
            return t[:rows, GH * g:GH * (g + 1), :]

        def bank(k, g):
            return pp[k][:, 512 * g:512 * g + GH * P].rearrange("p (h t) -> p h t", h=GH)

        def staggered(do):
            for t in range(NC_P * PS + LAG):
                for g in range(2):
                    n = t - LAG * g
                    if 0 <= n < NC_P * PS:
                        do(g, n // PS, n % PS + 1)

        with nc.Block() as block:
            @block.tensor
            def _(pe):
                def step(g, c, k):
                    tk = slice(offset(c), offset(c) + P)
                    hs = [(h, GH * g + h) for h in range(GH)]
                    at_d, at_a, at_g = DV_N * c, ACT_N * c, POOL_N * c
                    if k == 1:
                        wait_after(pe, d_d[g], at_d)
                        for i, h in hs:
                            TE.matmul(bank(0, g)[:, i, :], bc(g_[:, c, h], 1, P), const("upper"), start=True, stop=True)
                        for i, h in hs:
                            TE.matmul(bank(1, g)[:, i, :], qkT[:, DN_H + h, tk], qkT[:, DN_H + h, tk], start=True, stop=True)
                        for i, h in hs:
                            ins = TE.matmul(bank(2, g)[:, i, :], qkT[:, DN_H + h, tk], qkT[:, h, tk], start=True, stop=True)
                    elif k == 2:
                        pe.wait_ge(d_d[g], at_d + DV_A)
                        for i, h in hs:
                            ins = TE.transpose(bank(0, g)[:, i, :], A[:, h, :], ident)
                    elif k < W_T and k % 2 == 1:
                        pe.wait_ge(d_d[g], at_d + DV_X + 3 * ((k - 3) // 2))
                        for i, h in hs:
                            ins = TE.matmul(bank(1, g)[:, i, :], AT[:, h, :], X[:, h, :], start=True, stop=True)
                    elif k < W_T:
                        pe.wait_ge(d_d[g], at_d + DV_X + 3 * ((k - 3) // 2) + 1)
                        for i, h in hs:
                            TE.matmul(bank(2, g)[:, i, :], XT[:, h, :], Y[:, h, :], start=True, stop=True)
                        for i, h in hs:
                            ins = TE.matmul(bank(3, g)[:, i, :], Y[:, h, :], XT[:, h, :], start=True, stop=True)
                    elif k == W_T:
                        pe.wait_ge(d_d[g], at_d + DV_X + 3 * NL)
                        pe.wait_ge(d_g[g], at_g + 1)
                        for i, h in hs:
                            ins = TE.matmul(bank(1, g)[:, i, :], Kb[:, h, :], XT[:, h, :], start=True, stop=True)
                    elif k == E_ROWS:
                        pe.wait_ge(d_g[g], at_g + 3)
                        for i, h in hs:
                            TE.matmul(bank(2, g)[:, i, :], XT[:, h, :], Vb[:, h, :], start=True, stop=False)
                            if i == 0:
                                pe.wait_ge(d_a[g], at_a + 4)
                                if c == 0:
                                    pe.wait_ge(s_zero, 1)
                            TE.matmul(bank(2, g)[:, i, :], wT[:, h, :], state[:, h, :], start=False, stop=True)
                        for i, h in hs:
                            ins = TE.matmul(bank(0, g)[:, i, :], qkT[:, h, tk], state[:, h, :], start=True, stop=True)
                    else:
                        pe.wait_ge(d_a[g], at_a + 5)
                        for i, h in hs:
                            TE.matmul(bank(3, g)[:, i, :], GT[:, h, :], e[:, h, :], start=True, stop=True)
                        for i, h in hs:
                            ins = TE.matmul(bank(1, g)[:, i, :], Kd[:, h, :], e[:, h, :], start=True, stop=True)
                    ins.then_inc(d_pe[g], 1)

                staggered(step)

            @block.gpsimd
            def _(pool):
                for c in range(NC_P):
                    for g in range(2):
                        for n, (dst, src, f) in enumerate(((Kb, 1, beG), (Vb, 2, beta), (Kd, 1, ekd))):
                            if c >= 1:
                                pool.wait_ge(d_pe[g], PS * (c - 1) + W_T + n)
                            G.tensor_tensor(group(dst, g), tok[src][:, c, GH * g * P:GH * (g + 1) * P].rearrange("p (h d) -> p h d", h=GH),
                                            bc(f[:, c, GH * g:GH * (g + 1)], 2, P), ALU.mult).then_inc(d_g[g], 1)

            @block.scalar
            def _(act):
                act.wait_ge(s_gs, 1)

                def step(g, c, k):
                    if k == 1:
                        act.wait_ge(d_d[g], DV_N * c + 3)
                        act.activation(group(A, g), group(A, g), ACT.Exp, scale=-1.0).then_inc(d_a[g], 1)
                        act.activation(group(GT, g), group(GT, g), ACT.Exp).then_inc(d_a[g], 1)
                    elif k == 2:
                        act.wait_ge(d_pe[g], PS * c + 2)
                        act.activation(group(AT, g), bank(0, g), ACT.Copy).then_inc(d_a[g], 1)
                    elif k == W_T:
                        act.wait_ge(d_pe[g], PS * c + W_T)
                        act.activation(group(wT, g), bank(1, g), ACT.Copy, scale=-1.0).then_inc(d_a[g], 1)
                    elif k == E_ROWS:
                        act.wait_ge(d_pe[g], PS * c + E_ROWS)
                        act.activation(group(e, g), bank(2, g), ACT.Copy).then_inc(d_a[g], 1)
                    elif k == LAST:
                        act.wait_ge(d_d[g], DV_N * (c + 1) - 1)
                        for i in range(GH):
                            h = GH * g + i
                            n = (c * 2 + g) * GH + i
                            if n >= 1:
                                act.wait_ge(s_sq, n)
                            act.activation(o_junk[:], rows_o[:, c, h * P:(h + 1) * P], ACT.Square, accum_out=gs[:, c, h:h + 1]).then_inc(s_sq, 1)

                staggered(step)

            @block.vector
            def _(dve):
                chain = [Chain(dve, s) for s in d_d]
                masks = {m: bc(const(m), 1, GH) for m in ["lower_big", "upper_neg", "level1", "level1T", "ident"] + [f"level{lv}" for lv in LV]}

                def step(g, c, k):
                    d = chain[g]
                    hg = slice(GH * g, GH * (g + 1))
                    A_, GT_, AT_, X_, XT_, Y_ = (group(t, g) for t in (A, GT, AT, X, XT, Y))
                    orow = rows_o[:, c, GH * g * P:GH * (g + 1) * P].rearrange("p (h d) -> p h d", h=GH)
                    st = group(state, g)
                    if k != W_T:
                        dve.wait_ge(d_pe[g], PS * c + k)
                    if k == 1:
                        d(V.tensor_tensor(Y_, bank(0, g), bc(G_[:, c, hg], 2, P), ALU.subtract))
                        d(V.scalar_tensor_tensor(A_, Y_, 0.0, masks["lower_big"], ALU.max, ALU.add))
                        d(V.scalar_tensor_tensor(GT_, Y_, 0.0, masks["upper_neg"], ALU.min, ALU.add))
                        dve.wait_ge(d_a[g], ACT_N * c + 1)
                        d(V.tensor_tensor(A_, A_, bank(1, g), ALU.mult))
                        dve.wait_ge(d_a[g], ACT_N * c + 2)
                        V.tensor_tensor(GT_, GT_, bank(2, g), ALU.mult).then_inc(d.sem, 1)
                        d.n += 1
                        d(V.tensor_tensor(A_, A_, bc(beta[:, c, hg], 2, P), ALU.mult))
                    elif k == 2:
                        d(V.tensor_tensor(X_, A_, masks["level1"], ALU.mult))
                        d(V.scalar_tensor_tensor(X_, X_, -1.0, masks["ident"], ALU.mult, ALU.add))
                        dve.wait_ge(d_a[g], ACT_N * c + 3)
                        d(V.tensor_tensor(XT_, AT_, masks["level1T"], ALU.mult))
                        d(V.scalar_tensor_tensor(XT_, XT_, -1.0, masks["ident"], ALU.mult, ALU.add))
                    elif k < W_T and k % 2 == 1:
                        d(V.tensor_tensor(Y_, bank(1, g), masks[f"level{LV[(k - 3) // 2]}"], ALU.mult))
                    elif k < W_T:
                        V.tensor_tensor(X_, X_, bank(2, g), ALU.subtract).then_inc(d.sem, 1)
                        d.n += 1
                        d(V.tensor_tensor(XT_, XT_, bank(3, g), ALU.subtract))
                    elif k == E_ROWS:
                        d(V.tensor_tensor(st, st, bc(dec[:, c, hg], 2, P), ALU.mult))
                        d(V.tensor_tensor(orow, bank(0, g), bc(eG[:, c, hg], 2, P), ALU.mult))
                    elif k == LAST:
                        d(V.tensor_tensor(orow, orow, bank(3, g), ALU.add))
                        d(V.tensor_tensor(st, st, bank(1, g), ALU.add))

                V.memset(gs[:], 1.0).then_inc(s_gs, 1)
                V.memset(state[:], 0.0).then_inc(s_zero, 1)
                dve.wait_ge(s_zero, 1)
                staggered(step)
        dump("o_rows", rows_o[:])
        s_state = sem("state_stored")
        SB = 4
        sS = [w.rearrange("p (b v) -> p b v", b=DB) for w in (uT_flat[:, 2304:3328], uT_flat[:, 3328:4352], ring[0][:, 4096:5120], ring[1][:, 4096:5120])]
        qwm = ring[0][:, 5120:6144].rearrange("p (k b n) -> p k b n", k=2, b=DB)
        km = [toks[0:NS, 1, 2 * k:2 * k + 2, :].rearrange("t c n -> t (c n)")[:, 0:DB * P].rearrange("t (b n) -> t b n", b=DB)
              for k in range(2)]
        s_w, s_qw, s_km, s_first, s_second = (sem(f"samples_{m}") for m in ("w_kept", "qw_masked", "k_masked", "first_products", "second_products"))
        s_sin, s_sout = [sem(f"states_in{k}") for k in range(SB)], [sem(f"states_out{k}") for k in range(SB)]

        def s_sync(sp, s_pe, s_d, s_a, s_g, n_lv):
            sp.dma_start(O["state_delta_prompt"][0, 0].rearrange("h k v -> k h v"), state[:]).then_inc(s_state, 16)
            B = 12 + 3 * n_lv
            for h in range(DN_H):
                if h >= SB:
                    store_s(sp, h - SB, s_d, B)
                    sp.wait_ge(s_sout[h % SB], 16)
                sp.dma_start(sS[h % SB], I["state_delta"][0, :, h].rearrange("b k v -> k b v")).then_inc(s_sin[h % SB], 16)
            for h in range(DN_H - SB, DN_H):
                store_s(sp, h, s_d, B)
            for k in range(SB):
                sp.wait_ge(s_sout[k], 16 * (-(-(DN_H - k) // SB)))
            sp.wait_ge(s_state, 16)

        def store_s(sp, h, s_d, B):
            sp.wait_ge(s_d, B + 4 * (h + 1))
            sp.dma_start(O["state_delta_sample"][0, :, h].rearrange("b k v -> k b v"), sS[h % SB]).then_inc(s_sout[h % SB], 16)

        def s_pe_tail(pe, s_pe, s_d, s_a, s_g, n_lv):
            B = 12 + 3 * n_lv

            def first(h):
                k, o = h % 2, (h % 2) * 512
                pe.wait_ge(s_sin[h % SB], 16 * (h // SB + 1))
                pe.wait_ge(s_qw, 2 * (h + 1))
                if h >= 2:
                    pe.wait_ge(s_d, B + 4 * (h - 1))
                for b in range(DB):
                    ins = TE.matmul(pp[2][0:2 * NS, o:o + P], qwm[:, k, b, :], sS[h % SB][:, b, :], start=(b == 0), stop=(b == DB - 1))
                    if b == 0:
                        TE.matmul(pp[2][NS:2 * NS, o:o + P], XT[0:NS, h, 0:NS], Vb[0:NS, h, :], start=False, stop=False)
                ins.then_inc(s_first, 1)

            def second(h):
                pe.wait_ge(s_a, 4 + h)
                pe.wait_ge(s_km, h + 1)
                TE.matmul(pp[3][0:NS, (h % 2) * 512:(h % 2) * 512 + P], GT[0:NS, h, 0:NS], e[0:NS, h, :], start=True, stop=True)
                for b in range(DB):
                    ins = TE.matmul(pp[h % 2][:, b * P:(b + 1) * P], km[h % 2][:, b, :], e[0:NS, h, :], start=True, stop=True)
                ins.then_inc(s_second, 1)

            pe.wait_ge(s_g, 3)
            first(0)
            for h in range(DN_H):
                if h == 0:
                    pe.wait_ge(s_w, 1)
                if h + 1 < DN_H:
                    first(h + 1)
                second(h)

        def s_act_tail(act, a, s_pe, s_d, s_a, s_g, n_lv):
            def squares(h):
                act.wait_ge(s_d, 12 + 3 * n_lv + 4 * h + 3)
                act.wait_ge(s_sq, DN_H * NC_P + h)
                S.activation(o_junk[0:NS, :], rows_o[0:NS, NC_P, h * P:(h + 1) * P], ACT.Square, accum_out=gs[0:NS, NC_P, h:h + 1]).then_inc(s_sq, 1)

            for h in range(DN_H):
                act.wait_ge(s_first, h + 1)
                a(S.activation(e[0:NS, h, :], pp[2][NS:2 * NS, (h % 2) * 512:(h % 2) * 512 + P], ACT.Copy))
                if h >= 1:
                    squares(h - 1)
            squares(DN_H - 1)

        wts = sb("w_samples", [P, DN_H, NS], where=DL)

        def s_pool_tail(pool, s_g):
            rowm = const("row_of").rearrange("p (b t) -> p b t", b=DB)
            pool.wait_ge(s_g, 3)
            pool.wait_ge(s_w, 1)
            for h in range(DN_H):
                k = h % 2
                if h >= 2:
                    pool.wait_ge(s_first, h - 1)
                G.tensor_tensor(qwm[:, k, :, 0:NS], bc(qkT[:, h, SEQ:T], 1, DB), rowm, ALU.mult).then_inc(s_qw, 1)
                G.tensor_tensor(qwm[:, k, :, NS:2 * NS], bc(wts[:, h, :], 1, DB), rowm, ALU.mult).then_inc(s_qw, 1)
                if h >= 2:
                    pool.wait_ge(s_second, h - 1)
                G.tensor_tensor(km[k], bc(Kd[0:NS, h, :], 1, DB), bc(const("col_of")[0:NS, :], 2, P), ALU.mult).then_inc(s_km, 1)

        def s_dve_tail(dve, d, s_pe, s_d, s_a, s_g, n_lv):
            c = NC_P
            dve.wait_ge(s_pe, 3 + 2 * n_lv)
            V.tensor_scalar(wts[:], pp[1][:, 0:DN_H * NS].rearrange("p (h t) -> p h t", h=DN_H), -1.0, None, ALU.mult).then_inc(s_w, 1)
            for h in range(DN_H):
                k, o = h % 2, (h % 2) * 512
                dve.wait_ge(s_first, h + 1)
                d(V.tensor_tensor(sS[h % SB], sS[h % SB], bc(dS[:, :, h], 2, P), ALU.mult))
                orow = rows_o[0:NS, c, h * P:(h + 1) * P]
                d(V.tensor_scalar(orow, pp[2][0:NS, o:o + P], eG[0:NS, c, h:h + 1], None, ALU.mult))
                dve.wait_ge(s_second, h + 1)
                d(V.tensor_tensor(orow, orow, pp[3][0:NS, o:o + P], ALU.add))
                d(V.tensor_tensor(sS[h % SB], sS[h % SB], pp[k][:].rearrange("p (b v) -> p b v", b=DB), ALU.add))

        delta_solve("deltas", NC_P, NS, s_pe_tail, s_dve_tail, s_act_tail, s_sync, s_pool_tail)
        DL.close()
        dump("o_all", rows_o[:])

        mergedT = uT
        with nc.Block() as block:
            s_a, s_d, s_g, s_t, s_k = (sem(f"gate_{m}") for m in ("act", "dve", "gated", "turned", "kept"))
            @block.scalar
            def _(act):
                act.wait_ge(s_d, 1)
                act.activation(gs[:], gs[:], ACT.Sqrt).then_inc(s_a, 1)
                for n in range(DN_H):
                    act.wait_ge(s_t, n + 1)
                    act.activation(mergedT[:, n, 0:SEQ], pp[n % 2][:, 0:SEQ], ACT.Copy)
                    act.activation(mergedT[:, n, SEQ:T], pp[n % 2][:, 512:512 + NS], ACT.Copy).then_inc(s_k, 1)

            @block.vector
            def _(dve):
                d = Chain(dve, s_d)
                d(V.tensor_scalar(gs[:], gs[:], 1.0 / P, EPS, ALU.mult, ALU.add))
                dve.wait_ge(s_a, 1)
                d(V.reciprocal(gs[:], gs[:]))
                for h in range(DN_H):
                    for c in range(NCH):
                        v = rows_o[:, c, h * P:(h + 1) * P]
                        ins = V.scalar_tensor_tensor(v, v, gs[:, c, h:h + 1], zs[:, c, h * P:(h + 1) * P], ALU.mult, ALU.mult)
                    ins.then_inc(s_g, 1)

            @block.tensor
            def _(pe):
                for n in range(DN_H):
                    pe.wait_ge(s_g, n + 1)
                    if n >= 2:
                        pe.wait_ge(s_k, n - 1)
                    for c in range(NC_P):
                        TE.transpose(pp[n % 2][:, c * P:(c + 1) * P], rows_o[:, c, n * P:(n + 1) * P], ident)
                    TE.transpose(pp[n % 2][:, 512:512 + NS], rows_o[0:NS, NC_P, n * P:(n + 1) * P], ident[0:NS, 0:NS]).then_inc(s_t, 1)

        def memory_attention(l, qmT, mkc, mvc, KT, pr, prT, Zq, stat):
            s_in, s_s, s_m, s_x, s_p, s_t, s_e, s_o, s_k, s_kt, s_kk, s_z, s_d = (
                sem(f"mem{l}_{m}") for m in ("cache_in", "scores", "max", "exp", "probs", "turned", "turned_kept", "out", "merged",
                                             "keys_turned", "keys_kept", "queries", "dve"))
            scale = MHD ** -0.5
            with nc.Block() as block:
                @block.sync
                def _(sp):
                    for dst, src in ((mkc, I["cache_mem_k"]), (mvc, I["cache_mem_v"])):
                        for m in range(2):
                            sp.dma_start(dst[:, :, m, :], src[l].rearrange("b m h d -> m b (h d)")[m * P:(m + 1) * P]).then_inc(s_in, 16)

                @block.tensor
                def _(pe):
                    def scores(c):
                        if c == NC_P:
                            pe.wait_ge(s_kk, 4)
                            pe.wait_ge(s_z, 1)
                        if c >= 2:
                            pe.wait_ge(s_x, c - 1)
                        if c < NC_P:
                            for h in range(MH):
                                j, a = divmod(h, 2)
                                ins = TE.matmul(pp[c % 2][:, h * MEM:(h + 1) * MEM], qmT[64 * j:64 * j + 64, a, c * P:(c + 1) * P],
                                                mem_kT[64 * j:64 * j + 64, l, a, :], start=True, stop=True)
                        else:
                            for b in range(DB):
                                for a in range(2):
                                    ins = TE.matmul(pp[c % 2][:, 0:MEM], Zq[:, a, b * P:(b + 1) * P], KT[:, a, b, :],
                                                    start=(b == 0 and a == 0), stop=(b == DB - 1 and a == 1))
                        ins.then_inc(s_s, 1)

                    def turn(c):
                        pe.wait_ge(s_p, c + 1)
                        if c >= 1:
                            pe.wait_ge(s_e, c)
                        if c == NC_P - 1:
                            pe.wait_ge(s_kk, 4)
                        for h in range(MH if c < NC_P else 1):
                            for m in range(2):
                                ins = TE.transpose(pp[2][:, (2 * h + m) * P:(2 * h + m + 1) * P], pr[c % 2][:, h * MEM + m * P:h * MEM + (m + 1) * P], ident)
                        ins.then_inc(s_t, 1)

                    def out(c):
                        pe.wait_ge(s_e, c + 1)
                        if c >= 1:
                            pe.wait_ge(s_k, c)
                        if c < NC_P:
                            for h in range(MH):
                                for m in range(2):
                                    ins = TE.matmul(pp[3][:, h * P:(h + 1) * P], mem_v[:, l, m, (h % 2) * P:(h % 2 + 1) * P],
                                                    prT[:, 2 * h + m, :], start=(m == 0), stop=(m == 1))
                        else:
                            for a in range(2):
                                for b in range(DB):
                                    for m in range(2):
                                        o = (a * DB + b) * MH * DS
                                        ins = TE.matmul(pp[3][:, o:o + MH * DS], mvc[:, b, m, a * P:(a + 1) * P],
                                                        prT[:, m, b * MH * DS:(b + 1) * MH * DS], start=(m == 0), stop=(m == 1))
                        ins.then_inc(s_o, 1)

                    def keys():
                        pe.wait_ge(s_in, 64)
                        pe.wait_ge(s_e, 3)
                        pe.wait_ge(s_k, 3)
                        for n in range(4):
                            if n >= 2:
                                pe.wait_ge(s_kk, n - 1)
                            for b in range(2):
                                for a in range(2):
                                    for m in range(2):
                                        o = (a * 2 + b) * MEM + m * P
                                        ins = TE.transpose(pp[2 + n % 2][:, o:o + P], mkc[:, 2 * n + b, m, a * P:(a + 1) * P], ident)
                            ins.then_inc(s_kt, 1)

                    scores(0)
                    scores(1)
                    for c in range(NCH):
                        turn(c)
                        if c + 2 < NC_P:
                            scores(c + 2)
                        out(c)
                        if c + 2 == NC_P:
                            keys()
                            scores(c + 2)

                @block.scalar
                def _(act):
                    def exp(c):
                        act.wait_ge(s_m, c + 1)
                        act.wait_ge(s_s, c + 1)
                        if c >= 2:
                            act.wait_ge(s_t, c - 1)
                        nh = MH if c < NC_P else 1
                        for h in range(nh):
                            ins = act.activation(pr[c % 2][:, h * MEM:(h + 1) * MEM], pp[c % 2][:, h * MEM:(h + 1) * MEM], ACT.Exp,
                                                 bias=stat[:, 1, c, h:h + 1], scale=scale, accum_out=stat[:, 2, c, h:h + 1])
                        ins.then_inc(s_x, 1)

                    exp(0)
                    for c in range(NCH):
                        nh = MH if c < NC_P else 1
                        if c + 1 < NC_P:
                            exp(c + 1)
                        act.wait_ge(s_t, c + 1)
                        if c >= 1:
                            act.wait_ge(s_o, c)
                        act.activation(prT[:, 0:2 * nh, :], pp[2][:, 0:2 * nh * P].rearrange("p (k t) -> p k t", t=P), ACT.Copy).then_inc(s_e, 1)
                        if c + 2 == NC_P:
                            for n in range(4):
                                act.wait_ge(s_kt, n + 1)
                                act.activation(KT[:, :, 2 * n:2 * n + 2, :], pp[2 + n % 2][:].rearrange("p (a b m) -> p a b m", a=2, b=2), ACT.Copy).then_inc(s_kk, 1)
                        if c + 1 == NC_P:
                            exp(c + 1)

                @block.vector
                def _(dve):
                    d = Chain(dve, s_d)

                    def maxima(c):
                        nh = MH if c < NC_P else 1
                        dve.wait_ge(s_s, c + 1)
                        d(V.tensor_reduce(stat[:, 0, c, 0:nh], pp[c % 2][:, 0:nh * MEM].rearrange("p (h m) -> p h m", h=nh), AX, ALU.max))
                        d(V.tensor_scalar(stat[:, 1, c, 0:nh], stat[:, 0, c, 0:nh], -scale, None, ALU.mult))
                        dve.sem_inc(s_m, 1)

                    def merged(c):
                        dve.wait_ge(s_o, c + 1)
                        for j in range(2):
                            k = slice(64 * j, 64 * j + 64)
                            if c < NC_P:
                                ins = V.tensor_copy(mergedT[k, 6:8, c * P:(c + 1) * P],
                                                    pp[3][k, 0:512].rearrange("p (j a t) -> p j a t", a=2, j=2)[:, j])
                                if j == 1:
                                    ins.then_inc(s_k, 1)
                            else:
                                for a in range(2):
                                    src = pp[3][k, a * P:(a + 1) * P].rearrange("p (b h t) -> p b h t", b=DB, h=MH)[:, :, 2 * a + j, :]
                                    V.tensor_copy(mergedT[k, 6 + a, SEQ:T].rearrange("p (b t) -> p b t", b=DB), src)

                    d(V.memset(Zq, 0.0))
                    for a in range(2):
                        for j in range(2):
                            k, o = slice(64 * j, 64 * j + 64), (2 * a + j) * DS
                            ins = V.tensor_copy(Zq[k, a, :].rearrange("p (b w) -> p b w", b=DB)[:, :, o:o + DS],
                                                qmT[k, a, SEQ:T].rearrange("p (b t) -> p b t", b=DB))
                    ins.then_inc(s_z, 1)
                    maxima(0)
                    maxima(1)
                    for c in range(NCH):
                        nh = MH if c < NC_P else 1
                        dve.wait_ge(s_x, c + 1)
                        d(V.reciprocal(stat[:, 3, c, 0:nh], stat[:, 2, c, 0:nh]))
                        v = pr[c % 2][:, 0:nh * MEM].rearrange("p (h m) -> p h m", h=nh)
                        V.tensor_tensor(v, v, bc(stat[:, 3, c, 0:nh], 2, MEM), ALU.mult).then_inc(s_p, 1)
                        if c >= 1:
                            merged(c - 1)
                        if c + 2 < NC_P:
                            maxima(c + 2)
                        if c + 1 == NC_P:
                            maxima(NC_P)
                    merged(NC_P)

        with ExitStack() as cx:
            stat = sb("mem_stat", [P, 4, NCH, MH], where=cx)
            x_b = x_flat[:, 0:4096].rearrange("p (b m n) -> p b m n", b=DB, m=2)
            q_b = qkT[:].rearrange("p n t -> p (n t)")[:, 0:4096].rearrange("p (b m n) -> p b m n", b=DB, m=2)
            f = toks[:].rearrange("p g c n -> p (g c n)")
            KT = f[:, 0:4096].rearrange("p (a b m) -> p a b m", a=2, b=DB)
            Zq = zs[:].rearrange("p c n -> p (c n)")[:, 0:2304].rearrange("p (a n) -> p a n", a=2)
            memory_attention(0, qmT, x_b, q_b, KT, [f[:, 4096:5120], f[:, 5120:6144]], f[:, 6144:7168].rearrange("p (k t) -> p k t", t=P), Zq, stat)

        def project_out(l, halves, junk, prefetch):
            s_x, s_m, s_v, s_sq, s_set = [sem(f"out{l}_{m}") for m in ("x_landed", "product", "added", "squares", "sums_set")]
            with nc.Block() as block:
                @block.sync
                def _(sp):
                    if l == 0:
                        sp.dma_start(x[:, 0:NC_P, :], I["x_prompt"][0].rearrange("(c p) d -> p c d", p=P)).then_inc(s_x, 16)
                        sp.dma_start(x[0:NS, NC_P, :], I["x_sample"].rearrange("b s d -> (b s) d")).then_inc(s_x, 16)
                    prefetch(sp)

                @block.tensor
                def _(pe):
                    for k, (w, name) in enumerate(halves):
                        arrived(pe, name)
                        for c in range(NC_P):
                            n = k * NC_P + c
                            for j in range(DJ):
                                ins = TE.matmul(pp[n // 2][:, (n % 2) * 512:(n % 2) * 512 + 512], mergedT[:, j, offset(c):offset(c) + P], w[:, j, :],
                                                start=(j == 0), stop=(j == DJ - 1))
                            ins.then_inc(s_m, 1)
                    pe.wait_ge(s_v, 1)
                    sample_parts(pp[0], mergedT, [lambda j, q=q: halves[q // 2][0][:, j, (q % 2) * 256:(q % 2 + 1) * 256] for q in range(4)]).then_inc(s_m, 1)

                @block.scalar
                def _(act):
                    act.wait_ge(s_set, 1)
                    for c, r in enumerate(ROWS):
                        act.wait_ge(s_v, NC_P + c + 1 if c < NC_P else 2 * NC_P + 4)
                        if c >= 2:
                            act.wait_ge(s_sq, c - 1)
                        act.activation(junk[:r, c % 2, :], x[:r, c, :], ACT.Square, accum_out=x_sums[:r, c:c + 1]).then_inc(s_sq, 1)

                @block.vector
                def _(dve):
                    V.memset(x_sums[:], 1.0).then_inc(s_set, 1)
                    if l == 0:
                        dve.wait_ge(s_x, 32)
                    for n in range(2 * NC_P):
                        k, c = divmod(n, NC_P)
                        dve.wait_ge(s_m, n + 1)
                        V.tensor_tensor(x[:, c, k * 512:(k + 1) * 512], x[:, c, k * 512:(k + 1) * 512],
                                        pp[n // 2][:, (n % 2) * 512:(n % 2) * 512 + 512], ALU.add).then_inc(s_v, 1)
                    dve.wait_ge(s_m, 2 * NC_P + 1)
                    for q in range(4):
                        xq = x[0:NS, NC_P, q * 256:(q + 1) * 256]
                        V.tensor_tensor(xq, xq, pp[0][NS * q:NS * (q + 1), 0:256], ALU.add).then_inc(s_v, 1)

        L0.close()


        DEEP = 5
        STEP = 2 * DEEP

        def experts(l, halves, prefetch=None):
            ME = ExitStack()
            with ME:
                def mb(name, shape, dt=F32):
                    return sb(f"{name}{l}", shape, dt, where=ME)

                slots = [ring[0], ring[1]] + [mb(f"ring{k}_", [P, 6144]) for k in range(2, DEEP)]

                def in_uT(*shapes):
                    flat, at, got = uT[:].rearrange("p j t -> p (j t)"), 0, []
                    for shape in shapes:
                        n = int(np.prod(shape[1:]))
                        v = flat[0:shape[0], at:at + n]
                        got.append(v if len(shape) == 2 else v.rearrange("p (a b) -> p a b", a=shape[1]))
                        at += n
                    return got
                xn = mb("scaled_rows", [P, NCH, D])
                lg = mb("logits", [P, NCH, NG + NE])
                gate = mb("gates", [P, 2, NCH])
                idx = mb("row_index", [P, NCH, 4], I32)
                base_i = mb("base_int", [P, NE], I32)
                over_i = mb("over_int", [P, 2], I32)
                n_i = mb("n_over_int", [P, 1], I32)
                gw = I["w_exp_gate"][l].rearrange("e (p j) n -> e p (j n)", p=P)
                uw = I["w_exp_up"][l].rearrange("e (p j) n -> e p (j n)", p=P)
                dw = I["w_exp_down"][l].rearrange("e (j p) n -> e p j n", p=P)

                class Lane:

                    def __init__(self, tag, deep, two):
                        self.deep, self.two = deep, two
                        self.w = [sem(f"{tag}_weights{k}") for k in range(deep)]
                        self.x = [sem(f"{tag}_rows{k}") for k in range(deep)]
                        self.st = [sem(f"{tag}_stored{k}") for k in range(two)]
                        self.turned, self.gu, self.sg, self.h, self.ht, self.hT, self.xT, self.dn, self.y, self.order = (
                            sem(f"{tag}_{m}") for m in ("turned", "gate_up", "silu", "hidden", "hidden_turned", "hidden_T", "tile_T", "down", "out", "order"))

                main = Lane(f"moe{l}", DEEP, 2)
                over = Lane(f"over{l}", 1, 1)

                def fetch_weights(sp, s, k, expert):
                    sp.dma_start(slots[k][:, 0:2048], gw[expert]).then_inc(s.w[k], 16)
                    sp.dma_start(slots[k][:, 2048:4096], uw[expert]).then_inc(s.w[k], 16)
                    sp.dma_start(slots[k][:, 4096:6144].rearrange("p (j n) -> p j n", j=2), dw[expert]).then_inc(s.w[k], 16)

                def weights_beyond_ring(sp):
                    for k in range(2, main.deep):
                        fetch_weights(sp, main, k, slice(k, k + 1))

                def weights_in_ring(sp):
                    for k in range(2):
                        fetch_weights(sp, main, k, slice(k, k + 1))

                project_out(l, halves, xn[:, 0:2, :], weights_beyond_ring)

                def chunk_logits(c):
                    r = ROWS[c]
                    for j in range(DJ):
                        ins = TE.matmul(pp[2][:r, P * c:P * c + NR3], uT[:, j, offset(c):offset(c) + r], w_rt[:, j].rearrange("p l n -> p (l n)"),
                                        start=(j == 0), stop=(j == DJ - 1))
                    ins.then_inc(s_lg, 1)

                s_lg = sem(f"route{l}_logits")
                norm_transposed(f"normf{l}", x, ROWS, [(G_FFN + l, uT)], kept_rows=xn, sync_extra=weights_in_ring, on_chunk=chunk_logits, sums=x_sums)
                RT = ExitStack()
                with RT:
                    w1, w2, oh1, oh2, em, rank, before, sc, ge, tb, ov, real = in_uT(
                        *[[P, NCH, NE]] * 6, [P, NCH + 1, NE], [P, 12, NCH], [P, NCH, NG], [P, 9, NE], [P, 2], [P, 1])
                    s_d, s_a, s_r, s_z, s_sc = (sem(f"route{l}_{m}") for m in ("dve", "act", "ranks", "table", "scattered"))
                    steps = {}
                    with nc.Block() as block:
                        @block.vector
                        def _(dve):
                            d = Chain(dve, s_d)
                            gb4 = small[:, 12 + 36 * l:48 + 36 * l]
                            d(V.memset(before[:, 0, :], 0.0))
                            d(V.tensor_scalar(real[:], const("rows"), float(NS), None, ALU.is_lt))
                            d(V.memset(lg[:], 0.0))
                            dve.wait_ge(s_lg, NCH)
                            own = slice(l * (NG + NE), (l + 1) * (NG + NE))
                            d(V.tensor_tensor(lg[:, 0:NC_P, :], pp[2][:, 0:P * NC_P].rearrange("p (c n) -> p c n", n=P)[:, :, own],
                                              bc(gb4, 1, NC_P), ALU.add))
                            d(V.tensor_tensor(lg[0:NS, NC_P, :], pp[2][0:NS, P * NC_P:P * NC_P + NR3][:, own], gb4[0:NS, :], ALU.add))
                            gl, el = lg[:, :, 0:NG], lg[:, :, NG:]
                            gmax, gval, v1, v2, m1, t, r1, a1, o1, lt = (sc[:, k, :] for k in range(10))
                            d(V.tensor_reduce(gmax, gl, AX, ALU.max))
                            d(V.tensor_tensor(ge[:], gl, bc(gmax, 2, NG), ALU.subtract))
                            steps["group"] = d.n
                            dve.wait_ge(s_a, 1)
                            d(V.tensor_reduce(gval, ge[:], AX, ALU.add))
                            d(V.reciprocal(gval, gval))
                            first = const("first_of_4")
                            d(V.tensor_tensor(ge[:], gl, bc(gmax, 2, NG), ALU.is_equal))
                            d(V.tensor_tensor(ge[:], ge[:], bc(first, 1, NCH), ALU.mult))
                            d(V.tensor_reduce(t, ge[:], AX, ALU.max))
                            d(V.tensor_tensor(ge[:], ge[:], bc(t, 2, NG), ALU.is_equal))
                            g8 = ge[:].rearrange("p c g -> p (c g)")
                            fl = lambda a: a.rearrange("p c (g e) -> p (c g) e", e=EPG)
                            w1g = w1[:].rearrange("p c (g e) -> p (c g) e", e=EPG)
                            d(V.tensor_copy(w1g, bc(g8, 2, EPG)))
                            d(V.tensor_tensor(em[:], el, w1[:], ALU.mult))
                            d(V.tensor_scalar(w1[:], w1[:], -1.0, BIG, ALU.add, ALU.mult))
                            d(V.tensor_tensor(em[:], em[:], w1[:], ALU.add))
                            for k, (v, oh) in enumerate(((v1, oh1), (v2, oh2))):
                                d(V.tensor_reduce(v, em[:], AX, ALU.max))
                                d(V.tensor_tensor(oh[:], em[:], bc(v, 2, NE), ALU.is_equal))
                                d(V.tensor_tensor(oh[:], oh[:], bc(const("first_of_32"), 1, NCH), ALU.mult))
                                d(V.tensor_reduce(m1, oh[:], AX, ALU.max))
                                d(V.tensor_tensor(oh[:], oh[:], bc(m1, 2, NE), ALU.is_equal))
                                if k == 0:
                                    d(V.scalar_tensor_tensor(em[:], oh[:], -BIG, em[:], ALU.mult, ALU.add))
                            d(V.tensor_tensor(w1[:], oh1[:], oh2[:], ALU.add))
                            d(V.tensor_scalar(w1[:, NC_P, :], w1[:, NC_P, :], real[:], None, ALU.mult))
                            for c in range(NCH):
                                d(V.tensor_tensor(before[:, c + 1, :], before[:, c, :], w1[:, c, :], ALU.add))
                            d(V.tensor_tensor(t, v2, v1, ALU.subtract))
                            steps["chosen"] = d.n
                            dve.wait_ge(s_a, 2)
                            g1, g2 = gate[:, 0, :], gate[:, 1, :]
                            d(V.tensor_scalar(g1, t, 1.0, None, ALU.add))
                            d(V.reciprocal(g1, g1))
                            d(V.tensor_tensor(g1, g1, gval, ALU.mult))
                            d(V.tensor_tensor(g2, g1, t, ALU.mult))
                            dve.wait_ge(s_r, 1)
                            d(V.tensor_copy(rank[:], pp[0][:, 0:NE * NCH].rearrange("p (c n) -> p c n", n=NE)))
                            cnt, base, no, oin, ob, A, Bt, sel, tmp = (tb[:, k, :] for k in range(9))
                            d(V.tensor_copy(cnt, pp[1][:, 0:NE]))
                            one = ones[:, 0:NE]
                            d(V.tensor_tensor_scan(base, one, cnt, 0.0, ALU.mult, ALU.add))
                            d(V.tensor_tensor(base, base, cnt, ALU.subtract))
                            d(V.scalar_tensor_tensor(em[:], rank[:], -1.0, bc(base, 1, NCH), ALU.add, ALU.add))
                            for k, oh in ((0, oh1), (1, oh2)):
                                d(V.tensor_tensor(w2[:], oh[:], em[:], ALU.mult))
                                d(V.tensor_reduce(t, w2[:], AX, ALU.add))
                                d(V.tensor_copy(idx[:, :, k], t))
                                steps[f"to{k}"] = d.n
                            d(V.tensor_scalar(no, cnt, float(SLOTS), None, ALU.is_gt))
                            for k in range(2, -(-T // SLOTS)):
                                d(V.scalar_tensor_tensor(no, cnt, float(SLOTS * k), no, ALU.is_gt, ALU.add))
                            d(V.tensor_tensor_scan(oin, one, no, 0.0, ALU.mult, ALU.add))
                            d(V.tensor_tensor(ob, oin, no, ALU.subtract))
                            d(V.tensor_copy(base_i[:], base))
                            d(V.tensor_copy(n_i[:], oin[:, NE - 1:NE]))
                            rows = const("rows")
                            d(V.tensor_scalar(sel, ob, rows, None, ALU.is_le))
                            d(V.tensor_scalar(tmp, oin, rows, None, ALU.is_gt))
                            d(V.tensor_tensor(sel, sel, tmp, ALU.mult))
                            d(V.tensor_tensor(tmp, sel, const("experts"), ALU.mult))
                            d(V.tensor_reduce(ov[:, 0:1], tmp, AX, ALU.add))
                            d(V.scalar_tensor_tensor(tmp, ob, -float(SLOTS), base, ALU.mult, ALU.add))
                            d(V.tensor_tensor(tmp, tmp, sel, ALU.mult))
                            d(V.tensor_reduce(ov[:, 1:2], tmp, AX, ALU.add))
                            d(V.tensor_tensor(ov[:, 1:2], ov[:, 1:2], const("over_shift"), ALU.add))
                            d(V.tensor_copy(over_i[:], ov[:]))
                            steps["over"] = d.n
                            d(V.tensor_scalar(Bt, ob, float(NE - 1), float(SLOTS), ALU.add, ALU.mult))
                            d(V.tensor_scalar(A, const("experts"), float(SLOTS), None, ALU.mult))
                            for k, oh in ((0, oh1), (1, oh2)):
                                for dst, src in ((r1, rank[:]), (a1, bc(A, 1, NCH)), (o1, bc(Bt, 1, NCH))):
                                    d(V.tensor_tensor(w2[:], oh[:], src, ALU.mult))
                                    d(V.tensor_reduce(dst, w2[:], AX, ALU.add))
                                d(V.tensor_scalar(r1, r1, -1.0, None, ALU.add))
                                d(V.tensor_scalar(lt, r1, float(SLOTS), None, ALU.is_lt))
                                d(V.tensor_tensor(a1, a1, o1, ALU.subtract))
                                d(V.tensor_tensor(a1, a1, lt, ALU.mult))
                                d(V.tensor_tensor(r1, r1, o1, ALU.add))
                                d(V.tensor_tensor(r1, r1, a1, ALU.add))
                                d(V.tensor_copy(idx[:, :, 2 + k], r1))

                        @block.tensor
                        def _(pe):
                            pe.wait_ge(s_d, steps["chosen"])
                            TE.matmul(pp[0][:, 0:NE * NCH], const("upper"), w1[:].rearrange("p c n -> p (c n)"), start=True, stop=False)
                            TE.matmul(pp[0][:, 0:NE * NCH], ones, before[:, 0:NCH, :].rearrange("p c n -> p (c n)"), start=False, stop=True)
                            ins = TE.matmul(pp[1][:, 0:NE], ones, before[:, NCH, :], start=True, stop=True)
                            ins.then_inc(s_r, 1)

                        @block.scalar
                        def _(act):
                            act.wait_ge(s_d, steps["group"])
                            act.activation(ge[:], ge[:], ACT.Exp).then_inc(s_a, 1)
                            act.wait_ge(s_d, steps["chosen"])
                            t = sc[:, 5, :]
                            act.activation(t, t, ACT.Exp).then_inc(s_a, 1)

                        @block.gpsimd
                        def _(pool):
                            for k in range(2):
                                pool.wait_ge(s_d, steps[f"to{k}"])
                                for c, r in enumerate(ROWS):
                                    pool.indirect_dma_start(xs, bass.IndirectOffsetOnAxis(idx[:r, c, k:k + 1], 0), xn[:r, c, :], None).then_inc(s_sc, 16)
                            pool.wait_ge(s_sc, 16 * 2 * NCH)

                        @block.sync
                        def _(sp):
                            sp.wait_ge(s_d, steps["over"])
                            sp.dma_start(over_rows, over_i[:]).then_inc(s_z, 16)
                            sp.wait_ge(s_z, 16)

                xg = xn[0:SLOTS, 0:DEEP, :]
                t = in_uT(*[[P, DJ, SLOTS]] * 2, *[[P, P]] * 4, *[[P, 2, SLOTS]] * 2, *[[P, D // 2]] * 2)
                xT, sg, hh, hT, yr = (t[2 * n:2 * n + 2] for n in range(5))

                def credits(pe, dve, act, s):
                    if pe is not None:
                        pe.sem_inc(s.turned, s.deep)
                        pe.sem_inc(s.dn, s.deep)
                        pe.sem_inc(s.gu, s.two)
                    if dve is not None:
                        dve.sem_inc(s.h, s.two)
                        dve.sem_inc(s.xT, 1)
                        dve.sem_inc(s.hT, 1)
                    if act is not None:
                        act.sem_inc(s.y, 1)
                        for st in s.st:
                            act.sem_inc(st, 16)

                def fetch_rows(sp, s, e, k, row):
                    sp.wait_ge(s.turned, e + 1)
                    sp.dma_start(xg[:, k % s.deep, :], xs[row, :]).then_inc(s.x[k % s.deep], 16)

                def fetch(sp, s, e, k, expert, row):
                    sp.wait_ge(s.dn, e + 1)
                    fetch_weights(sp, s, k % s.deep, expert)
                    fetch_rows(sp, s, e, k, row)

                def turn(pe, s, e, k, n):
                    pe.wait_ge(s.x[k % s.deep], 16 * (n + 1))
                    pe.wait_ge(s.xT, e + 1)
                    xv = xg[:, k % s.deep, :].rearrange("t (p j) -> t j p", j=DJ)
                    pe.sem_inc(s.order, 1)
                    for j in range(DJ):
                        ins = TE.transpose(pp[3][:, j * SLOTS:(j + 1) * SLOTS], xv[:, j, :], ident[:SLOTS, :SLOTS])
                    ins.then_inc(s.turned, 1)

                def gate_up(pe, s, e, k, n, half):
                    b = k % s.two
                    if half == 0:
                        pe.wait_ge(s.xT, e + 2)
                        pe.wait_ge(s.w[k % s.deep], 48 * (n + 1))
                        pe.wait_ge(s.h, e + 1)
                    w = slots[k % s.deep][:, 0:4096].rearrange("p (g j n) -> p g j n", g=2, j=DJ)
                    for j in range(half * DJ // 2, (half + 1) * DJ // 2):
                        for q in range(2):
                            ins = TE.matmul(pp[0][q * SLOTS:(q + 1) * SLOTS, b * 512:b * 512 + 2 * P], xT[b][:, j, :], w[:, :, j, q * P:(q + 1) * P],
                                            start=(j == 0), stop=(j == DJ - 1))
                    if half == 1:
                        ins.then_inc(s.gu, 1)

                def turn_hidden(pe, s, e, k):
                    b = k % s.two
                    pe.wait_ge(s.h, e + 1 + s.two)
                    pe.wait_ge(s.hT, e + 1)
                    pe.sem_inc(s.order, 1)
                    TE.transpose(pp[1][:, 0:P], hh[b][:], ident).then_inc(s.ht, 1)

                def down(pe, s, e, k):
                    b = k % s.two
                    pe.wait_ge(s.hT, e + 2)
                    pe.wait_ge(s.y, e + 1)
                    w = slots[k % s.deep][:, 4096:6144].rearrange("p (j n) -> p j n", j=2)
                    for j in range(2):
                        for q in range(2):
                            ins = TE.matmul(pp[2][q * SLOTS:(q + 1) * SLOTS, 0:512], hT[b][:, j, :], w[:, j, q * 512:(q + 1) * 512], start=(j == 0), stop=(j == 1))
                    ins.then_inc(s.dn, 1)

                def keep_tile(dve, s, e, k):
                    b = k % s.two
                    dve.wait_ge(s.turned, e + 1 + s.deep)
                    dve.wait_ge(s.gu, e + 1)
                    V.tensor_tensor(xT[b][:], pp[3][:, 0:DJ * SLOTS].rearrange("p (j t) -> p j t", j=DJ), bc(gains[:, G_FFN + l, :], 2, SLOTS),
                                    ALU.mult).then_inc(s.xT, 1)

                def hidden(dve, s, e, k):
                    b = k % s.two
                    dve.wait_ge(s.sg, e + 1)
                    V.tensor_tensor(hh[b][:], sg[b][:], pp[0][:, b * 512 + P:b * 512 + 2 * P], ALU.mult).then_inc(s.h, 1)

                def keep_hidden(dve, s, e, k):
                    b = k % s.two
                    dve.wait_ge(s.ht, e + 1)
                    V.tensor_copy(hT[b][:], pp[1][:, 0:2 * SLOTS].rearrange("p (j t) -> p j t", j=2)).then_inc(s.hT, 1)

                def silu(act, s, e, k):
                    b = k % s.two
                    act.wait_ge(s.gu, e + 1 + s.two)
                    act.wait_ge(s.h, e + 1)
                    act.activation(sg[b][:], pp[0][:, b * 512:b * 512 + P], ACT.Silu).then_inc(s.sg, 1)

                def store(act, s, e, k, n, dst):
                    b = k % s.two
                    act.wait_ge(s.dn, e + 1 + s.deep)
                    act.wait_ge(s.st[b], 16 * n + 16)
                    act.activation(yr[b][:], pp[2][:, 0:512], ACT.Copy).then_inc(s.y, 1)
                    act.wait_ge(s.y, e + 2)
                    act.dma_start(dst.rearrange("t (q n) -> q t n", q=2), yr[b][:]).then_inc(s.st[b], 16)

                with nc.Block() as block:
                    @block.sync
                    def _(sp):
                        def row_of(e):
                            row = sp.value_load(base_i[0:1, e], min_val=0, max_val=2 * T)
                            return bass.ds(row, SLOTS)

                        for e in range(DEEP):
                            fetch_rows(sp, main, e, e, row_of(slice(e, e + 1)))
                        loops = (NE - DEEP) // STEP
                        with sp.Fori(0, loops) as i:
                            for k in range(DEEP, DEEP + STEP):
                                e = i * STEP + k
                                fetch(sp, main, e, k % STEP, bass.ds(e, 1), row_of(bass.ds(e, 1)))
                        for e in range(DEEP + loops * STEP, NE):
                            fetch(sp, main, e, e % STEP, slice(e, e + 1), row_of(slice(e, e + 1)))

                    loops = (NE - 2) // STEP
                    rest = range(1 + loops * STEP, NE)

                    @block.tensor
                    def _(pe):
                        def step(e, k, n, n_next):
                            gate_up(pe, main, e, k, n, 0)
                            turn_hidden(pe, main, e - 1, (k - 1) % STEP)
                            if n_next is not None:
                                turn(pe, main, e + 1, (k + 1) % STEP, n_next)
                            gate_up(pe, main, e, k, n, 1)
                            down(pe, main, e - 1, (k - 1) % STEP)

                        credits(pe, None, None, main)
                        turn(pe, main, 0, 0, 0)
                        gate_up(pe, main, 0, 0, 0, 0)
                        turn(pe, main, 1, 1, 0)
                        gate_up(pe, main, 0, 0, 0, 1)
                        with pe.Fori(0, loops) as i:
                            for k in range(1, 1 + STEP):
                                step(i * STEP + k, k % STEP, i * 2 + k // DEEP, i * 2 + (k + 1) // DEEP)
                        for e in rest:
                            step(e, e % STEP, e // DEEP, (e + 1) // DEEP if e + 1 < NE else None)
                        turn_hidden(pe, main, NE - 1, (NE - 1) % STEP)
                        down(pe, main, NE - 1, (NE - 1) % STEP)

                    @block.vector
                    def _(dve):
                        def step(e, k, last=False):
                            keep_hidden(dve, main, e - 1, (k - 1) % STEP)
                            if not last:
                                keep_tile(dve, main, e + 1, (k + 1) % STEP)
                            hidden(dve, main, e, k)

                        credits(None, dve, None, main)
                        keep_tile(dve, main, 0, 0)
                        keep_tile(dve, main, 1, 1)
                        hidden(dve, main, 0, 0)
                        with dve.Fori(0, loops) as i:
                            for k in range(1, 1 + STEP):
                                step(i * STEP + k, k % STEP)
                        for e in rest:
                            step(e, e % STEP, last=e == NE - 1)
                        keep_hidden(dve, main, NE - 1, (NE - 1) % STEP)

                    @block.scalar
                    def _(act):
                        def step(e, k, n):
                            silu(act, main, e, k)
                            store(act, main, e - 1, (k - 1) % STEP, n, ys[bass.ds((e - 1) * SLOTS, SLOTS), :])

                        credits(None, None, act, main)
                        silu(act, main, 0, 0)
                        with act.Fori(0, loops) as i:
                            for k in range(1, 1 + STEP):
                                step(i * STEP + k, k % STEP, i * DEEP + (k - 1) // 2)
                        for e in rest:
                            step(e, e % STEP, (e - 1) // 2)
                        store(act, main, NE - 1, (NE - 1) % STEP, (NE - 1) // 2, ys[bass.ds((NE - 1) * SLOTS, SLOTS), :])
                        for b in range(2):
                            act.wait_ge(main.st[b], 16 + 16 * NE // 2)

                with nc.Block() as block:
                    def count(eng):
                        return eng.value_load(n_i[0:1, 0:1], min_val=0, max_val=OVER)

                    @block.sync
                    def _(sp):
                        n = count(sp)
                        with sp.If(n > 0):
                            with sp.Fori(0, n) as j:
                                expert = sp.value_load(over_rows[bass.ds(j, 1), 0:1], min_val=0, max_val=NE - 1)
                                row = sp.value_load(over_rows[bass.ds(j, 1), 1:2], min_val=0, max_val=2 * T)
                                fetch(sp, over, j, 0, bass.ds(expert, 1), bass.ds(row, SLOTS))

                    @block.tensor
                    def _(pe):
                        n = count(pe)
                        credits(pe, None, None, over)
                        with pe.If(n > 0):
                            with pe.Fori(0, n) as j:
                                turn(pe, over, j, 0, j)
                                gate_up(pe, over, j, 0, j, 0)
                                gate_up(pe, over, j, 0, j, 1)
                                turn_hidden(pe, over, j, 0)
                                down(pe, over, j, 0)

                    @block.vector
                    def _(dve):
                        n = count(dve)
                        credits(None, dve, None, over)
                        with dve.If(n > 0):
                            with dve.Fori(0, n) as j:
                                keep_tile(dve, over, j, 0)
                                hidden(dve, over, j, 0)
                                keep_hidden(dve, over, j, 0)

                    @block.scalar
                    def _(act):
                        n = count(act)
                        credits(None, None, act, over)
                        with act.If(n > 0):
                            with act.Fori(0, n) as j:
                                silu(act, over, j, 0)
                                store(act, over, j, 0, j, ys[bass.ds(j * SLOTS + NE * SLOTS, SLOTS), :])
                                act.wait_ge(over.st[0], j * 16 + 32)

                parts = [slots[2 + n // 6][:, (n % 6) * D:(n % 6 + 1) * D] for n in range(2 * NCH)]
                junk = slots[3][:, 4 * D:6 * D].rearrange("p (k d) -> p k d", k=2)
                s_y, s_c = [sem(f"gather{l}_{n}") for n in range(2 * NCH)], sem(f"combine{l}")
                s_sq = sem(f"x_squares{l}")
                combined.append(s_c)
                with nc.Block() as block:
                    if prefetch:
                        block.sync(prefetch)

                    @block.scalar
                    def _(act):
                        for c, r in enumerate(ROWS):
                            act.wait_ge(s_c, 1 + 2 * (c + 1))
                            if c >= 2:
                                act.wait_ge(s_sq, c - 1)
                            act.activation(junk[:r, c % 2, :], x[:r, c, :], ACT.Square, accum_out=x_sums[:r, c:c + 1]).then_inc(s_sq, 1)

                    @block.gpsimd
                    def _(pool):
                        for n in range(2 * NCH):
                            c, k = divmod(n, 2)
                            r = ROWS[c]
                            pool.indirect_dma_start(parts[n][:r, :], None, ys, bass.IndirectOffsetOnAxis(idx[:r, c, 2 + k:3 + k], 0)).then_inc(s_y[n], 16)

                    @block.vector
                    def _(dve):
                        d = Chain(dve, s_c)
                        d(V.memset(x_sums[:], 1.0))
                        for n in range(2 * NCH):
                            c, k = divmod(n, 2)
                            r = ROWS[c]
                            dve.wait_ge(s_y[n], 16)
                            d(V.scalar_tensor_tensor(x[:r, c, :], parts[n][:r, :], gate[:r, k, c:c + 1], x[:r, c, :], ALU.mult, ALU.add))

        reuse_semaphores()
        W_KV = KL + RP
        w_dkv = ring[0][:, 0:DJ * W_KV].rearrange("p (j n) -> p j n", j=DJ)
        w_uq = ring[0][:, DJ * W_KV:DJ * W_KV + 3 * 1152].rearrange("p (j n) -> p j n", j=3)
        w_inb = ring[1][:, 0:DJ * 640].rearrange("p (j n) -> p j n", j=DJ)

        combined = []

        def layer1_weights(sp):
            sp.wait_ge(combined[0], 1 + NCH)
            load(sp, 0, "dkv", (w_dkv, pj(I["w_dkv"])))
            load(sp, 1, "inb", (w_inb, pj(I["w_in_b"][0])))

        experts(0, [(slot3(1, 512), "out0"), (slot3(0, 512), "out1")], layer1_weights)
        reuse_semaphores()
        dump("x_1", x[:, 0:NC_P, :])
        dump("x_1_s", x[0:NS, NC_P, :])

        L1 = ctx.enter_context(ExitStack())
        cT = sb("latent_T", [P, 2, T], where=L1)
        krT = sb("rope_T", [RP, T], where=L1)
        c_tok = sb("latent_rows", [P, NCH, KL], where=L1)
        qmT1 = sb("qmT1", [P, 2, T], where=L1)
        w_uv = sb("w_uv_rows", [P, 2, DN_H * P], where=L1)
        AT1 = ctx.enter_context(ExitStack())
        q_latT = sb("q_latent_T", [P, DN_H, 2, T], where=AT1)
        qrT = sb("q_rope_T", [RP, DN_H, T], where=AT1)
        w_ukT = sb("w_uk_T", [P, DN_H, KL], where=AT1)
        page_i = sb("page_index", [P, DB], U32, where=AT1)
        QX = ctx.enter_context(ExitStack())
        cqT = sb("cq_T", [P, 3, T], where=QX)
        hT = q_latT[:].rearrange("p h a t -> p (h a t)")[:, 0:DJ * T].rearrange("p (j t) -> p j t", j=DJ)
        norm_transposed("norm1", x, ROWS, [(G_MIX + 1, uT), (G_KV, hT)], sums=x_sums)
        cos = const("cos").rearrange("p (c f) -> p c f", c=NCH)
        sin = const("sin").rearrange("p (c f) -> p c f", c=NCH)

        def rotate(d, out, src, tmp, lead):
            h = RP // 2
            a, b = src[..., 0:h], src[..., h:RP]
            d(V.tensor_tensor(out[..., 0:h], a, lead(cos), ALU.mult))
            d(V.tensor_tensor(tmp, b, lead(sin), ALU.mult))
            d(V.tensor_tensor(out[..., 0:h], out[..., 0:h], tmp, ALU.subtract))
            d(V.tensor_tensor(out[..., h:RP], b, lead(cos), ALU.mult))
            d(V.tensor_tensor(tmp, a, lead(sin), ALU.mult))
            d(V.tensor_tensor(out[..., h:RP], out[..., h:RP], tmp, ALU.add))

        with ExitStack() as cx:
            raw1 = sb("kv_raw", [P, NCH, W_KV], where=cx)
            rawq = sb("cq_raw", [P, NCH, QL], where=cx)
            sqr = sb("sq1", [P, QL], where=cx)
            kr_tok = sb("rope_rows", [P, NCH, RP], where=cx)
            tmp = sb("rope_tmp", [P, NCH, RP // 2], where=cx)
            st = sb("rms1", [P, 2, NCH], where=cx)
            g_lat = sb("g_lat", [P, KL], where=cx)
            gq = sb("g_q", [P, 3], where=cx)
            pg = sb("pages", [P, DB], I32, where=cx)
            pgf = sb("pages_f", [P, DB], where=cx)
            s_w, s_m, s_q, s_d, s_a, s_c, s_t, s_k, s_st, s_v, s_qm, s_i = (
                sem(f"kv_{m}") for m in ("weights", "product", "cq_product", "dve", "act", "copied", "turned", "kept", "stored", "uv", "queries", "small"))
            with nc.Block() as block:
                @block.sync
                def _(sp):
                    sp.dma_start(g_lat[:], I["g_kv_latent"].partition_broadcast(P)).then_inc(s_i, 16)
                    sp.dma_start(gq[:], I["g_q"][0].rearrange("(p j) -> p j", p=P)).then_inc(s_i, 16)
                    with nc.allow_non_contiguous_dma("a table of 128 page numbers"):
                        for j in range(NPG):
                            sp.dma_start(pg[8 * j:8 * j + 8, :], I["page_table"][:, j].partition_broadcast(8)).then_inc(s_i, 16)
                    sp.dma_start(w_uq, pj(I["w_uq"][0])).then_inc(s_v, 16)
                    sp.dma_start(w_uv[:], I["w_uv"].rearrange("(a p) h v -> p a (h v)", p=P)).then_inc(s_v, 16)
                    sp.wait_ge(s_d, 7 + 11)
                    sp.dma_start(O["kv_latent_prompt"][0].rearrange("(c p) n -> p c n", p=P), c_tok[:, 0:NC_P, :]).then_inc(s_st, 16)
                    sp.dma_start(O["kv_latent_sample"].rearrange("b t n -> (b t) n"), c_tok[0:NS, NC_P, :]).then_inc(s_st, 16)
                    sp.dma_start(O["k_rope_prompt"][0].rearrange("(c p) n -> p c n", p=P), kr_tok[:, 0:NC_P, :]).then_inc(s_st, 16)
                    sp.dma_start(O["k_rope_sample"].rearrange("b t n -> (b t) n"), kr_tok[0:NS, NC_P, :]).then_inc(s_st, 16)
                    sp.wait_ge(s_st, 64)
                    sp.wait_ge(s_v, 32)

                @block.tensor
                def _(pe):
                    arrived(pe, "dkv")
                    arrived(pe, "inb")
                    for c, r in enumerate(ROWS):
                        b = (c % 2) * 512
                        if c >= 2:
                            pe.wait_ge(s_c, 2 * (c - 1))
                        if c == NC_P:
                            h = W_KV // 2
                            sample_parts(pp[0][:, b:b + 512], hT, [lambda j, q=q, h=h: w_dkv[:, j, q * h:(q + 1) * h] for q in range(2)]).then_inc(s_m, 1)
                            h = QL // 2
                            sample_parts(pp[1][:, b:b + 512], uT, [lambda j, q=q, h=h: w_inb[:, j, q * h:(q + 1) * h] for q in range(2)]).then_inc(s_m, 1)
                            continue
                        for j in range(DJ):
                            ins = TE.matmul(pp[0][:r, b:b + W_KV], hT[:, j, offset(c):offset(c) + r], w_dkv[:, j, :], start=(j == 0), stop=(j == DJ - 1))
                        ins.then_inc(s_m, 1)
                        for j in range(DJ):
                            ins = TE.matmul(pp[1][:r, b:b + QL], uT[:, j, offset(c):offset(c) + r], w_inb[:, j, 0:QL], start=(j == 0), stop=(j == DJ - 1))
                        ins.then_inc(s_m, 1)
                    for pr in range(2):
                        for t, at in HALVES:
                            for j in range(DJ):
                                ins = TE.matmul(pp[2 + pr][:, at], w_inb[:, j, QL + pr * P:QL + (pr + 1) * P], uT[:, j, t], start=(j == 0), stop=(j == DJ - 1))
                        ins.then_inc(s_qm, 1)
                    pe.wait_ge(s_d, 7 + 11)
                    for c, r in enumerate(ROWS):
                        if c >= 2:
                            pe.wait_ge(s_k, 3 * (c - 1))
                        q = pp[c % 2]
                        for a in range(2):
                            TE.transpose(q[:, a * P:a * P + r], c_tok[:r, c, a * P:(a + 1) * P], ident[:r, :r])
                        TE.transpose(q[0:RP, 2 * P:2 * P + r], kr_tok[:r, c, :], ident[:r, :r])
                        qv = rawq[:r, c, :].rearrange("t (p j) -> t j p", j=3)
                        for j in range(3):
                            ins = TE.transpose(q[:, (4 + j) * P:(4 + j) * P + r], qv[:, j, :], ident[:r, :r])
                        ins.then_inc(s_t, 1)

                @block.scalar
                def _(act):
                    a = Chain(act, s_a)
                    for c in range(NCH):
                        act.wait_ge(s_c, 2 * (c + 1))
                        a(act.activation(sqr[:, 0:KL], raw1[:, c, 0:KL], ACT.Square, accum_out=st[:, 0, c:c + 1]))
                        a(act.activation(sqr[:], rawq[:, c, :], ACT.Square, accum_out=st[:, 1, c:c + 1]))
                    act.wait_ge(s_d, 4)
                    a(act.activation(st[:], st[:], ACT.Sqrt))
                    for pr in range(2):
                        act.wait_ge(s_qm, pr + 1)
                        act.activation(all_tokens(qmT1[:, pr, :]), halves(pp[2 + pr]), ACT.Copy).then_inc(s_q, 1)

                @block.vector
                def _(dve):
                    d = Chain(dve, s_d)
                    d(V.memset(raw1[:, NC_P, :], 0.0))
                    d(V.memset(rawq[:, NC_P, :], 0.0))
                    for c, r in enumerate(ROWS):
                        b = (c % 2) * 512
                        for k, (dst, n) in enumerate(((raw1, W_KV), (rawq, QL))):
                            dve.wait_ge(s_m, 2 * c + k + 1)
                            if c == NC_P:
                                V.tensor_copy(dst[:r, c, 0:n // 2], pp[k][:r, b:b + n // 2])
                                V.tensor_copy(dst[:r, c, n // 2:n], pp[k][NS:NS + r, b:b + n // 2]).then_inc(s_c, 1)
                            else:
                                V.tensor_copy(dst[:r, c, :], pp[k][:r, b:b + n]).then_inc(s_c, 1)
                    dve.wait_ge(s_a, 10)
                    dve.wait_ge(s_i, 32 + 16 * NPG)
                    d(V.tensor_scalar(st[:, 0, :], st[:, 0, :], 1.0 / KL, EPS, ALU.mult, ALU.add))
                    d(V.tensor_scalar(st[:, 1, :], st[:, 1, :], 1.0 / QL, EPS, ALU.mult, ALU.add))
                    dve.wait_ge(s_a, 11)
                    d(V.reciprocal(st[:], st[:]))
                    d(V.tensor_tensor(c_tok[:], raw1[:, :, 0:KL], bc(st[:, 0, :], 2, KL), ALU.mult))
                    d(V.tensor_tensor(c_tok[:], c_tok[:], bc(g_lat[:], 1, NCH), ALU.mult))
                    d(V.tensor_tensor(rawq[:], rawq[:], bc(st[:, 1, :], 2, QL), ALU.mult))
                    rotate(d, kr_tok[:], raw1[:, :, KL:], tmp[:], lambda t: t)
                    d(V.tensor_copy(pgf[:], pg[:]))
                    d(V.tensor_scalar(pgf[:], pgf[:], 8.0, const("eighth"), ALU.mult, ALU.add))
                    d(V.tensor_copy(page_i[:], pgf[:]))
                    d(V.memset(tmp[:], 0.0))
                    for c, r in enumerate(ROWS):
                        dve.wait_ge(s_t, c + 1)
                        q = pp[c % 2]
                        V.tensor_copy(cT[:, :, offset(c):offset(c) + r], q[:, 0:2 * P].rearrange("p (a t) -> p a t", a=2)[:, :, :r]).then_inc(s_k, 1)
                        V.tensor_copy(krT[:, offset(c):offset(c) + r], q[0:RP, 2 * P:2 * P + r]).then_inc(s_k, 1)
                        V.tensor_tensor(cqT[:, :, offset(c):offset(c) + r], q[:, 4 * P:7 * P].rearrange("p (j t) -> p j t", j=3)[:, :, :r],
                                        bc(gq[:], 2, r), ALU.mult).then_inc(s_k, 1)

        with ExitStack() as cx:
            w_uk = ring[1][:, 0:1536].rearrange("p (a n) -> p a n", a=2)
            q_nT = sb("q_nope_T", [P, DN_H, T], where=cx)
            qr_raw = ring[1][:, 1536:3456].rearrange("p (c h n) -> p c h n", c=NCH, h=DN_H)
            qr_tok = ring[1][:, 3456:5376].rearrange("p (c h n) -> p c h n", c=NCH, h=DN_H)
            tmq = sb("qr_tmp", [P, NCH, DN_H, RP // 2], where=cx)
            s_w, s_n, s_nk, s_r, s_rk, s_d, s_u, s_uk, s_l, s_lk, s_t, s_tk = (
                sem(f"q_{m}") for m in ("w_uk", "nope", "nope_kept", "rope", "rope_kept", "dve", "uk_turned", "uk_kept", "latent", "latent_kept", "turned", "turned_kept"))
            with nc.Block() as block:
                @block.sync
                def _(sp):
                    sp.dma_start(w_uk, I["w_uk"].rearrange("(a p) h n -> p a (h n)", p=P)).then_inc(s_w, 16)

                @block.tensor
                def _(pe):
                    wr = w_uq.rearrange("p j (h n) -> p j h n", h=DN_H)
                    for c, r in enumerate(ROWS):
                        if c >= 2:
                            pe.wait_ge(s_rk, c - 1)
                        for j in range(3):
                            ins = TE.matmul(pp[3][:r, (c % 2) * 512:(c % 2) * 512 + DN_H * RP], cqT[:, j, offset(c):offset(c) + r],
                                            wr[:, j, :, P:P + RP], start=(j == 0), stop=(j == 2))
                        ins.then_inc(s_r, 1)
                    pe.wait_ge(s_w, 16)
                    for h in range(DN_H):
                        if h >= 2:
                            pe.wait_ge(s_uk, h - 1)
                        for a in range(2):
                            ins = TE.transpose(pp[2][:, (h % 2) * 512 + a * P:(h % 2) * 512 + (a + 1) * P], w_uk[:, a, h * P:(h + 1) * P], ident)
                        ins.then_inc(s_u, 1)
                    for h in range(DN_H):
                        if h >= 2:
                            pe.wait_ge(s_nk, h - 1)
                        for t, at in HALVES:
                            for j in range(3):
                                ins = TE.matmul(pp[h % 2][:, at], wr[:, j, h, 0:P], cqT[:, j, t], start=(j == 0), stop=(j == 2))
                        ins.then_inc(s_n, 1)
                    pe.wait_ge(s_d, 7)
                    for h in range(DN_H):
                        if h == 0:
                            pe.wait_ge(s_rk, NCH)
                        else:
                            pe.wait_ge(s_tk, h)
                        for c in range(NC_P):
                            TE.transpose(pp[3][0:RP, c * P:(c + 1) * P], qr_tok[:, c, h, :], ident)
                        TE.transpose(pp[3][0:RP, SEQ:T], qr_tok[0:NS, NC_P, h, :], ident[0:NS, 0:NS]).then_inc(s_t, 1)
                        for a in range(2):
                            n = 2 * h + a
                            if n == 0:
                                pe.wait_ge(s_nk, DN_H)
                            if n >= 2:
                                pe.wait_ge(s_lk, n - 1)
                            if n == 0:
                                pe.wait_ge(s_uk, DN_H)
                            for t, at in HALVES:
                                ins = TE.matmul(pp[n % 2][:, at], w_ukT[:, h, a * P:(a + 1) * P], q_nT[:, h, t], start=True, stop=True)
                            ins.then_inc(s_l, 1)

                @block.scalar
                def _(act):
                    for h in range(DN_H):
                        act.wait_ge(s_n, h + 1)
                        act.activation(all_tokens(q_nT[:, h, :]), halves(pp[h % 2]), ACT.Copy).then_inc(s_nk, 1)
                    for h in range(DN_H):
                        for a in range(2):
                            act.wait_ge(s_l, 2 * h + a + 1)
                            act.activation(all_tokens(q_latT[:, h, a, :]), halves(pp[a]), ACT.Copy).then_inc(s_lk, 1)

                @block.vector
                def _(dve):
                    d = Chain(dve, s_d)
                    d(V.memset(qr_raw[:, NC_P], 0.0))
                    for c, r in enumerate(ROWS):
                        dve.wait_ge(s_r, c + 1)
                        V.tensor_copy(qr_raw[:r, c], pp[3][:r, (c % 2) * 512:(c % 2) * 512 + DN_H * RP].rearrange("p (h n) -> p h n", h=DN_H)).then_inc(s_rk, 1)
                    for h in range(DN_H):
                        dve.wait_ge(s_u, h + 1)
                        V.tensor_copy(w_ukT[:, h, :], pp[2][:, (h % 2) * 512:(h % 2) * 512 + KL]).then_inc(s_uk, 1)
                    dve.wait_ge(s_rk, NCH)
                    hf = RP // 2
                    for k, (o, f1, f2, op) in enumerate(((0, cos, sin, ALU.subtract), (hf, sin, cos, ALU.add))):
                        for h in range(DN_H):
                            V.tensor_tensor(qr_tok[:, :, h, o:o + hf], qr_raw[:, :, h, 0:hf], f1, ALU.mult)
                            ins = V.tensor_tensor(tmq[:, :, h, :], qr_raw[:, :, h, hf:RP], f2, ALU.mult)
                        d(ins)
                        v = qr_tok.rearrange("p c h n -> p (c h) n")[:, :, o:o + hf]
                        d(V.tensor_tensor(v, v, tmq[:].rearrange("p c h n -> p (c h) n"), op))
                    d(V.memset(tmq[:, 0, 0, :], 0.0))
                    d(V.memset(tmq[:, 0, 0, :], 0.0))
                    for h in range(DN_H):
                        dve.wait_ge(s_t, h + 1)
                        V.tensor_copy(qrT[:, h, :], pp[3][0:RP, 0:T]).then_inc(s_tk, 1)
        QX.close()
        dump("q_latT", q_latT[:])
        dump("qrT", qrT[:])

        E8 = PAGE // 8
        lat_e = I["cache_kv_latent"].rearrange("n (e t) c -> (n e) (t c)", e=8)
        rope_e = I["cache_k_rope"].rearrange("n (e t) c -> (n e) (t c)", e=8)
        CB = 3
        s_pages = [sem(f"pages{k}") for k in range(CB)]
        rope_rows2 = sb("rope_cache2", [P, E8 * RP], where=AT1)

        def cache_of(b):
            k = b % CB
            if k < 2:
                return ring[k][:, 0:E8 * KL], ring[k][:, E8 * KL:E8 * W_KV]
            return uT[:].rearrange("p j t -> p (j t)")[:, 0:E8 * KL], rope_rows2[:]

        def fetch_pages(pool, b):
            for dst, src in zip(cache_of(b), (lat_e, rope_e)):
                pool.indirect_dma_start(dst, None, src, bass.IndirectOffsetOnAxis(page_i[:, b:b + 1], 0)).then_inc(s_pages[b % CB], 16)

        with ExitStack() as cx:
            pr = [sb(f"pr{k}", [P, SEQ], where=cx) for k in range(2)]
            prT = [sb(f"prT{k}", [P, NC_P, P], where=cx) for k in range(2)]
            st = sb("attn_stat", [P, 4, DN_H * NC_P], where=cx)
            units = [(h, i) for h in range(DN_H) for i in range(NC_P)]
            s_s, s_m, s_x, s_p, s_t, s_e, s_o, s_k, s_d = (sem(f"attn_{m}") for m in ("scores", "max", "exp", "probs", "turned", "turned_kept", "out", "kept", "dve"))
            with nc.Block() as block:
                @block.gpsimd
                def _(pool):
                    for b in range(CB):
                        fetch_pages(pool, b)

                @block.tensor
                def _(pe):
                    def scores(n):
                        h, i = units[n]
                        if n >= 2:
                            pe.wait_ge(s_x, n - 1)
                        o, k = (n % 2) * 512, (i + 1) * P
                        tq = slice(i * P, (i + 1) * P)
                        for a in range(2):
                            TE.matmul(pp[0][:, o:o + k], q_latT[:, h, a, tq], cT[:, a, 0:k], start=(a == 0), stop=False)
                        TE.matmul(pp[0][:, o:o + k], qrT[:, h, tq], krT[:, 0:k], start=False, stop=True).then_inc(s_s, 1)

                    def turn(n):
                        h, i = units[n]
                        o = (n % 2) * 512
                        pe.wait_ge(s_p, n + 1)
                        if n >= 2:
                            pe.wait_ge(s_e, n - 1)
                        for k in range(i + 1):
                            ins = TE.transpose(pp[1][:, o + k * P:o + (k + 1) * P], pr[n % 2][:, k * P:(k + 1) * P], ident)
                        ins.then_inc(s_t, 1)

                    def out(n):
                        h, i = units[n]
                        o = (n % 2) * 512
                        pe.wait_ge(s_e, n + 1)
                        if n >= 2:
                            pe.wait_ge(s_k, n - 1)
                        for a in range(2):
                            for k in range(i + 1):
                                ins = TE.matmul(pp[2][:, o + a * P:o + (a + 1) * P], c_tok[:, k, a * P:(a + 1) * P], prT[n % 2][:, k, :], start=(k == 0), stop=(k == i))
                        ins.then_inc(s_o, 1)

                    scores(0)
                    scores(1)
                    turn(0)
                    for n in range(len(units)):
                        if n + 2 < len(units):
                            scores(n + 2)
                        if n + 1 < len(units):
                            turn(n + 1)
                        out(n)

                @block.scalar
                def _(act):
                    def exp(n):
                        h, i = units[n]
                        o, k = (n % 2) * 512, (i + 1) * P
                        act.wait_ge(s_m, n + 1)
                        if n >= 2:
                            act.wait_ge(s_t, n - 1)
                        act.activation(pr[n % 2][:, 0:k], pp[0][:, o:o + k], ACT.Exp, bias=st[:, 1, n:n + 1], scale=MLA_SCALE, accum_out=st[:, 2, n:n + 1]).then_inc(s_x, 1)

                    exp(0)
                    for n, (h, i) in enumerate(units):
                        o, k = (n % 2) * 512, (i + 1) * P
                        if n + 1 < len(units):
                            exp(n + 1)
                        act.wait_ge(s_t, n + 1)
                        if n >= 2:
                            act.wait_ge(s_o, n - 1)
                        act.activation(prT[n % 2][:, 0:i + 1, :], pp[1][:, o:o + k].rearrange("p (k t) -> p k t", t=P), ACT.Copy).then_inc(s_e, 1)

                def keep(dve, n):
                    h, i = units[n]
                    dve.wait_ge(s_o, n + 1)
                    o = (n % 2) * 512
                    V.tensor_copy(q_latT[:, h, :, i * P:(i + 1) * P], pp[2][:, o:o + 2 * P].rearrange("p (a t) -> p a t", a=2)).then_inc(s_k, 1)

                @block.vector
                def _(dve):
                    d = Chain(dve, s_d)

                    def maximum(n):
                        h, i = units[n]
                        o, k = (n % 2) * 512, (i + 1) * P
                        dve.wait_ge(s_s, n + 1)
                        d(V.tensor_tensor(pp[0][:, o + k - P:o + k], pp[0][:, o + k - P:o + k], const("causal"), ALU.add))
                        d(V.tensor_reduce(st[:, 0, n:n + 1], pp[0][:, o:o + k], AX, ALU.max))
                        V.tensor_scalar(st[:, 1, n:n + 1], st[:, 0, n:n + 1], -MLA_SCALE, None, ALU.mult).then_inc(s_m, 1)

                    def normalise(n):
                        k = (units[n][1] + 1) * P
                        dve.wait_ge(s_x, n + 1)
                        d(V.reciprocal(st[:, 3, n:n + 1], st[:, 2, n:n + 1]))
                        V.tensor_scalar(pr[n % 2][:, 0:k], pr[n % 2][:, 0:k], st[:, 3, n:n + 1], None, ALU.mult).then_inc(s_p, 1)

                    maximum(0)
                    maximum(1)
                    normalise(0)
                    for n in range(len(units)):
                        if n + 1 < len(units):
                            normalise(n + 1)
                        if n + 2 < len(units):
                            maximum(n + 2)
                        if n >= 1:
                            keep(dve, n - 1)
                    keep(dve, len(units) - 1)


        HQ, HP = DN_H * DS, 32
        NG4 = P // HP
        KG = E8 // NG4
        with ExitStack() as cx:
            KT = sb("keys_T", [P, 2, E8 * P], where=cx)
            KR = sb("rope_keys_T", [P, E8 * P], where=cx)
            pb = [sb(f"probs{k}", [P, KG * P], where=cx) for k in range(2)]
            pT = mem_v[:, 0].rearrange("p m (k t) -> p (m k) t", t=P)
            st = sb("samples_stat", [P, 7, DB], where=cx)
            mx, nb, ss, s2, wt, Mb, L = (st[:, k, :] for k in range(7))
            qls = w_ukT[:, 0:2, :].rearrange("p a (b q) -> p a b q", b=DB)
            qrs = w_ukT[:, 2, :].rearrange("p (b q) -> p b q", b=DB)
            snT, sn = w_ukT[0:NS, 3, :], w_ukT[0:HP, 4, :]
            pn, pTn, mn, M8, Mg = (w_ukT[0:n, 5, o:o + k] for n, o, k in ((HP, 0, NS), (NS, 32, HP), (HP, 64, DB), (DB, 72, HP), (DB, 104, P)))
            outs = [ring[k][:, E8 * W_KV:E8 * W_KV + DB // 2 * KL].rearrange("p (i c) -> p i c", c=KL) for k in range(2)]
            s_q, s_tr, s_ea, s_ed, s_s, s_m, s_x, s_pt, s_pk, s_o, s_n, s_d, s_nw, s_nc, s_c, s_w = (
                sem(f"samp_{m}") for m in ("queries", "keys_turned", "keys_kept_a", "keys_kept_v", "scores", "max", "exp", "probs_turned", "probs_kept",
                                           "out", "out_kept", "dve", "new_keys", "new_copied", "combine", "weights"))
            NGR = 12

            def group(b, g):
                lat, rope = cache_of(b)
                if g < 8:
                    a, t0 = g // 4, 4 * (g % 4)
                    return [lat[:, (t0 + t) * KL + a * P:(t0 + t) * KL + (a + 1) * P] for t in range(4)], P, KT[:, a, t0 * P:(t0 + 4) * P]
                t0 = 4 * (g - 8)
                return [rope[:, (t0 + t) * RP:(t0 + t + 1) * RP] for t in range(4)], RP, KR[0:RP, t0 * P:(t0 + 4) * P]

            with nc.Block() as block:
                @block.gpsimd
                def _(pool):
                    for b in range(CB, DB):
                        pool.wait_ge(s_o, b - CB + 1)
                        fetch_pages(pool, b)

                @block.tensor
                def _(pe):
                    def keys(b, groups):
                        if groups[0] == 0:
                            pe.wait_ge(s_pages[b % CB], 32 * (b // CB + 1))
                        for g in groups:
                            n = b * NGR + g
                            if n >= 2:
                                pe.wait_ge(s_ea if n % 2 == 0 else s_ed, n // 2)
                            src, m, _ = group(b, g)
                            for t in range(4):
                                ins = TE.transpose(pp[3][0:m, (n % 2) * 512 + t * P:(n % 2) * 512 + (t + 1) * P], src[t], ident)
                            ins.then_inc(s_tr, 1)

                    def scores(b):
                        pe.wait_ge(s_ea, NGR // 2 * (b + 1))
                        pe.wait_ge(s_ed, NGR // 2 * (b + 1))
                        if b == 0:
                            pe.wait_ge(s_q, 1)
                        if b >= 2:
                            pe.wait_ge(s_x, b - 1)
                        for k in range(3):
                            for n in range(NG4):
                                q, kt = (qls[:, k, b, :], KT[:, k, n * 512:(n + 1) * 512]) if k < 2 else (qrs[:, b, :], KR[:, n * 512:(n + 1) * 512])
                                ins = TE.matmul(pp[0][HP * n:HP * (n + 1), (b % 2) * 512:(b % 2) * 512 + 512], q, kt, start=(k == 0), stop=(k == 2))
                        ins.then_inc(s_s, 1)

                    def turn(b):
                        pe.wait_ge(s_x, b + 1)
                        if b >= 1:
                            pe.wait_ge(s_pk, b)
                        for t in range(KG):
                            TE.transpose(pp[1][:, t * P:(t + 1) * P], pb[b % 2][:, t * P:(t + 1) * P], ident)
                        TE.transpose(pp[1][0:NS, 512:512 + HP], pn, ident[:HP, :HP]).then_inc(s_pt, 1)

                    def out(b):
                        pe.wait_ge(s_pk, b + 1)
                        if b >= 2:
                            pe.wait_ge(s_n, b - 1)
                        lat, o = cache_of(b)[0], (b % 2) * 512
                        for t in range(KG):
                            for n in range(NG4):
                                TE.matmul(pp[2][HP * n:HP * (n + 1), o:o + KL], pT[:, t, HP * n:HP * (n + 1)], lat[:, (KG * n + t) * KL:(KG * n + t + 1) * KL],
                                          start=(t == 0), stop=(t == KG - 1 and n > 0))
                        TE.matmul(pp[2][0:HP, o:o + KL], pTn, c_tok[0:NS, NC_P, :], start=False, stop=True).then_inc(s_o, 1)

                    pe.wait_ge(s_q, 1)
                    for a in range(2):
                        TE.matmul(pp[1][0:NS, 512:512 + DB * HP], cT[:, a, SEQ:T], qls[:, a].rearrange("p b q -> p (b q)"), start=(a == 0), stop=False)
                    TE.matmul(pp[1][0:NS, 512:512 + DB * HP], krT[:, SEQ:T], w_ukT[0:RP, 2, :], start=False, stop=True).then_inc(s_nw, 1)
                    keys(0, range(0, 4))
                    pe.wait_ge(s_nc, 1)
                    for b in range(DB):
                        ins = TE.transpose(pp[1][0:HP, b * NS:(b + 1) * NS], snT[:, b * HP:(b + 1) * HP], ident[:NS, :NS])
                    ins.then_inc(s_nw, 1)
                    keys(0, range(4, NGR))
                    scores(0)
                    for b in range(DB):
                        if b + 1 < DB:
                            keys(b + 1, range(0, 8))
                        if b == 0:
                            pe.wait_ge(s_nc, 2)
                        turn(b)
                        if b + 1 < DB:
                            keys(b + 1, range(8, NGR))
                        out(b)
                        if b + 1 < DB:
                            scores(b + 1)
                    TE.transpose(pp[1][0:DB, 0:P], mx, ident).then_inc(s_c, 1)
                    pe.wait_ge(s_w, 1)
                    TE.transpose(pp[1][:, 512:512 + DB], Mg, ident[:DB, :DB]).then_inc(s_c, 1)
                    pe.wait_ge(s_w, 2)
                    TE.matmul(pp[0][:, 0:DB], const("same_row"), L, start=True, stop=True).then_inc(s_c, 1)
                    pe.wait_ge(s_w, 4)
                    for a in range(2):
                        for b in range(DB):
                            o = (a * DB + b) * HP
                            ins = TE.matmul(pp[3][:, o:o + HP], outs[b % 2][:, b // 2, a * P:(a + 1) * P], const("same_row")[:, 0:HP], start=True, stop=True)
                    ins.then_inc(s_c, 1)

                @block.scalar
                def _(act):
                    def keep(b):
                        for g in range(0, NGR, 2):
                            n = b * NGR + g
                            act.wait_ge(s_tr, n + 1)
                            if g == 0 and b >= 1:
                                act.wait_ge(s_s, b)
                            _, m, dst = group(b, g)
                            act.activation(dst, pp[3][0:m, 0:512], ACT.Copy).then_inc(s_ea, 1)

                    keep(0)
                    for b in range(DB):
                        act.wait_ge(s_m, b + 1)
                        if b >= 1:
                            act.wait_ge(s_pt, b)
                        act.activation(pb[b % 2][:], pp[0][:, (b % 2) * 512:(b % 2) * 512 + 512], ACT.Exp, bias=nb[:, b:b + 1], scale=MLA_SCALE, accum_out=ss[:, b:b + 1])
                        act.activation(pn, sn[:, b * NS:(b + 1) * NS], ACT.Exp, bias=nb[0:HP, b:b + 1], scale=MLA_SCALE, accum_out=s2[0:HP, b:b + 1]).then_inc(s_x, 1)
                        if b + 1 < DB:
                            keep(b + 1)
                        act.wait_ge(s_o, b + 1)
                        act.activation(outs[b % 2][:, b // 2, :], pp[2][:, (b % 2) * 512:(b % 2) * 512 + KL], ACT.Copy).then_inc(s_n, 1)
                    act.wait_ge(s_nc, 3)
                    act.activation(wt, wt, ACT.Exp, scale=MLA_SCALE).then_inc(s_nc, 1)

                @block.vector
                def _(dve):
                    d = Chain(dve, s_d)

                    def keep(b):
                        for g in range(1, NGR, 2):
                            n = b * NGR + g
                            dve.wait_ge(s_tr, n + 1)
                            if g == 1 and b >= 1:
                                dve.wait_ge(s_s, b)
                            _, m, dst = group(b, g)
                            V.tensor_copy(dst, pp[3][0:m, 512:1024]).then_inc(s_ed, 1)

                    d(V.memset(w_ukT[:, 0:3, :], 0.0))
                    V.memset(KR[RP:P, :], 0.0).then_inc(s_d, 1)
                    d.n += 1
                    for a in range(2):
                        d(V.tensor_copy(qls[:, a, :, 0:HQ].rearrange("p b (h t) -> p b h t", h=DN_H), q_latT[:, :, a, SEQ:T].rearrange("p h (b t) -> p b h t", b=DB)))
                    V.tensor_copy(qrs[0:RP, :, 0:HQ].rearrange("p b (h t) -> p b h t", h=DN_H), qrT[:, :, SEQ:T].rearrange("p h (b t) -> p b h t", b=DB)).then_inc(s_q, 1)
                    dve.wait_ge(s_nw, 1)
                    V.tensor_copy(snT, pp[1][0:NS, 512:512 + DB * HP]).then_inc(s_nc, 1)
                    keep(0)
                    dve.wait_ge(s_nw, 2)
                    V.tensor_tensor(sn, pp[1][0:HP, 0:DB * NS], const("new_keys")[0:HP, :], ALU.add).then_inc(s_nc, 1)
                    dve.wait_ge(s_nc, 2)
                    d(V.tensor_reduce(mn, sn.rearrange("q (b k) -> q b k", b=DB), AX, ALU.max))
                    for b in range(DB):
                        dve.wait_ge(s_s, b + 1)
                        d(V.tensor_reduce(mx[:, b:b + 1], pp[0][:, (b % 2) * 512:(b % 2) * 512 + 512], AX, ALU.max))
                        d(V.tensor_tensor(mx[0:HP, b:b + 1], mx[0:HP, b:b + 1], mn[:, b:b + 1], ALU.max))
                        V.tensor_scalar(nb[:, b:b + 1], mx[:, b:b + 1], -MLA_SCALE, None, ALU.mult).then_inc(s_m, 1)
                        if b + 1 < DB:
                            keep(b + 1)
                        dve.wait_ge(s_pt, b + 1)
                        if b >= 1:
                            dve.wait_ge(s_o, b)
                        V.tensor_copy(pTn, pp[1][0:NS, 512:512 + HP])
                        V.tensor_copy(pT, pp[1][:, 0:512].rearrange("p (t q) -> p t q", t=KG)).then_inc(s_pk, 1)
                    dve.wait_ge(s_x, DB)
                    d(V.tensor_tensor(ss[0:HP, :], ss[0:HP, :], s2[0:HP, :], ALU.add))
                    dve.wait_ge(s_c, 1)
                    d(V.tensor_reduce(M8, pp[1][0:DB, 0:P].rearrange("b (n q) -> b q n", n=NG4), AX, ALU.max))
                    V.tensor_copy(Mg.rearrange("b (n q) -> b n q", n=NG4), bc(M8, 1, NG4)).then_inc(s_w, 1)
                    dve.wait_ge(s_c, 2)
                    d(V.tensor_copy(Mb, pp[1][:, 512:512 + DB]))
                    V.tensor_tensor(wt, mx, Mb, ALU.subtract).then_inc(s_nc, 1)
                    dve.wait_ge(s_nc, 4)
                    V.tensor_tensor(L, wt, ss, ALU.mult).then_inc(s_w, 1)
                    dve.wait_ge(s_c, 3)
                    d(V.reciprocal(Mb, pp[0][:, 0:DB]))
                    d(V.tensor_tensor(wt, wt, Mb, ALU.mult))
                    dve.wait_ge(s_n, DB)
                    for k in range(2):
                        V.tensor_tensor(outs[k], outs[k], bc(wt.rearrange("p (i k) -> p k i", k=2)[:, k], 2, KL), ALU.mult).then_inc(s_w, 1)
                    dve.wait_ge(s_c, 4)
                    for a in range(2):
                        V.tensor_copy(q_latT[:, :, a, SEQ:T].rearrange("p h (b t) -> p h b t", b=DB),
                                      pp[3][:, a * DB * HP:(a + 1) * DB * HP].rearrange("p (b q) -> p b q", b=DB)[:, :, 0:HQ].rearrange("p b (h t) -> p h b t", h=DN_H))

        w_outb = I["w_out_b"][0].rearrange("(j p) n -> p j n", p=P)
        with nc.Block() as block:
            s_m, s_k = sem("values_product"), sem("values_kept")

            @block.sync
            def _(sp):
                for n in range(2):
                    load(sp, n, f"outb{n}", (slot3(n, 512), w_outb[:, :, n * 512:(n + 1) * 512]))

            @block.tensor
            def _(pe):
                for h in range(DN_H):
                    if h >= 4:
                        pe.wait_ge(s_k, h - 3)
                    for t, at in HALVES:
                        for a in range(2):
                            ins = TE.matmul(pp[h % 4][:, at], w_uv[:, a, h * P:(h + 1) * P], q_latT[:, h, a, t], start=(a == 0), stop=(a == 1))
                    ins.then_inc(s_m, 1)

            @block.scalar
            def _(act):
                for h in range(DN_H):
                    act.wait_ge(s_m, h + 1)
                    act.activation(all_tokens(mergedT[:, h, :]), halves(pp[h % 4]), ACT.Copy).then_inc(s_k, 1)
        AT1.close()
        with ExitStack() as cx:
            mk1, mv1 = (sb(f"mem_cache_{n}", [P, DB, 2, MEM], where=cx) for n in "kv")
            kt1 = sb("mem_keys_T1", [P, 2, DB, MEM], where=cx)
            pr1 = [sb(f"mem_pr{k}", [P, 1024], where=cx) for k in range(2)]
            prT1 = sb("mem_prT", [P, 8, P], where=cx)
            zq1 = sb("mem_q", [P, 2, 1152], where=cx)
            st1 = sb("mem_stat1", [P, 4, NCH, MH], where=cx)
            memory_attention(1, qmT1, mk1[:], mv1[:], kt1, [pr1[0][:], pr1[1][:]], prT1[:], zq1[:], st1)
        L1.close()
        dump("x_mixed", x[:, 0:NC_P, :])
        dump("x_mixed_s", x[0:NS, NC_P, :])
        reuse_semaphores()
        experts(1, [(slot3(0, 512), "outb0"), (slot3(1, 512), "outb1")])

        with ExitStack() as cx:
            gf = sb("g_final_rows", [P, D], where=cx)
            y = sb("y", [P, NCH, D], where=cx)
            ss = x_sums
            s_g, s_r, s_d, s_y, s_o = (sem(f"final_{m}") for m in ("gain", "root", "dve", "rows", "stored"))
            with nc.Block() as block:
                @block.sync
                def _(sp):
                    sp.dma_start(gf[:], I["g_final"].partition_broadcast(P)).then_inc(s_g, 16)
                    for c in range(NCH):
                        sp.wait_ge(s_y, c + 1)
                        if c < NC_P:
                            sp.dma_start(O["y_prompt"][0, c * P:(c + 1) * P, :], y[:, c, :]).then_inc(s_o, 16)
                        else:
                            sp.dma_start(O["y_sample"].rearrange("b t d -> (b t) d"), y[0:NS, c, :]).then_inc(s_o, 16)
                    sp.wait_ge(s_o, 16 * NCH)

                @block.scalar
                def _(act):
                    act.wait_ge(s_d, 1)
                    act.activation(ss[:], ss[:], ACT.Sqrt).then_inc(s_r, 1)

                @block.vector
                def _(dve):
                    d = Chain(dve, s_d)
                    d(V.tensor_scalar(ss[:], ss[:], 1.0 / D, EPS, ALU.mult, ALU.add))
                    dve.wait_ge(s_r, 1)
                    d(V.reciprocal(ss[:], ss[:]))
                    dve.wait_ge(s_g, 16)
                    for c, r in enumerate(ROWS):
                        V.scalar_tensor_tensor(y[:r, c, :], x[:r, c, :], ss[:r, c:c + 1], gf[:r, :], ALU.mult, ALU.mult).then_inc(s_y, 1)
        return debug_out


_INS = ["x_prompt", "x_sample", "mem_prompt", "state_delta", "cache_conv", "cache_kv_latent", "cache_k_rope",
        "cache_mem_k", "cache_mem_v", "page_table", "g_mix", "g_ffn", "g_final", "w_in_a", "conv_w", "a_log", "dt_bias",
        "g_onorm", "w_out_a", "g_kv_in", "w_dkv", "g_kv_latent", "w_uk", "w_uv", "w_in_b", "g_q", "w_uq", "w_out_b",
        "g_mem", "w_mem_k", "w_mem_v", "w_router_group", "b_router_group", "w_router_expert", "b_router_expert",
        "w_exp_gate", "w_exp_up", "w_exp_down"]
_OUTS = [("y_prompt", (1, SEQ, D)), ("y_sample", (DB, DS, D)), ("kv_latent_prompt", (1, SEQ, KL)), ("k_rope_prompt", (1, SEQ, RP)),
         ("kv_latent_sample", (DB, DS, KL)), ("k_rope_sample", (DB, DS, RP)), ("state_delta_prompt", (1, 1, DN_H, P, P)),
         ("cache_conv_prompt", (1, 1, 3, CONV_CH)), ("state_delta_sample", (1, DB, DN_H, P, P)),
         ("cache_conv_sample", (1, DB, 3, CONV_CH)), ("mem_k_prompt", (2, 1, MEM, MH, MHD)), ("mem_v_prompt", (2, 1, MEM, MH, MHD))]


def kernel(**inputs):
    import concourse.bacc as _bacc
    from concourse.bass_utils import run_bass_kernel_spmd as _run

    nc = _bacc.Bacc("TRN2", target_bir_lowering=False, num_devices=1)
    arrays, I, O = {}, {}, {}
    for name in _INS + ["consts"]:
        a = CONSTS if name == "consts" else np.ascontiguousarray(inputs[name])
        arrays[f"in_{name}"] = a
        I[name] = nc.dram_tensor(f"in_{name}", a.shape, mybir.dt.from_np(a.dtype), kind="ExternalInput").ap()
    for name, shape in _OUTS:
        O[name] = nc.dram_tensor(f"out_{name}", shape, F32, kind="ExternalOutput").ap()
    build(nc, I, O)
    r = _run(nc, [arrays], core_ids=[0])
    return tuple(r.results[0][f"out_{name}"] for name, _ in _OUTS)
```
